# Optimizing a Trainium2 kernel written in Bass

```python
import jax, jax.numpy as jnp
from jax import lax
import numpy as np

D_MODEL = 1024
BATCH = 1
SEQ = 512
DEPTH = 2
DEC_BATCH = 8
DEC_SEQ = 1
PAST_LEN = 2048
PAGE_SIZE = 128

N_A_LAYERS = DEPTH // 2
N_B_LAYERS = DEPTH - N_A_LAYERS
RMS_EPS = 1e-6
RW_HEAD = 64
RW_HEADS = D_MODEL // RW_HEAD
RW_DECAY_LORA = 64
RW_AAA_LORA = 64
RW_GATE_LORA = 128
RW_GN_EPS = 64e-5
N_HEADS = 16
HEAD_DIM = D_MODEL // N_HEADS
KV_HEADS = 4
GQA_R = N_HEADS // KV_HEADS
ATT_SCALE = HEAD_DIM ** -0.5
ROPE_DIMS = HEAD_DIM // 4
ROPE_THETA = 500000.0
N_KV_STREAMS = 6
CMP_BLOCK = 32
CMP_STRIDE = 16
CMP_HIDDEN = 2 * HEAD_DIM
SEL_BLOCK = 64
N_SEL = 16
N_LOCAL_BLOCKS = 2
FORCE_SCORE = 1.0e4
WINDOW = 512
WIN_Q_BLOCK = 128
SEL_Q_BLOCK = 16
N_GROUPS = 4
EXPERTS_PER_GROUP = 8
TOP_K_IN_GROUP = 2
D_EXPERT = 256

kernel_name = 'rwkv7_yoco_nsa_hmoe_step'

F32 = jnp.float32

def rmsnorm(x, g):
    xf = x.astype(F32)
    y = xf * lax.rsqrt(jnp.mean(xf * xf, axis=-1, keepdims=True) + RMS_EPS)
    return (y * g.astype(F32)).astype(x.dtype)

def rope(x, pos):
    half = ROPE_DIMS // 2
    inv = jnp.power(ROPE_THETA, -jnp.arange(half, dtype=F32) * (2.0 / ROPE_DIMS))
    ang = pos.astype(F32)[:, None] * inv[None, :]
    cos = jnp.cos(ang)[:, None, :]
    sin = jnp.sin(ang)[:, None, :]
    xf = x.astype(F32)
    x1 = xf[..., :half]
    x2 = xf[..., half:ROPE_DIMS]
    out = jnp.concatenate([x1 * cos - x2 * sin, x2 * cos + x1 * sin, xf[..., ROPE_DIMS:]], axis=-1)
    return out.astype(x.dtype)

def masked_softmax(s, mask):
    s = jnp.where(mask, s, -jnp.inf)
    m = jnp.max(s, axis=-1, keepdims=True)
    m = jnp.where(jnp.isfinite(m), m, 0.0)
    e = jnp.where(mask, jnp.exp(s - m), 0.0)
    return e / jnp.maximum(jnp.sum(e, axis=-1, keepdims=True), 1e-30)

def map_query_blocks(fn, blk, q_pos, *arrs):
    T = q_pos.shape[0]
    nb = -(-T // blk)
    pad = nb * blk - T
    if pad:
        q_pos = jnp.pad(q_pos, (0, pad), mode='edge')
        arrs = tuple(jnp.pad(a, [(0, 0), (0, pad)] + [(0, 0)] * (a.ndim - 2)) for a in arrs)
    B = arrs[0].shape[0]
    pos_b = q_pos.reshape(nb, blk)
    arr_b = tuple(jnp.moveaxis(a.reshape(B, nb, blk, *a.shape[2:]), 1, 0) for a in arrs)
    out = lax.map(lambda xs: fn(*xs), (pos_b,) + arr_b)
    out = jnp.moveaxis(out, 0, 1)
    return out.reshape(B, nb * blk, *out.shape[3:])[:, :T]

def rwkv7_mixer(xn, prev, s0, mu, w_r, w_k, w_v, w_o, w0, w1, w2, a0, a1, a2, g1, g2, k_k, k_a, r_k, gn_w, gn_b):
    B, T, D = xn.shape
    xx = prev - xn
    xr, xw, xk, xv, xa, xg = (xn + xx * mu[i] for i in range(6))
    r = xr @ w_r
    k = xk @ w_k
    v = xv @ w_v
    w_log = -jax.nn.softplus(-(w0 + jnp.tanh(xw @ w1) @ w2).astype(F32)) - 0.5
    a = jax.nn.sigmoid((a0 + (xa @ a1) @ a2).astype(F32))
    g = jax.nn.sigmoid(xg @ g1) @ g2
    heads = lambda t: t.astype(F32).reshape(B, T, RW_HEADS, RW_HEAD)
    r, k, v, a, w_log = heads(r), heads(k), heads(v), heads(a), heads(w_log)
    kk = k * k_k.astype(F32).reshape(RW_HEADS, RW_HEAD)
    kk = kk / jnp.maximum(jnp.sqrt(jnp.sum(kk * kk, axis=-1, keepdims=True)), 1e-12)
    k = k * (1.0 + (a - 1.0) * k_a.astype(F32).reshape(RW_HEADS, RW_HEAD))
    decay = jnp.exp(-jnp.exp(w_log))

    def step(S, inp):
        r_t, d_t, k_t, v_t, kk_t, a_t = inp
        sa = jnp.einsum('bhij,bhj->bhi', S, -kk_t)
        S = S * d_t[:, :, None, :] + sa[..., None] * (kk_t * a_t)[:, :, None, :] + v_t[..., None] * k_t[:, :, None, :]
        return S, jnp.einsum('bhij,bhj->bhi', S, r_t)

    tm = lambda t: jnp.swapaxes(t, 0, 1)
    s_T, o = lax.scan(step, s0.astype(F32), (tm(r), tm(decay), tm(k), tm(v), tm(kk), tm(a)))
    o = tm(o)
    mean = jnp.mean(o, axis=-1, keepdims=True)
    var = jnp.mean(jnp.square(o - mean), axis=-1, keepdims=True)
    o = ((o - mean) * lax.rsqrt(var + RW_GN_EPS)).reshape(B, T, D) * gn_w.astype(F32) + gn_b.astype(F32)
    bonus = jnp.sum(r * k * r_k.astype(F32), axis=-1, keepdims=True) * v
    o = (o + bonus.reshape(B, T, D)).astype(xn.dtype)
    return (o * g) @ w_o, s_T

def hmoe(xn, w_rg, b_rg, w_re, b_re, w_gate, w_up, w_down):
    B, T, D = xn.shape
    x = xn.reshape(B * T, D)
    lg = (x @ w_rg + b_rg).astype(F32)
    g_sel = jnp.argmax(lg, axis=-1)
    p_g = jnp.max(jax.nn.softmax(lg, axis=-1), axis=-1)
    le = (x @ w_re + b_re).astype(F32).reshape(-1, N_GROUPS, EXPERTS_PER_GROUP)
    le_g = jnp.take_along_axis(le, g_sel[:, None, None], axis=1)[:, 0]
    top_p, top_i = lax.top_k(jax.nn.softmax(le_g, axis=-1), TOP_K_IN_GROUP)
    w_top = p_g[:, None] * top_p / jnp.sum(top_p, axis=-1, keepdims=True)
    comb = jnp.sum(jax.nn.one_hot(top_i, EXPERTS_PER_GROUP, dtype=F32) * w_top[..., None], axis=1)
    y = jnp.zeros((B * T, D), F32)
    for gi in range(N_GROUPS):
        c = jnp.where((g_sel == gi)[:, None], comb, 0.0).astype(x.dtype)
        hid = jax.nn.silu(jnp.einsum('nd,edf->nef', x, w_gate[gi])) * jnp.einsum('nd,edf->nef', x, w_up[gi])
        y = y + jnp.einsum('nef,ne,efd->nd', hid, c, w_down[gi]).astype(F32)
    return y.astype(xn.dtype).reshape(B, T, D)

def compress(rows, pe, w1, b1, w2):
    B, L, G, hd = rows.shape
    nh = CMP_BLOCK // CMP_STRIDE
    nsub = L // CMP_STRIDE
    n_cmp = nsub - nh + 1
    sub = rows[:, :nsub * CMP_STRIDE].reshape(B, nsub, CMP_STRIDE, G, hd)
    w1b = w1.reshape(nh, CMP_STRIDE, hd, CMP_HIDDEN)
    part = jnp.einsum('bnjgd,hjdc->hbngc', sub, w1b)
    pe_term = jnp.einsum('jd,jdc->c', pe, w1.reshape(CMP_BLOCK, hd, CMP_HIDDEN)) + b1
    pre = sum(part[i, :, i:i + n_cmp] for i in range(nh)) + pe_term
    return jax.nn.gelu(pre.astype(F32)).astype(rows.dtype) @ w2

def shared_kv(h, past_len, past_rows, win_buf, ln_kv, w_kv, cmp_pe, cmp_w1, cmp_b1, cmp_w2):
    B, T, _ = h.shape
    q_pos = past_len + jnp.arange(T)
    kv = (rmsnorm(h, ln_kv) @ w_kv).reshape(B, T, N_KV_STREAMS, KV_HEADS, HEAD_DIM)
    k_sel = rope(kv[:, :, 2], q_pos)
    k_win = rope(kv[:, :, 4], q_pos)
    new_rows = jnp.stack([kv[:, :, 0], kv[:, :, 1], k_sel, kv[:, :, 3]], axis=2)
    new_win = jnp.stack([k_win, kv[:, :, 5]], axis=2)
    if past_rows is None:
        rows, win_all, win_pos0 = new_rows, new_win, past_len
    else:
        rows = jnp.concatenate([past_rows.astype(new_rows.dtype), new_rows], axis=1)
        win_all = jnp.concatenate([win_buf.astype(new_win.dtype), new_win], axis=1)
        win_pos0 = past_len - win_buf.shape[1]
    L = rows.shape[1]
    kc = compress(rows[:, :, 0], cmp_pe[0], cmp_w1[0], cmp_b1[0], cmp_w2[0])
    vc = compress(rows[:, :, 1], cmp_pe[1], cmp_w1[1], cmp_b1[1], cmp_w2[1])
    n_cmp = kc.shape[1]
    cmp_start = jnp.arange(n_cmp) * CMP_STRIDE
    cmp_end = cmp_start + CMP_BLOCK - 1
    n_sblk = -(-L // SEL_BLOCK)
    sel_start = jnp.arange(n_sblk) * SEL_BLOCK
    overlap = ((cmp_start[:, None] < sel_start[None, :] + SEL_BLOCK) & (cmp_end[:, None] >= sel_start[None, :])).astype(F32)
    sel = jnp.pad(rows[:, :, 2:4], ((0, 0), (0, n_sblk * SEL_BLOCK - L), (0, 0), (0, 0), (0, 0)))
    sel = sel.reshape(B, n_sblk, SEL_BLOCK, 2, KV_HEADS, HEAD_DIM).transpose(3, 0, 4, 1, 2, 5)
    shared = (kc, vc, cmp_end, overlap, sel[0], sel[1], win_all[:, :, 0], win_all[:, :, 1], win_pos0)
    new_win_state = win_all[:, -min(WINDOW, win_all.shape[1]):]
    return shared, new_rows, new_win_state

def nsa_mixer(xn, q_pos, shared, w_qg, w_o):
    kc, vc, cmp_end, overlap, kb, vb, kw, vw, win_pos0 = shared
    B, T, _ = xn.shape
    qg = xn @ w_qg
    q = qg[..., :N_HEADS * HEAD_DIM].reshape(B, T, N_HEADS, HEAD_DIM)
    gates = jax.nn.sigmoid(qg[..., N_HEADS * HEAD_DIM:].astype(F32)).reshape(B, T, N_HEADS, 3, 1)
    q_c = q.reshape(B, T, KV_HEADS, GQA_R, HEAD_DIM)
    q_r = rope(q, q_pos).reshape(B, T, KV_HEADS, GQA_R, HEAD_DIM)

    s = jnp.einsum('btgrd,bngd->btgrn', q_c, kc).astype(F32) * ATT_SCALE
    p = masked_softmax(s, (cmp_end[None, :] <= q_pos[:, None])[None, :, None, None, :])
    o_cmp = jnp.einsum('btgrn,bngd->btgrd', p.astype(vc.dtype), vc)

    n_sblk = kb.shape[2]
    imp = jnp.einsum('btgrn,ns->btgs', p, overlap)
    j = jnp.arange(n_sblk)[None, :]
    qblk = (q_pos // SEL_BLOCK)[:, None]
    allowed = j <= qblk
    forced = (j == 0) | ((j > qblk - N_LOCAL_BLOCKS) & allowed)
    score = jnp.where(forced[None, :, None, :], FORCE_SCORE, imp)
    score = jnp.where(allowed[None, :, None, :], score, -jnp.inf)
    top_s, top_i = lax.top_k(score, min(N_SEL, n_sblk))
    valid = jnp.isfinite(top_s)

    bi = jnp.arange(B)[:, None, None, None]
    gi = jnp.arange(KV_HEADS)[None, None, :, None]

    def sel_block(pb, qb, ib, okb):
        kg = kb[bi, gi, ib]
        vg = vb[bi, gi, ib]
        nq, n_k = qb.shape[1], ib.shape[-1]
        sc = jnp.einsum('btgrd,btgkjd->btgrkj', qb, kg).astype(F32) * ATT_SCALE
        tok = ib[..., None] * SEL_BLOCK + jnp.arange(SEL_BLOCK)
        mask = okb[..., None] & (tok <= pb[None, :, None, None, None])
        pr = masked_softmax(sc.reshape(B, nq, KV_HEADS, GQA_R, n_k * SEL_BLOCK), mask.reshape(B, nq, KV_HEADS, 1, n_k * SEL_BLOCK))
        return jnp.einsum('btgrm,btgmd->btgrd', pr.astype(vg.dtype), vg.reshape(B, nq, KV_HEADS, n_k * SEL_BLOCK, HEAD_DIM))

    o_sel = map_query_blocks(sel_block, min(SEL_Q_BLOCK, T), q_pos, q_r, top_i, valid)

    wblk = min(WIN_Q_BLOCK, T)
    span = WINDOW - 1 + wblk
    kp = jnp.pad(kw, ((0, 0), (WINDOW - 1, wblk), (0, 0), (0, 0)))
    vp = jnp.pad(vw, ((0, 0), (WINDOW - 1, wblk), (0, 0), (0, 0)))

    def win_block(pb, qb):
        start = pb[0] - win_pos0
        kblk = lax.dynamic_slice_in_dim(kp, start, span, axis=1)
        vblk = lax.dynamic_slice_in_dim(vp, start, span, axis=1)
        kpos = pb[0] - (WINDOW - 1) + jnp.arange(span)
        mask = (kpos[None, :] <= pb[:, None]) & (kpos[None, :] > pb[:, None] - WINDOW) & (kpos[None, :] >= win_pos0)
        sc = jnp.einsum('btgrd,bsgd->btgrs', qb, kblk).astype(F32) * ATT_SCALE
        pr = masked_softmax(sc, mask[None, :, None, None, :])
        return jnp.einsum('btgrs,bsgd->btgrd', pr.astype(vblk.dtype), vblk)

    o_win = map_query_blocks(win_block, wblk, q_pos, q_r)

    branches = jnp.stack([t.reshape(B, T, N_HEADS, HEAD_DIM) for t in (o_cmp, o_sel, o_win)], axis=3).astype(F32)
    o = jnp.sum(gates * branches, axis=3).astype(xn.dtype).reshape(B, T, N_HEADS * HEAD_DIM)
    return o @ w_o

def run_group(x, past_len, wkv0, shift0, past_rows, win_buf, P):
    B, T, _ = x.shape
    q_pos = past_len + jnp.arange(T)
    h = x
    wkv_new, shift_new = [], []
    shared = new_rows = new_win = None
    for layer in range(DEPTH):
        xn = rmsnorm(h, P['ln_mix'][layer])
        if layer < N_A_LAYERS:
            prev = jnp.concatenate([shift0[layer][:, None].astype(xn.dtype), xn[:, :-1]], axis=1)
            rw = [P[n][layer] for n in ('rw_mu', 'rw_wr', 'rw_wk', 'rw_wv', 'rw_wo', 'rw_w0', 'rw_w1', 'rw_w2',
                                        'rw_a0', 'rw_a1', 'rw_a2', 'rw_g1', 'rw_g2', 'rw_kk', 'rw_ka', 'rw_rk',
                                        'rw_lnw', 'rw_lnb')]
            y, s_T = rwkv7_mixer(xn, prev, wkv0[layer], *rw)
            wkv_new.append(s_T)
            shift_new.append(xn[:, -1])
        else:
            if shared is None:
                shared, new_rows, new_win = shared_kv(h, past_len, past_rows, win_buf, P['ln_kv'], P['w_kv'],
                                                      P['cmp_pe'], P['cmp_w1'], P['cmp_b1'], P['cmp_w2'])
            y = nsa_mixer(xn, q_pos, shared, P['nsa_wqg'][layer - N_A_LAYERS], P['nsa_wo'][layer - N_A_LAYERS])
        h = h + y
        moe = [P[n][layer] for n in ('moe_wrg', 'moe_brg', 'moe_wre', 'moe_bre', 'moe_wgate', 'moe_wup', 'moe_wdown')]
        h = h + hmoe(rmsnorm(h, P['ln_ffn'][layer]), *moe)
    return rmsnorm(h, P['ln_out']), jnp.stack(wkv_new), jnp.stack(shift_new), new_rows, new_win

def setup_inputs(seed: int = 0) -> dict:
    key = jax.random.key(seed)
    ks = iter(jax.random.split(key, 64))
    nrm = lambda shape, scale: jax.random.normal(next(ks), shape, jnp.float32) * scale
    D = D_MODEL
    n_pages = PAST_LEN // PAGE_SIZE
    n_used = DEC_BATCH * n_pages
    n_phys = n_used + max(1, n_used // 4)
    win_buf = min(WINDOW, PAST_LEN)
    page_table = jax.random.permutation(next(ks), n_phys)[:n_used].reshape(DEC_BATCH, n_pages).astype(jnp.int32)
    NA, GE = N_A_LAYERS, N_GROUPS * EXPERTS_PER_GROUP
    return {
        'x_prompt': nrm((BATCH, SEQ, D), 1.0),
        'x_sample': nrm((DEC_BATCH, DEC_SEQ, D), 1.0),
        'state_wkv': nrm((NA, DEC_BATCH, RW_HEADS, RW_HEAD, RW_HEAD), 0.5),
        'state_shift': nrm((NA, DEC_BATCH, D), 1.0),
        'cache_kv': nrm((n_phys, PAGE_SIZE, 4, KV_HEADS, HEAD_DIM), 1.0),
        'cache_win': nrm((DEC_BATCH, win_buf, 2, KV_HEADS, HEAD_DIM), 1.0),
        'page_table': page_table,
        'ln_mix': 1.0 + nrm((DEPTH, D), 0.05),
        'ln_ffn': 1.0 + nrm((DEPTH, D), 0.05),
        'ln_kv': 1.0 + nrm((D,), 0.05),
        'ln_out': 1.0 + nrm((D,), 0.05),
        'rw_mu': jax.random.uniform(next(ks), (NA, 6, D), jnp.float32),
        'rw_wr': nrm((NA, D, D), D ** -0.5),
        'rw_wk': nrm((NA, D, D), D ** -0.5),
        'rw_wv': nrm((NA, D, D), D ** -0.5),
        'rw_wo': nrm((NA, D, D), D ** -0.5),
        'rw_w0': jax.random.uniform(next(ks), (NA, D), jnp.float32, minval=-6.0, maxval=-1.0),
        'rw_w1': nrm((NA, D, RW_DECAY_LORA), D ** -0.5),
        'rw_w2': nrm((NA, RW_DECAY_LORA, D), 0.1 * RW_DECAY_LORA ** -0.5),
        'rw_a0': nrm((NA, D), 0.1),
        'rw_a1': nrm((NA, D, RW_AAA_LORA), D ** -0.5),
        'rw_a2': nrm((NA, RW_AAA_LORA, D), 0.5 * RW_AAA_LORA ** -0.5),
        'rw_g1': nrm((NA, D, RW_GATE_LORA), D ** -0.5),
        'rw_g2': nrm((NA, RW_GATE_LORA, D), RW_GATE_LORA ** -0.5),
        'rw_kk': 0.85 + nrm((NA, D), 0.05),
        'rw_ka': 1.0 + nrm((NA, D), 0.05),
        'rw_rk': nrm((NA, RW_HEADS, RW_HEAD), 0.1),
        'rw_lnw': 1.0 + nrm((NA, D), 0.05),
        'rw_lnb': nrm((NA, D), 0.02),
        'w_kv': nrm((D, N_KV_STREAMS * KV_HEADS * HEAD_DIM), D ** -0.5),
        'cmp_pe': nrm((2, CMP_BLOCK, HEAD_DIM), 0.1),
        'cmp_w1': nrm((2, CMP_BLOCK * HEAD_DIM, CMP_HIDDEN), (CMP_BLOCK * HEAD_DIM) ** -0.5),
        'cmp_b1': nrm((2, CMP_HIDDEN), 0.02),
        'cmp_w2': nrm((2, CMP_HIDDEN, HEAD_DIM), CMP_HIDDEN ** -0.5),
        'nsa_wqg': nrm((N_B_LAYERS, D, N_HEADS * HEAD_DIM + 3 * N_HEADS), D ** -0.5),
        'nsa_wo': nrm((N_B_LAYERS, N_HEADS * HEAD_DIM, D), (N_HEADS * HEAD_DIM) ** -0.5),
        'moe_wrg': nrm((DEPTH, D, N_GROUPS), D ** -0.5),
        'moe_brg': nrm((DEPTH, N_GROUPS), 0.01),
        'moe_wre': nrm((DEPTH, D, GE), D ** -0.5),
        'moe_bre': nrm((DEPTH, GE), 0.01),
        'moe_wgate': nrm((DEPTH, N_GROUPS, EXPERTS_PER_GROUP, D, D_EXPERT), D ** -0.5),
        'moe_wup': nrm((DEPTH, N_GROUPS, EXPERTS_PER_GROUP, D, D_EXPERT), D ** -0.5),
        'moe_wdown': nrm((DEPTH, N_GROUPS, EXPERTS_PER_GROUP, D_EXPERT, D), D_EXPERT ** -0.5),
    }

def reference(x_prompt, x_sample, state_wkv, state_shift, cache_kv, cache_win, page_table,
              ln_mix, ln_ffn, ln_kv, ln_out,
              rw_mu, rw_wr, rw_wk, rw_wv, rw_wo, rw_w0, rw_w1, rw_w2, rw_a0, rw_a1, rw_a2, rw_g1, rw_g2,
              rw_kk, rw_ka, rw_rk, rw_lnw, rw_lnb,
              w_kv, cmp_pe, cmp_w1, cmp_b1, cmp_w2, nsa_wqg, nsa_wo,
              moe_wrg, moe_brg, moe_wre, moe_bre, moe_wgate, moe_wup, moe_wdown):
    P = dict(ln_mix=ln_mix, ln_ffn=ln_ffn, ln_kv=ln_kv, ln_out=ln_out,
             rw_mu=rw_mu, rw_wr=rw_wr, rw_wk=rw_wk, rw_wv=rw_wv, rw_wo=rw_wo, rw_w0=rw_w0, rw_w1=rw_w1,
             rw_w2=rw_w2, rw_a0=rw_a0, rw_a1=rw_a1, rw_a2=rw_a2, rw_g1=rw_g1, rw_g2=rw_g2, rw_kk=rw_kk,
             rw_ka=rw_ka, rw_rk=rw_rk, rw_lnw=rw_lnw, rw_lnb=rw_lnb,
             w_kv=w_kv, cmp_pe=cmp_pe, cmp_w1=cmp_w1, cmp_b1=cmp_b1, cmp_w2=cmp_w2,
             nsa_wqg=nsa_wqg, nsa_wo=nsa_wo,
             moe_wrg=moe_wrg, moe_brg=moe_brg, moe_wre=moe_wre, moe_bre=moe_bre,
             moe_wgate=moe_wgate, moe_wup=moe_wup, moe_wdown=moe_wdown)
    Bp = x_prompt.shape[0]
    wkv0 = jnp.zeros((N_A_LAYERS, Bp, RW_HEADS, RW_HEAD, RW_HEAD), F32)
    shift0 = jnp.zeros((N_A_LAYERS, Bp, D_MODEL), x_prompt.dtype)
    y_prompt, p_wkv, p_shift, p_rows, p_win = run_group(x_prompt, 0, wkv0, shift0, None, None, P)
    Bs = x_sample.shape[0]
    past_len = page_table.shape[1] * cache_kv.shape[1]
    past_rows = cache_kv[page_table].reshape(Bs, past_len, *cache_kv.shape[2:])
    y_sample, s_wkv, s_shift, s_rows, s_win = run_group(x_sample, past_len, state_wkv, state_shift, past_rows, cache_win, P)
    return (y_prompt, y_sample, p_wkv, p_shift, p_rows, p_win, s_wkv, s_shift, s_rows, s_win)


_drawn_inputs = setup_inputs


def setup_inputs(seed=0):
    import zlib

    import numpy as np

    out = dict(_drawn_inputs(seed))
    spreads = {}
    factors = {'rw_w1': 5.055, 'rw_w2': 8.0, 'cmp_b1': 5.36, 'moe_brg': 3.783, 'moe_bre': 2.832}
    for name, (base, spread) in spreads.items():
        noise = np.random.default_rng([zlib.crc32(name.encode()), seed]).standard_normal(out[name].shape)
        drawn = base * np.exp(spread * noise) if base else spread * noise
        out[name] = __import__('jax').numpy.asarray(drawn.astype(out[name].dtype))
    for name, factor in factors.items():
        out[name] = (out[name] * factor).astype(out[name].dtype)
    return out
```

```python
from contextlib import ExitStack

import numpy as np
import concourse.bass as bass
from concourse import mybir

F32 = mybir.dt.float32
I32 = mybir.dt.int32
U32 = mybir.dt.uint32
ALU = mybir.AluOpType
ACT = mybir.ActivationFunctionType
AX = mybir.AxisListType
ds = bass.ds

P = 128
D = 1024
KT = D // P
TP = 512
NB = 8
NT = TP + NB
HALF = NT // 2
TT = TP // P
HD = 64
NH = 16
KVH = 4
CH = 64
NCH = TP // CH
PAST = 2048
PAGE = 128
NPG = PAST // PAGE
NPHYS = 160
WIN = 512
SUB = 16
NSUB = PAST // SUB
NCMP_S = NSUB - 1
NCMP_P = TP // SUB - 1
CH_HID = 128
NSB = PAST // HD + 1
NSEL = 16
E = 32
FE = 256
SCALE = HD ** -0.5
EPS = 1e-6
GN_EPS = 64e-5
NEG = -1.0e30

PVEC = ["mu0", "mu1", "mu2", "mu3", "mu4", "mu5", "mix0", "mix1", "ffn0", "ffn1", "kv", "out",
        "w0", "a0", "kk", "ka", "rk", "lnw", "lnb"]

def build_constants():
    cols, parts, at = {}, [], 0

    def put(name, a):
        nonlocal at
        a = np.asarray(a, np.float32)
        full = np.zeros((P, a.shape[1]), np.float32)
        full[:a.shape[0]] = a
        cols[name] = (at, at + a.shape[1])
        at += a.shape[1]
        parts.append(full)

    i, j = np.arange(P)[:, None], np.arange(P)[None, :]
    put("ident", i == j)
    put("ones", np.ones((P, P)))
    put("headones", (i // HD) == (j // HD))
    s, t = np.arange(P)[:, None] % HD, np.arange(HD)[None, :]
    put("ident64", s == t)
    put("before", s < t)
    put("upto", s <= t)
    for lvl in range(6):
        b = 1 << lvl
        put(f"join{lvl}", (s < t) & ((s ^ t) >= b) & ((s ^ t) < 2 * b))
    put("joinT0", ((t < s) & ((s ^ t) >= 1) & ((s ^ t) < 2)))
    put("keep", np.tile((np.arange(TP)[None, :] % CH != 0), (P, 1)))
    put("causal", np.where(j <= i, 0.0, NEG))
    half = 8
    inv = np.power(np.float32(500000.0), -np.arange(half, dtype=np.float32) * np.float32(2.0 / 16))
    pos = np.concatenate([np.arange(TP), np.full(NB, PAST)]).astype(np.float32)
    ang = pos[None, :] * inv[:, None].astype(np.float32)
    cs, sn = np.cos(ang), np.sin(ang)
    c64 = np.ones((HD, NT)); s64 = np.zeros((HD, NT))
    c64[:half] = cs; c64[half:16] = cs
    s64[:half] = -sn; s64[half:16] = sn
    put("cos", np.tile(c64, (2, 1)))
    put("sin", np.tile(s64, (2, 1)))
    perm = np.zeros((P, P))
    for q in range(2):
        for c in range(half):
            perm[q * HD + half + c, q * HD + c] = 1
            perm[q * HD + c, q * HD + half + c] = 1
    put("swap", perm)
    tok = np.arange(TP).reshape(TT, P).T[:, :, None]
    end = (np.arange(NCMP_P) * SUB + 31)[None, None, :]
    put("cmpneg", np.where(end <= tok, 0.0, NEG).reshape(P, -1))
    put("cmpone", (end <= tok).astype(np.float32).reshape(P, -1))
    st = np.arange(NCMP_S)[:, None] * SUB
    bl = np.arange(NSB)[None, :] * HD
    put("overlap", (st < bl + HD) & (st + 31 >= bl))
    hh = np.arange(NH)
    put("samegroup", (hh[:, None] // 4) == (hh[None, :] // 4))
    forced = np.zeros(NSB); forced[[0, NSB - 2, NSB - 1]] = 1
    put("notforced", np.tile(1 - forced, (NH, 1)))
    put("forced", np.tile(forced * 1.0e4, (NH, 1)))
    e = (np.arange(NSB)[None, :] < np.arange(NSB)[:, None]).astype(np.float32).reshape(1, -1)
    put("earlier", np.tile(e, (NH, 1)))
    own = (hh[:, None, None] // 4 == np.arange(KVH)[None, :, None]) * np.ones((1, 1, HD))
    put("ownkv", own.reshape(NH, -1))
    put("tokrow", np.arange(P)[:, None] * 2.0 + 1.0)
    oq = (hh[None, None, :] // 4 % 2 == (np.arange(P) // HD)[:, None, None]) & (hh[None, None, :] // 8 == np.arange(2)[None, :, None])
    put("ownquery", oq.reshape(P, -1))
    put("rank4", np.tile(4.0 - np.arange(4)[None, :], (P, 1)))
    put("rank8", np.tile(8.0 - np.arange(8)[None, :], (P, 1)))
    return cols, np.concatenate(parts, 1)


CCOL, CONSTS = build_constants()
NCONST = CONSTS.shape[1]



class Core:

    def __init__(self, nc, io):
        self.nc, self.io = nc, io
        self.n, self.last_sems = 0, []
        self.comb = nc.dram_tensor("combination_weights", [E, NT], F32).ap()
        self.slots = nc.alloc_sbuf_tensor("slots", [P, 10 * KT * NT], F32)
        self.work = nc.alloc_sbuf_tensor("work", [P, 8320], F32)
        self.base = nc.alloc_sbuf_tensor("base_constants", [P, 384], F32)
        self.par = nc.alloc_sbuf_tensor("parameters", [P, 8 * len(PVEC)], F32)
        self.small = nc.alloc_sbuf_tensor("small", [P, 704], F32)
        self.z_state = nc.alloc_sbuf_tensor("z_state", [P, KT * HD], F32)
        psum = nc.alloc_psum_tensor("banks", [P, 8, 512], F32)
        self.bank = [psum[:, b, :] for b in range(8)]
        self.pair = [psum[:, 2 * b:2 * b + 2, 0:NT // 2] for b in range(4)]
        self.ident, self.ones, self.headones = (self.base[:, 128 * n:128 * n + 128] for n in range(3))

        keep = nc.alloc_sbuf_tensor("keep", [P, 840], F32)
        self.gate = keep[:, 0:240].rearrange("p (n g) -> p n g", n=TT + 1)
        self.kv_sample = keep[:, 240:336].rearrange("p (k b) -> p k b", b=NB)
        self.cmp_keys = keep[:, 336:336 + 4 * NCMP_P].rearrange("p (g n) -> p g n", g=KVH)
        self.cmp_values = keep[:, 464:464 + KVH * HD]
        self.cmp_bias = keep[:, 720:722]
        self.query_mask = keep[:, 724:756]
        self.queries = keep[:, 756:820].rearrange("p (a g h) -> p a g h", a=2, g=2)
        self.gate_rows = nc.dram_tensor("sample_gates", [NB, 3 * NH], F32).ap()
        self.query_rows = nc.dram_tensor("sample_queries", [2, NB, D], F32).ap()
        self.prompt_keys = self.slots[:, 8 * KT * NT:8 * KT * NT + 4096].rearrange("p (a g t) -> p a g t", a=2, g=KVH)

    def slot(self, n):
        return self.slots[:, n * KT * NT:(n + 1) * KT * NT].rearrange("p (k t) -> p k t", t=NT)

    def flat(self, n, count=1):
        return self.slots[:, n * KT * NT:(n + count) * KT * NT]

    def vec(self, name, k):
        c = 8 * PVEC.index(name) + k
        return self.par[:, c:c + 1]

    def stage(self, name):
        self.n += 1
        return Stage(self, f"{self.n}_{name}")


class Stage:

    def __init__(self, core, name):
        self.nc, self.core, self.name = core.nc, core, name

    def __enter__(self):
        self.ctx, self.sems, self.last, self.starts = ExitStack(), [], self.core.last_sems, []
        return self

    def sem(self, name, start=0):
        self.sems.append(self.nc.alloc_semaphore(f"{name}_{self.name}"))
        if start:
            self.starts.append((self.sems[-1], start))
        return self.sems[-1]

    def block(self):
        self.nc.clear_and_free_semaphores(self.last)
        for sem, start in self.starts:
            self.nc.gpsimd.sem_inc(sem, start)
        if self.starts:
            self.nc.all_engine_barrier()
        return self.ctx.enter_context(self.nc.Block())

    def __exit__(self, *a):
        self.ctx.close()
        self.core.last_sems = self.sems


def load_parameters(c):
    nc, io = c.nc, c.io
    nv = len(PVEC) * 8
    rows = c.work[:, 0:256]
    src = [io["rw_mu"][0, n, :] for n in range(6)] + [
        io["ln_mix"][0, :], io["ln_mix"][1, :], io["ln_ffn"][0, :], io["ln_ffn"][1, :], io["ln_kv"][:],
        io["ln_out"][:], io["rw_w0"][0, :], io["rw_a0"][0, :], io["rw_kk"][0, :], io["rw_ka"][0, :],
        io["rw_rk"][0, :, :].rearrange("h d -> (h d)"), io["rw_lnw"][0, :], io["rw_lnb"][0, :]]
    with c.stage("parameters") as st:
        loaded, cleared, turned = st.sem("vectors_loaded"), st.sem("rows_cleared"), st.sem("columns_in_psum")
        block = st.block()

        @block.sync
        def _(sp):
            sp.dma_start(c.base[:, :], io["consts"][:, 0:384]).then_inc(loaded, 16)
            sp.wait_ge(cleared, 1)
            for n, v in enumerate(src):
                r, half = (8 * n) % P, (8 * n) // P
                sp.dma_start(rows[r:r + 8, half * P:half * P + P],
                             v.rearrange("(k p) -> k p", p=P)).then_inc(loaded, 16)

        @block.vector
        def _(dve):
            nc.vector.memset(rows, 0.0).then_inc(cleared, 1)
            dve.wait_ge(turned, 1)
            nc.vector.tensor_copy(c.par[:, 0:nv], c.bank[0][:, 0:nv])

        @block.tensor
        def _(pe):
            pe.wait_ge(loaded, 16 * (len(src) + 1))
            nc.tensor.transpose(c.bank[0][:, 0:P], rows[:, 0:P], c.ident)
            nc.tensor.transpose(c.bank[0][:, P:2 * P], rows[:, P:2 * P], c.ident).then_inc(turned, 1)


def load_tokens(c):
    nc, io = c.nc, c.io
    h, prev = c.slot(0), c.slot(2)
    tiles = [(io["x_prompt"][0, P * n:P * n + P, :], h, P * n, P) for n in range(TT)]
    tiles += [(io["x_sample"][:, 0, :], h, TP, NB), (io["state_shift"][0, :, :], prev, TP, NB)]
    with c.stage("tokens") as st:
        loaded, turned, moved = st.sem("rows_loaded"), st.sem("tile_in_psum"), st.sem("tile_moved")
        block = st.block()
        rows = [c.work[:, D * n:D * n + D] for n in range(len(tiles))]

        @block.sync
        def _(sp):
            for n, (src, _, _, m) in enumerate(tiles):
                sp.dma_start(rows[n][0:m, :], src).then_inc(loaded, 16)

        @block.tensor
        def _(pe):
            pe.wait_ge(loaded, 16 * len(tiles))
            for n, (_, _, _, m) in enumerate(tiles):
                if n >= 2:
                    pe.wait_ge(moved, 2 * (n - 1))
                for k in range(KT):
                    out = c.bank[2 * (n % 2) + k // 4][:, P * (k % 4):P * (k % 4) + m]
                    last = nc.tensor.transpose(out, rows[n][0:m, P * k:P * k + P], c.ident[0:m, 0:m])
                last.then_inc(turned, 1)

        @block.vector
        def _(dve):
            for n, (_, dst, t0, m) in enumerate(tiles):
                dve.wait_ge(turned, n + 1)
                for a in range(2):
                    src = c.bank[2 * (n % 2) + a][:, :].rearrange("p (k t) -> p k t", t=P)
                    nc.vector.tensor_copy(dst[:, 4 * a:4 * a + 4, t0:t0 + m], src[:, :, 0:m]).then_inc(moved, 1)


def rms_norm(c, src, gain, dst, square):
    nc = c.nc
    rstd = c.work[:, 0:NT]
    with c.stage("norm_" + gain) as st:
        squared, summed = st.sem("squares_ready"), st.sem("sums_in_psum")
        means, roots = st.sem("means_ready"), st.sem("roots_ready")
        block = st.block()

        @block.scalar
        def _(act):
            for k in range(KT):
                nc.scalar.activation(square[:, k, :], src[:, k, :], ACT.Square).then_inc(squared, 1)
            act.wait_ge(means, 1)
            nc.scalar.activation(rstd, rstd, ACT.Sqrt).then_inc(roots, 1)

        @block.tensor
        def _(pe):
            for k in range(KT):
                pe.wait_ge(squared, k + 1)
                nc.tensor.matmul(c.bank[0][:, :], c.ones, square[:, k, 0:TP], start=(k == 0), stop=(k == KT - 1))
                last = nc.tensor.matmul(c.bank[1][:, 0:NB], c.ones, square[:, k, TP:NT],
                                        start=(k == 0), stop=(k == KT - 1))
            last.then_inc(summed, 1)

        @block.vector
        def _(dve):
            dve.wait_ge(summed, 1)
            for bank, a, b in ((0, 0, TP), (1, TP, NT)):
                nc.vector.tensor_scalar(rstd[:, a:b], c.bank[bank][:, 0:b - a], 1.0 / D, EPS, ALU.mult, ALU.add)
            dve.drain().then_inc(means, 1)
            dve.wait_ge(roots, 1)
            nc.vector.reciprocal(rstd, rstd)
            dve.drain()
            for k in range(KT):
                nc.vector.scalar_tensor_tensor(dst[:, k, :], src[:, k, :], c.vec(gain, k), rstd, ALU.mult, ALU.mult)


def project(c, name, x, kt, weight, tiles, evacuate, engine, out_rows=P):
    nc = c.nc
    U = 4 if tiles % 4 == 0 else 1
    ring = [c.work[:, kt * out_rows * u:kt * out_rows * (u + 1)].rearrange("p (k n) -> p k n", n=out_rows)
            for u in range(U)]
    wv = weight.rearrange("(k p) n -> p k n", p=P)
    with c.stage(name) as st:
        ready = [st.sem(f"weight_ready{u}") for u in range(U)]
        done, free = st.sem("tiles_done"), st.sem("bank_free")
        block = st.block()

        @block.sync
        def _(sp):
            with sp.Fori(0, tiles // U) as i:
                for u in range(U):
                    sp.wait_ge(done, i * U + (u + 1))
                    sp.dma_start(ring[u], wv[:, :, ds((i * U + u) * out_rows, out_rows)]).then_inc(ready[u], 16)

        @block.tensor
        def _(pe):
            pe.sem_inc(done, U)
            with pe.Fori(0, tiles // U) as i:
                for u in range(U):
                    pe.wait_ge(ready[u], i * 16 + 16)
                    pe.wait_ge(free, i * U + (u + 1))
                    for k in range(kt):
                        for s in range(2):
                            last = nc.tensor.matmul(c.pair[u][0:out_rows, s, :], ring[u][:, k, :],
                                                    x[:, k, HALF * s:HALF * s + HALF],
                                                    start=(k == 0), stop=(k == kt - 1))
                    last.then_inc(done, 1)

        def copies(eng):
            eng.sem_inc(free, U)
            with eng.Fori(0, tiles // U) as i:
                for u in range(U):
                    eng.wait_ge(done, i * U + (U + u + 1))
                    evacuate(eng, i * U + u, c.pair[u][0:out_rows]).then_inc(free, 1)

        if engine == "act":
            block.scalar(copies)
        else:
            block.vector(copies)


def copy_to(c, dst, rows=P):
    def evacuate(eng, m, tile):
        return c.nc.scalar.activation(dst[0:rows, ds(m, 1), :].rearrange("p a (s t) -> p (a s) t", s=2), tile,
                                      ACT.Copy)
    return evacuate


def add_to(c, dst):
    def evacuate(eng, m, tile):
        o = dst[:, ds(m, 1), :].rearrange("p a (s t) -> p (a s) t", s=2)
        return c.nc.vector.tensor_tensor(o, o, tile, ALU.add)
    return evacuate


def elementwise(c, name, body):
    with c.stage(name) as st:
        block = st.block()

        @block.vector
        def _(dve):
            body(dve)


def transpose_out(c, name, src, cols, stores):
    nc = c.nc
    with c.stage(name) as st:
        turned, moved, stored = st.sem("rows_in_psum"), st.sem("rows_moved"), st.sem("rows_stored")
        block = st.block()

        @block.tensor
        def _(pe):
            for n, (a, b, _) in enumerate(stores):
                if n >= 2:
                    pe.wait_ge(moved, 2 * (n - 1))
                for k in range(KT):
                    last = nc.tensor.transpose(c.bank[2 * (n % 2) + k // 4][0:b - a, P * (k % 4):P * (k % 4) + P],
                                               src[:, k, a:b], c.ident)
                last.then_inc(turned, 1)

        @block.vector
        def _(dve):
            for n, (a, b, _) in enumerate(stores):
                dve.wait_ge(turned, n + 1)
                for k in range(2):
                    nc.vector.tensor_copy(c.work[0:b - a, D * n + 512 * k:D * n + 512 * k + 512],
                                          c.bank[2 * (n % 2) + k][0:b - a, :]).then_inc(moved, 1)

        @block.sync
        def _(sp):
            for n, (a, b, dst) in enumerate(stores):
                sp.wait_ge(moved, 2 * (n + 1))
                sp.dma_start(dst, c.work[0:b - a, D * n:D * n + D]).then_inc(stored, 16)
            sp.wait_ge(stored, 16 * len(stores))



def rwkv_inputs(c):
    nc, io = c.nc, c.io
    xn, xx, xi = c.slot(1), c.slot(2), c.slot(3)

    def differences(dve):
        nc.vector.tensor_tensor(xx[:, :, 1:TP], xn[:, :, 0:TP - 1], xn[:, :, 1:TP], ALU.subtract)
        nc.vector.tensor_scalar(xx[:, :, 0:1], xn[:, :, 0:1], -1.0, None, ALU.mult)
        nc.vector.tensor_tensor(xx[:, :, TP:NT], xx[:, :, TP:NT], xn[:, :, TP:NT], ALU.subtract)

    elementwise(c, "shift", differences)

    def mixed(n):
        def body(dve):
            for k in range(KT):
                nc.vector.scalar_tensor_tensor(xi[:, k, :], xx[:, k, :], c.vec(f"mu{n}", k), xn[:, k, :],
                                               ALU.mult, ALU.add)
        elementwise(c, f"mix{n}", body)

    hidden = c.slots[:, 4160 * 9:4160 * 9 + NT].rearrange("p (a t) -> p a t", a=1)

    def squash(func, rows):
        def evacuate(eng, m, tile):
            return nc.scalar.activation(hidden[0:rows, 0, :].rearrange("p (s t) -> p s t", s=2), tile, func)
        return evacuate

    def second(name, weight, rows, dst, bias):
        w2 = c.work[0:rows, 4096:4096 + D]
        with c.stage(name) as st:
            ready, full, free = st.sem("weight_ready"), st.sem("bank_full"), st.sem("bank_free")
            block = st.block()

            @block.sync
            def _(sp):
                sp.dma_start(w2, weight).then_inc(ready, 16)

            @block.tensor
            def _(pe):
                pe.wait_ge(ready, 16)
                for m in range(KT):
                    if m >= 4:
                        pe.wait_ge(free, m - 3)
                    for s in range(2):
                        last = nc.tensor.matmul(c.pair[m % 4][:, s, :], w2[:, P * m:P * m + P],
                                                hidden[0:rows, 0, HALF * s:HALF * s + HALF], start=True, stop=True)
                    last.then_inc(full, 1)

            @block.scalar
            def _(act):
                for m in range(KT):
                    act.wait_ge(full, m + 1)
                    o = dst[:, m, :].rearrange("p (s t) -> p s t", s=2)
                    if bias:
                        nc.scalar.activation(o, c.pair[m % 4], ACT.Sigmoid, bias=c.vec(bias, m)).then_inc(free, 1)
                    else:
                        nc.scalar.activation(o, c.pair[m % 4], ACT.Copy).then_inc(free, 1)

    for n, w, dst in ((0, "rw_wr", 4), (2, "rw_wk", 5), (3, "rw_wv", 6)):
        mixed(n)
        project(c, w, xi, KT, io[w][0, :, :], KT, copy_to(c, c.slot(dst)), "act")
    mixed(1)
    project(c, "rw_w1", xi, KT, io["rw_w1"][0, :, :], 1, squash(ACT.Tanh, 64), "act", 64)
    second("rw_w2", io["rw_w2"][0, :, :], 64, c.slot(7), "w0")
    mixed(4)
    project(c, "rw_a1", xi, KT, io["rw_a1"][0, :, :], 1, squash(ACT.Copy, 64), "act", 64)
    second("rw_a2", io["rw_a2"][0, :, :], 64, c.slot(8), "a0")
    mixed(5)
    project(c, "rw_g1", xi, KT, io["rw_g1"][0, :, :], 1, squash(ACT.Sigmoid, P), "act")
    second("rw_g2", io["rw_g2"][0, :, :], P, c.slot(1), None)
    elementwise(c, "gate_home", lambda dve: nc.vector.tensor_copy(c.flat(9), c.flat(1)))


def rwkv_prepare(c):
    nc, io = c.nc, c.io
    r, k_, v, w, a = (c.slot(n) for n in range(4, 9))
    kk, tmp, bonus = c.slot(1), c.slot(2), c.slot(3)
    keep = c.work[:, 0:TP]
    norm = [c.work[:, TP + NT * n:TP + NT * (n + 1)] for n in range(2)]
    ends = c.small[:, 0:KT * NCH].rearrange("p (k n) -> p k n", n=NCH)
    NLOG = -float(np.exp(-0.5))
    with c.stage("rwkv_prepare") as st:
        keep_in = st.sem("keep_loaded")
        sq, nrm, nfree = st.sem("squares_ready"), st.sem("norms_in_psum"), st.sem("norms_used")
        rk, bon, bfree = st.sem("rk_ready"), st.sem("bonus_in_psum"), st.sem("bonus_used")
        g_ready, ex, done = st.sem("decay_sums_ready"), st.sem("factors_ready"), st.sem("tile_done")
        roots = st.sem("norms_inverted")
        block = st.block()

        @block.sync
        def _(sp):
            lo, hi = CCOL["keep"]
            sp.dma_start(keep, io["consts"][:, lo:hi]).then_inc(keep_in, 16)

        @block.vector
        def _(dve):
            dve.wait_ge(keep_in, 16)
            for k in range(KT):
                nc.vector.tensor_scalar(kk[:, k, :], k_[:, k, :], c.vec("kk", k), None, ALU.mult)
                dve.drain()
                nc.vector.tensor_tensor(tmp[:, k, :], kk[:, k, :], kk[:, k, :], ALU.mult).then_inc(sq, 1)
                nc.vector.tensor_scalar(bonus[:, k, :], a[:, k, :], -1.0, c.vec("ka", k), ALU.add, ALU.mult)
                dve.drain()
                nc.vector.scalar_tensor_tensor(k_[:, k, :], bonus[:, k, :], 1.0, k_[:, k, :], ALU.add, ALU.mult)
                dve.drain()
                nc.vector.scalar_tensor_tensor(bonus[:, k, :], r[:, k, :], c.vec("rk", k), k_[:, k, :],
                                               ALU.mult, ALU.mult).then_inc(rk, 1)
                dve.wait_ge(nrm, k + 1)
                rn = norm[k % 2]
                for bank, lo, hi in ((0, 0, TP), (1, TP, NT)):
                    nc.vector.tensor_scalar(rn[:, lo:hi], c.bank[bank][:, 0:hi - lo], 1e-24, None, ALU.max)
                dve.drain().then_inc(nfree, 1)
                dve.wait_ge(roots, k + 1)
                nc.vector.reciprocal(rn, rn)
                dve.drain()
                nc.vector.tensor_tensor(kk[:, k, :], kk[:, k, :], rn, ALU.mult)
                dve.drain()
                nc.vector.tensor_tensor(a[:, k, :], a[:, k, :], kk[:, k, :], ALU.mult)
                dve.wait_ge(bon, k + 1)
                for bank, lo, hi in ((2, 0, TP), (3, TP, NT)):
                    last = nc.vector.tensor_tensor(bonus[:, k, lo:hi], c.bank[bank][:, 0:hi - lo], v[:, k, lo:hi],
                                                   ALU.mult)
                last.then_inc(bfree, 1)
                nc.vector.tensor_scalar(w[:, k, :], w[:, k, :], NLOG, None, ALU.mult)
                dve.drain()
                nc.vector.tensor_tensor_scan(tmp[:, k, 0:TP], keep, w[:, k, 0:TP], 0.0, ALU.mult, ALU.add)
                dve.drain()
                nc.vector.tensor_copy(ends[:, k, :], tmp[:, k, CH - 1:TP:CH])
                nc.vector.tensor_tensor(w[:, k, 0:TP], tmp[:, k, 0:TP], w[:, k, 0:TP],
                                        ALU.subtract).then_inc(g_ready, 1)

        @block.tensor
        def _(pe):
            for k in range(KT):
                if k >= 1:
                    pe.wait_ge(nfree, k)
                pe.wait_ge(sq, k + 1)
                nc.tensor.matmul(c.bank[0][:, :], c.headones, tmp[:, k, 0:TP], start=True, stop=True)
                nc.tensor.matmul(c.bank[1][:, 0:NB], c.headones, tmp[:, k, TP:NT], start=True,
                                 stop=True).then_inc(nrm, 1)
                if k >= 1:
                    pe.wait_ge(bfree, k)
                pe.wait_ge(rk, k + 1)
                nc.tensor.matmul(c.bank[2][:, :], c.headones, bonus[:, k, 0:TP], start=True, stop=True)
                nc.tensor.matmul(c.bank[3][:, 0:NB], c.headones, bonus[:, k, TP:NT], start=True,
                                 stop=True).then_inc(bon, 1)

        @block.scalar
        def _(act):
            for k in range(KT):
                act.wait_ge(nfree, k + 1)
                nc.scalar.activation(norm[k % 2], norm[k % 2], ACT.Sqrt).then_inc(roots, 1)
                act.wait_ge(g_ready, k + 1)
                nc.scalar.activation(ends[:, k, :], ends[:, k, :], ACT.Exp)
                nc.scalar.activation(w[:, k, :], w[:, k, :], ACT.Exp)

    prompt = slice(0, TP)
    with c.stage("rwkv_scale") as st:
        up, down = st.sem("growth_ready"), st.sem("shrink_ready")
        used = st.sem("growth_used")
        block = st.block()
        bufs = [c.work[:, 2048 + TP * n:2048 + TP * (n + 1)] for n in range(4)]

        @block.scalar
        def _(act):
            for k in range(KT):
                if k >= 2:
                    act.wait_ge(used, k - 1)
                nc.scalar.activation(bufs[k % 2], tmp[:, k, prompt], ACT.Exp)
                nc.scalar.activation(bufs[2 + k % 2], tmp[:, k, prompt], ACT.Exp, scale=-1.0).then_inc(up, 1)

        @block.vector
        def _(dve):
            for k in range(KT):
                nc.vector.scalar_tensor_tensor(w[:, k, prompt], kk[:, k, prompt], -1.0, w[:, k, prompt],
                                               ALU.mult, ALU.mult)
                dve.wait_ge(up, k + 1)
                nc.vector.tensor_tensor(r[:, k, prompt], r[:, k, prompt], bufs[k % 2], ALU.mult)
                nc.vector.tensor_tensor(k_[:, k, prompt], k_[:, k, prompt], bufs[2 + k % 2], ALU.mult)
                nc.vector.tensor_tensor(a[:, k, prompt], a[:, k, prompt], bufs[2 + k % 2], ALU.mult).then_inc(used, 1)


def sample_state(c):
    nc, io = c.nc, c.io
    arrays = [c.slot(4), c.slot(5), c.slot(6), c.slot(7), c.slot(1), c.slot(8)]
    scratch = nc.dram_tensor("sample_vectors", [6, NB, D], F32).ap()
    out_scratch = nc.dram_tensor("sample_mixed", [NB, D], F32).ap()
    rows = c.work[0:NB, 0:6 * D].rearrange("b (n e) -> b n e", e=D)
    with c.stage("sample_vectors") as st:
        turned, moved, stored = st.sem("rows_in_psum"), st.sem("rows_moved"), st.sem("rows_stored")
        block = st.block()

        @block.tensor
        def _(pe):
            for n, a in enumerate(arrays):
                if n >= 2:
                    pe.wait_ge(moved, 2 * (n - 1))
                for k in range(KT):
                    last = nc.tensor.transpose(c.bank[2 * (n % 2) + k // 4][0:NB, P * (k % 4):P * (k % 4) + P],
                                               a[:, k, TP:NT], c.ident)
                last.then_inc(turned, 1)

        @block.vector
        def _(dve):
            for n in range(6):
                dve.wait_ge(turned, n + 1)
                for k in range(2):
                    nc.vector.tensor_copy(rows[:, n, 512 * k:512 * k + 512],
                                          c.bank[2 * (n % 2) + k][0:NB, :]).then_inc(moved, 1)

        @block.sync
        def _(sp):
            sp.wait_ge(moved, 12)
            sp.dma_start(scratch.rearrange("n b e -> b n e"), rows).then_inc(stored, 16)
            sp.wait_ge(stored, 16)

    S = c.flat(1)[:, 0:HD * HD].rearrange("p (i j) -> p i j", j=HD)
    t1 = c.flat(2)[:, 0:HD * HD].rearrange("p (i j) -> p i j", j=HD)
    t2 = c.work[:, 0:HD * HD].rearrange("p (i j) -> p i j", j=HD)
    vec = c.work[:, 4096:4096 + 6 * HD].rearrange("p (n d) -> p n d", d=HD)
    sa, o = c.work[:, 4608:4608 + HD], c.work[:, 4672:4672 + HD]
    key = lambda n: vec[:, n, :].unsqueeze(1).to_broadcast([P, HD, HD])
    val = lambda a: a.unsqueeze(2).to_broadcast([P, HD, HD])
    with c.stage("sample_state") as st:
        loaded, stepped, mixed, stored = (st.sem(n) for n in ("state_loaded", "state_stepped", "output_ready",
                                                              "stored"))
        block = st.block()

        @block.sync
        def _(sp):
            sp.dma_start(vec, scratch.rearrange("n b (h d) -> (b h) n d", d=HD)).then_inc(loaded, 16)
            sp.dma_start(S, io["state_wkv"][0].rearrange("b h i j -> (b h) i j")).then_inc(loaded, 16)
            sp.wait_ge(stepped, 1)
            sp.dma_start(io["o_sample_wkv"][0].rearrange("b h i j -> (b h) i j"), S).then_inc(stored, 16)
            sp.wait_ge(mixed, 1)
            sp.dma_start(out_scratch.rearrange("b (h d) -> (b h) d", d=HD), o).then_inc(stored, 16)
            sp.wait_ge(stored, 32)

        @block.vector
        def _(dve):
            tt = nc.vector.tensor_tensor
            dve.wait_ge(loaded, 32)
            tt(t1, S, key(4), ALU.mult)
            tt(t2, key(1), val(vec[:, 2, :]), ALU.mult)
            dve.drain()
            nc.vector.tensor_reduce(sa, t1, AX.X, ALU.add)
            tt(S, S, key(3), ALU.mult)
            dve.drain()
            tt(t1, key(5), val(sa), ALU.mult)
            tt(S, S, t2, ALU.add)
            dve.drain()
            tt(S, S, t1, ALU.subtract)
            dve.drain().then_inc(stepped, 1)
            tt(t1, S, key(0), ALU.mult)
            dve.drain()
            nc.vector.tensor_reduce(o, t1, AX.X, ALU.add).then_inc(mixed, 1)

    back = c.work[0:NB, 0:D]
    with c.stage("sample_output") as st:
        loaded, turned = st.sem("rows_loaded"), st.sem("columns_in_psum")
        block = st.block()

        @block.sync
        def _(sp):
            sp.dma_start(back, out_scratch).then_inc(loaded, 16)

        @block.tensor
        def _(pe):
            pe.wait_ge(loaded, 16)
            for k in range(KT):
                last = nc.tensor.transpose(c.bank[0][:, NB * k:NB * k + NB], back[:, P * k:P * k + P],
                                           c.ident[0:NB, 0:NB])
            last.then_inc(turned, 1)

        @block.vector
        def _(dve):
            dve.wait_ge(turned, 1)
            nc.vector.tensor_copy(c.slot(4)[:, :, TP:NT], c.bank[0][:, 0:NB * KT].rearrange("p (k b) -> p k b", b=NB))


def rwkv_chunks(c):
    nc, io = c.nc, c.io
    lo, hi = CCOL["ident64"][0], CCOL["joinT0"][1]
    table = c.small[:, 64:64 + hi - lo]
    const = lambda name: table[:, CCOL[name][0] - lo:CCOL[name][1] - lo]
    wide = lambda a: a.unsqueeze(1).to_broadcast([P, KT, CH])
    ends = c.small[:, 0:KT * NCH].rearrange("p (k n) -> p k n", n=NCH)
    area = [c.flat(1, 2), c.work[:, :]]
    names = ["r", "k", "a", "b", "v", "LT", "join", "T", "TT", "X", "MT", "AB", "AK", "Bt", "Kt", "Vt"]
    buf = [{n: area[u][:, 512 * x:512 * x + 512].rearrange("p (k t) -> p k t", t=CH)
            for x, n in enumerate(names)} for u in range(2)]
    for u in range(2):
        buf[u]["RHS"], buf[u]["U"] = buf[u]["X"], buf[u]["T"]
    Z = c.z_state[:, :].rearrange("p (k i) -> p k i", i=HD)
    src = {"r": c.slot(4), "k": c.slot(5), "v": c.slot(6), "a": c.slot(7), "b": c.slot(8)}

    order = [(u, n) for u in range(2) for n in ("LT", "L")]
    filler = {1: ["MT", "AB"], 2: ["AK"], 3: ["Bt"], 4: ["Kt"], 5: ["Vt"]}
    for lvl in range(1, 6):
        order += [(u, f"X{lvl}") for u in range(2)]
        order += [(u, n) for n in filler[lvl] for u in range(2)]
        order += [(u, f"{n}{lvl}") for u in range(2) for n in (("T", "TT") if lvl < 5 else ("TT",))]
    order += [(u, n) for u in range(2) for n in ("RHS", "U", "O", "Z")]
    place, per_round = {}, [0] * 8
    for u in range(2):
        for x, n in enumerate([n for v, n in order if v == u]):
            b = 4 * u + x % 4
            place[u, n] = (b, per_round[b])
            per_round[b] += 1

    with c.stage("rwkv_chunks") as st:
        table_in = st.sem("masks_loaded")
        chunk_ready = [st.sem(f"chunk_ready{u}") for u in range(2)]
        joins = [st.sem(f"join_ready{u}") for u in range(2)]
        state_ready = st.sem("state_ready", 1)
        full = [st.sem(f"product_in_bank{b}") for b in range(8)]
        taken = [st.sem(f"product_taken{b}", 1) for b in range(8)]
        block = st.block()

        def produced(eng, i, u, name):
            b, n = place[u, name]
            eng.wait_ge(full[b], i * per_round[b] + (n + 1))

        def in_sbuf(eng, i, u, names, before=None):
            least = {}
            for name in names:
                b, n = place[u, name]
                least[b] = max(least.get(b, 0), n + 1)
            if before:
                b, n = place[u, before]
                least[b] = max(least.get(b, 0), n)
            for b, n in least.items():
                eng.wait_ge(taken[b], i * per_round[b] + (n + 1))

        def bank(u, name):
            return c.bank[place[u, name][0]][:, :].rearrange("p (k t) -> p k t", t=CH)

        @block.sync
        def _(sp):
            sp.dma_start(table, io["consts"][:, lo:hi]).then_inc(table_in, 16)

        @block.tensor
        def _(pe):
            pe.wait_ge(table_in, 16)

            def product(i, u, name, terms, needs=()):
                b = place[u, name][0]
                in_sbuf(pe, i, u, needs, before=name)
                pe.nop(nofuse=True)
                out = bank(u, name)
                for k in range(KT):
                    for q in range(2):
                        half = slice(HD * q, HD * q + HD)
                        for x, (lhsT, rhs) in enumerate(terms):
                            right = const("ident64")[half, :] if rhs is None else rhs[half, k, :]
                            last = nc.tensor.matmul(out[half, k, :], lhsT[half, k, :], right,
                                                    start=(x == 0), stop=(x == len(terms) - 1))
                return last.then_inc(full[b], 1)

            with pe.Fori(0, NCH // 2) as i:
                for u in range(2):
                    w = buf[u]
                    pe.wait_ge(chunk_ready[u], i * 5 + 5)
                    product(i, u, "LT", [(w["b"], w["a"])])
                    product(i, u, "L", [(w["a"], w["b"])])
                for lvl in range(1, 6):
                    for u in range(2):
                        w = buf[u]
                        pe.wait_ge(joins[u], i * 5 + lvl)
                        product(i, u, f"X{lvl}", [(w["join"], w["T"])], ["L" if lvl == 1 else f"T{lvl - 1}"])
                    for name in filler[lvl]:
                        for u in range(2):
                            w = buf[u]
                            product(i, u, name, {
                                "MT": [(w["k"], w["a"])], "AB": [(w["b"], w["r"])], "AK": [(w["k"], w["r"])],
                                "Bt": [(w["b"], None)], "Kt": [(w["k"], None)], "Vt": [(w["v"], None)]}[name])
                    for u in range(2):
                        w = buf[u]
                        needs = [f"X{lvl}", "LT" if lvl == 1 else f"TT{lvl - 1}"]
                        if lvl < 5:
                            product(i, u, f"T{lvl}", [(w["TT"], w["X"])], needs)
                        product(i, u, f"TT{lvl}", [(w["X"], w["TT"])], needs)
                for u in range(2):
                    w = buf[u]
                    pe.wait_ge(state_ready, i * 2 + (u + 2))
                    product(i, u, "RHS", [(w["a"], Z), (w["MT"], w["Vt"])], ["MT", "Vt"])
                    product(i, u, "U", [(w["TT"], w["RHS"])], ["TT5", "RHS"])
                    product(i, u, "O", [(Z, w["r"]), (w["U"], w["AB"]), (w["Vt"], w["AK"])], ["U", "AB", "AK"])
                    product(i, u, "Z", [(w["Bt"], w["U"]), (w["Kt"], w["Vt"])], ["Bt", "Kt"])

        def take(eng, i, u, name, op):
            produced(eng, i, u, name)
            op(bank(u, name)).then_inc(taken[place[u, name][0]], 1)

        @block.scalar
        def _(act):
            with act.Fori(0, NCH // 2) as i:
                for u in range(2):
                    act.wait_ge(state_ready, i * 2 + (u + 1))
                    for n in ("a", "v"):
                        nc.scalar.copy(buf[u][n], src[n][:, :, ds(i * 2 * CH + u * CH, CH)]).then_inc(chunk_ready[u], 1)
                for u, name in order:
                    stem = name.rstrip("0123456789")
                    if stem in ("X", "Bt", "Kt", "Vt", "RHS", "U"):
                        take(act, i, u, name, lambda p: nc.scalar.copy(buf[u][stem], p))
                    if stem == "O":
                        take(act, i, u, name,
                             lambda p: nc.scalar.copy(c.slot(4)[:, :, ds(i * 2 * CH + u * CH, CH)], p))

        @block.gpsimd
        def _(pool):
            pool.wait_ge(table_in, 16)
            with pool.Fori(0, NCH // 2) as i:
                for u in range(2):
                    pool.wait_ge(state_ready, i * 2 + (u + 1))
                    for n in ("b", "r", "k"):
                        nc.gpsimd.tensor_copy(buf[u][n],
                                              src[n][:, :, ds(i * 2 * CH + u * CH, CH)]).then_inc(chunk_ready[u], 1)
                for lvl in range(1, 6):
                    for u in range(2):
                        if lvl == 1:
                            in_sbuf(pool, i, u, ["LT"])
                        else:
                            produced(pool, i, u, f"X{lvl - 1}")
                        nc.gpsimd.tensor_tensor(buf[u]["join"], buf[u]["LT"], wide(const(f"join{lvl}")),
                                                ALU.mult).then_inc(joins[u], 1)

        @block.vector
        def _(dve):
            nc.vector.memset(Z, 0.0).then_inc(state_ready, 1)
            dve.wait_ge(table_in, 16)
            tt = nc.vector.tensor_tensor
            with dve.Fori(0, NCH // 2) as i:
                for u, name in order:
                    w = buf[u]
                    stem = name.rstrip("0123456789")
                    if name == "LT":
                        produced(dve, i, u, name)
                        nc.vector.tensor_copy(w["LT"], bank(u, name))
                        tt(w["TT"], bank(u, name), wide(const("join0")), ALU.mult)
                        dve.drain()
                        tt(w["TT"], w["TT"], wide(const("ident64")), ALU.add).then_inc(taken[place[u, name][0]], 1)
                    if name == "L":
                        produced(dve, i, u, name)
                        tt(w["T"], bank(u, name), wide(const("joinT0")), ALU.mult)
                        dve.drain()
                        tt(w["T"], w["T"], wide(const("ident64")), ALU.add).then_inc(taken[place[u, name][0]], 1)
                    if name in ("MT", "AB", "AK"):
                        mask = const("before" if name == "MT" else "upto")
                        take(dve, i, u, name, lambda p: tt(w[name], p, wide(mask), ALU.mult))
                    if stem in ("T", "TT"):
                        take(dve, i, u, name, lambda p: tt(w[stem], w[stem], p, ALU.add))
                    if name == "Z":
                        take(dve, i, u, name, lambda p: tt(Z, Z, p, ALU.add))
                        dve.drain()
                        end = ends[:, :, ds(i * 2 + u, 1)].to_broadcast([P, KT, HD])
                        tt(Z, Z, end, ALU.mult).then_inc(state_ready, 1)


def rwkv_state_out(c):
    nc, io = c.nc, c.io
    Z = c.z_state[:, :].rearrange("p (k i) -> p k i", i=HD)
    rows = c.work[0:HD, 0:D]
    with c.stage("rwkv_state_out") as st:
        turned, moved, stored = st.sem("state_in_psum"), st.sem("state_moved"), st.sem("state_stored")
        block = st.block()

        @block.tensor
        def _(pe):
            for k in range(KT):
                last = nc.tensor.transpose(c.bank[k // 4][0:HD, P * (k % 4):P * (k % 4) + P], Z[:, k, :], c.ident)
            last.then_inc(turned, 1)

        @block.vector
        def _(dve):
            dve.wait_ge(turned, 1)
            for a in range(2):
                nc.vector.tensor_copy(rows[:, 512 * a:512 * a + 512], c.bank[a][0:HD, :]).then_inc(moved, 1)

        @block.sync
        def _(sp):
            sp.wait_ge(moved, 2)
            sp.dma_start(io["o_prompt_wkv"][0, 0].rearrange("h i j -> i h j"),
                         rows.rearrange("i (h j) -> i h j", j=HD)).then_inc(stored, 16)
            sp.wait_ge(stored, 16)


def rwkv_finish(c):
    nc = c.nc
    o, bonus, g, sq = c.slot(4), c.slot(3), c.slot(9), c.slot(1)
    rn = c.work[:, 0:NT]
    cols = ((0, 0, TP), (1, TP, NT))
    with c.stage("rwkv_finish") as st:
        mean, centred, var, used = (st.sem(n) for n in ("mean_in_psum", "squares_ready", "variance_in_psum",
                                                        "banks_used"))
        roots = st.sem("deviation_inverted")
        block = st.block()

        @block.scalar
        def _(act):
            for k in range(KT):
                act.wait_ge(used, 2 * k + 2)
                nc.scalar.activation(rn, rn, ACT.Sqrt).then_inc(roots, 1)

        @block.tensor
        def _(pe):
            for k in range(KT):
                if k >= 1:
                    pe.wait_ge(used, 2 * k)
                nc.tensor.matmul(c.bank[0][:, :], c.headones, o[:, k, 0:TP], start=True, stop=True)
                nc.tensor.matmul(c.bank[1][:, 0:NB], c.headones, o[:, k, TP:NT], start=True,
                                 stop=True).then_inc(mean, 1)
                pe.wait_ge(centred, k + 1)
                nc.tensor.matmul(c.bank[2][:, :], c.headones, sq[:, k, 0:TP], start=True, stop=True)
                nc.tensor.matmul(c.bank[3][:, 0:NB], c.headones, sq[:, k, TP:NT], start=True,
                                 stop=True).then_inc(var, 1)

        @block.vector
        def _(dve):
            for k in range(KT):
                dve.wait_ge(mean, k + 1)
                for b, lo, hi in cols:
                    nc.vector.scalar_tensor_tensor(sq[:, k, lo:hi], c.bank[b][:, 0:hi - lo], -1.0 / HD, o[:, k, lo:hi],
                                                   ALU.mult, ALU.add)
                dve.drain()
                nc.vector.tensor_copy(o[:, k, :], sq[:, k, :])
                dve.drain().then_inc(used, 1)
                nc.vector.tensor_tensor(sq[:, k, :], sq[:, k, :], o[:, k, :], ALU.mult).then_inc(centred, 1)
                dve.wait_ge(var, k + 1)
                for b, lo, hi in cols:
                    nc.vector.tensor_scalar(rn[:, lo:hi], c.bank[2 + b][:, 0:hi - lo], 1.0 / HD, GN_EPS,
                                            ALU.mult, ALU.add)
                dve.drain().then_inc(used, 1)
                dve.wait_ge(roots, k + 1)
                nc.vector.reciprocal(rn, rn)
                dve.drain()
                nc.vector.scalar_tensor_tensor(o[:, k, :], o[:, k, :], c.vec("lnw", k), rn, ALU.mult, ALU.mult)
                dve.drain()
                nc.vector.scalar_tensor_tensor(o[:, k, :], o[:, k, :], c.vec("lnb", k), bonus[:, k, :],
                                               ALU.add, ALU.add)
                dve.drain()
                nc.vector.tensor_tensor(o[:, k, :], o[:, k, :], g[:, k, :], ALU.mult)



def route(c, layer):
    nc, io = c.nc, c.io
    x = c.slot(1)
    NTILE, NL, NG, EG = TT + 1, 36, 4, 8
    wr = c.work[:, 0:KT * NL].rearrange("p (k n) -> p k n", n=NL)
    bias = c.work[0:1, 300:300 + NL]
    at = [400]

    def area(*shape):
        n = int(np.prod(shape))
        a = c.work[:, at[0]:at[0] + n]
        at[0] += n
        return a if len(shape) == 1 else a.rearrange("p (a b) -> p a b", b=shape[1])

    rank4, rank8 = area(NG), area(EG)
    L = area(NTILE, NL)
    gmax, gexp, gsum, gkey, gtop = area(NTILE, 1), area(NTILE, NG), area(NTILE, 1), area(NTILE, NG), area(NTILE, 1)
    ghot, picked, part = area(NTILE, NG), area(NTILE, EG), area(NTILE, EG)
    m1, m2, k1, h1, h2 = area(NTILE, 1), area(NTILE, 1), area(NTILE, EG), area(NTILE, EG), area(NTILE, EG)
    e2, w1 = area(NTILE, 1), area(NTILE, 1)
    comb = area(NTILE, E)
    combT = c.work[0:E, at[0]:at[0] + NT]
    wide = lambda a, n: a.to_broadcast([P, NTILE, n])
    with c.stage(f"route{layer}") as st:
        loaded, logits, differences, exps, ready = (st.sem(n) for n in (
            "router_loaded", "logits_in_psum", "differences_ready", "exponentials_ready", "weights_ready"))
        turned, moved, stored, clean = (st.sem(n) for n in ("weights_turned", "weights_moved", "weights_stored",
                                                            "logits_cleared"))
        block = st.block()

        @block.sync
        def _(sp):
            sp.dma_start(wr[:, :, 0:NG], io["moe_wrg"][layer].rearrange("(k p) n -> p k n", p=P)).then_inc(loaded, 16)
            sp.dma_start(wr[:, :, NG:NL], io["moe_wre"][layer].rearrange("(k p) n -> p k n", p=P)).then_inc(loaded, 16)
            sp.dma_start(bias[:, 0:NG], io["moe_brg"][layer:layer + 1, :]).then_inc(loaded, 16)
            sp.dma_start(bias[:, NG:NL], io["moe_bre"][layer:layer + 1, :]).then_inc(loaded, 16)
            for dst, name in ((rank4, "rank4"), (rank8, "rank8")):
                sp.dma_start(dst, io["consts"][:, CCOL[name][0]:CCOL[name][1]]).then_inc(loaded, 16)
            sp.wait_ge(moved, 1)
            sp.dma_start(c.comb, combT).then_inc(stored, 16)
            sp.wait_ge(stored, 16)

        @block.tensor
        def _(pe):
            pe.wait_ge(loaded, 96)
            for n in range(NTILE):
                m = P if n < TT else NB
                out = c.bank[0][0:m, NL * n:NL * n + NL]
                for k in range(KT):
                    nc.tensor.matmul(out, x[:, k, P * n:P * n + m], wr[:, k, :], start=(k == 0), stop=False)
                last = nc.tensor.matmul(out, c.ones[0:1, 0:m], bias, start=False, stop=True)
            last.then_inc(logits, 1)
            pe.wait_ge(ready, 1)
            for n in range(NTILE):
                m = P if n < TT else NB
                last = nc.tensor.transpose(c.bank[2 + n // 4][0:E, P * (n % 4):P * (n % 4) + m], comb[0:m, n, :],
                                           c.ident[0:m, 0:m])
            last.then_inc(turned, 1)

        @block.scalar
        def _(act):
            act.wait_ge(differences, 1)
            nc.scalar.activation(gexp, gkey, ACT.Exp).then_inc(exps, 1)
            act.wait_ge(differences, 2)
            nc.scalar.activation(e2, m2, ACT.Exp).then_inc(exps, 1)

        @block.vector
        def _(dve):
            tt, ts = nc.vector.tensor_tensor, nc.vector.tensor_scalar
            reduce = nc.vector.tensor_reduce
            nc.vector.memset(L, 0.0)
            dve.wait_ge(logits, 1)
            dve.drain()
            nc.vector.tensor_copy(L[:, 0:TT, :], c.bank[0][:, 0:TT * NL].rearrange("p (a b) -> p a b", b=NL))
            nc.vector.tensor_copy(L[0:NB, TT, :], c.bank[0][0:NB, TT * NL:NTILE * NL])
            dve.drain()
            lg = L[:, :, 0:NG]
            reduce(gmax, lg, AX.X, ALU.max)
            dve.drain()
            tt(gkey, lg, wide(gmax, NG), ALU.subtract)
            dve.drain().then_inc(differences, 1)
            dve.wait_ge(exps, 1)
            reduce(gsum, gexp, AX.X, ALU.add)

            def first_of(hot, values, top, rank, n, key):
                tt(key, values, wide(top, n), ALU.is_equal)
                dve.drain()
                tt(key, key, rank.unsqueeze(1).to_broadcast([P, NTILE, n]), ALU.mult)
                dve.drain()
                reduce(gtop, key, AX.X, ALU.max)
                dve.drain()
                tt(hot, key, wide(gtop, n), ALU.is_equal)
                dve.drain()

            first_of(ghot, lg, gmax, rank4, NG, gkey)
            for g in range(NG):
                dst = picked if g == 0 else part
                tt(dst, L[:, :, NG + EG * g:NG + EG * g + EG], wide(ghot[:, :, g:g + 1], EG), ALU.mult)
                dve.drain()
                if g:
                    tt(picked, picked, part, ALU.add)
                    dve.drain()
            reduce(m1, picked, AX.X, ALU.max)
            dve.drain()
            first_of(h1, picked, m1, rank8, EG, k1)
            nc.vector.scalar_tensor_tensor(part, h1, NEG, picked, ALU.mult, ALU.add)
            dve.drain()
            reduce(m2, part, AX.X, ALU.max)
            dve.drain()
            first_of(h2, part, m2, rank8, EG, k1)
            tt(m2, m2, m1, ALU.subtract)
            dve.drain().then_inc(differences, 1)
            dve.wait_ge(exps, 2)
            ts(w1, e2, 1.0, None, ALU.add)
            dve.drain()
            tt(w1, w1, gsum, ALU.mult)
            dve.drain()
            nc.vector.reciprocal(w1, w1)
            dve.drain()
            tt(e2, e2, w1, ALU.mult)
            dve.drain()
            tt(h1, h1, wide(w1, EG), ALU.mult)
            tt(h2, h2, wide(e2, EG), ALU.mult)
            dve.drain()
            tt(h1, h1, h2, ALU.add)
            dve.drain()
            for g in range(NG):
                last = tt(comb[:, :, EG * g:EG * g + EG], h1, wide(ghot[:, :, g:g + 1], EG), ALU.mult)
            dve.drain().then_inc(ready, 1)
            dve.wait_ge(turned, 1)
            nc.vector.tensor_copy(combT[:, 0:TP], c.bank[2][0:E, :])
            nc.vector.tensor_copy(combT[:, TP:NT], c.bank[3][0:E, 0:NB])
            dve.drain().then_inc(moved, 1)


def experts(c, layer):
    nc, io = c.nc, c.io
    x, h = c.slot(1), c.slot(0)
    FT = FE // P
    area = [c.flat(4, 2)[:, 0:6144], c.flat(6, 2)[:, 0:6144]]
    wg, wu, wd = ([a[:, n * 2048:n * 2048 + 2048].rearrange("p (k n) -> p k n", n=(FE if n < 2 else D))
                   for a in area] for n in range(3))
    hid = [c.flat(8)[:, 2 * NT * u:2 * NT * (u + 1)].rearrange("p (f t) -> p f t", t=NT) for u in range(2)]
    act_out = [c.flat(9)[:, NT * f:NT * f + NT] for f in range(2)]
    cw = [c.flat(9)[:, NT * (2 + u):NT * (3 + u)] for u in range(2)]
    halves = lambda a: a.rearrange("p (s t) -> p s t", s=2)

    order = [(u, f"{n}{f}") for u in range(2) for f in range(FT) for n in "GU"]
    order += [(u, f"D{m}") for u in range(2) for m in range(KT)]
    place = {p: (x % 4, x // 4) for x, p in enumerate(order)}
    per_round = len(order) // 4
    src = {"g": io["moe_wgate"][layer].rearrange("g e d f -> (g e) d f"),
           "u": io["moe_wup"][layer].rearrange("g e d f -> (g e) d f"),
           "d": io["moe_wdown"][layer].rearrange("g e f d -> (g e) f d")}

    with c.stage(f"experts{layer}") as st:
        up_ready = [st.sem(f"gate_up_loaded{u}") for u in range(2)]
        down_ready = [st.sem(f"down_loaded{u}") for u in range(2)]
        comb_ready = [st.sem(f"weights_loaded{u}") for u in range(2)]
        full = [st.sem(f"product_in_pair{b}") for b in range(4)]
        taken = [st.sem(f"product_taken{b}", 1) for b in range(4)]
        hid_ready, silu_ready = st.sem("hidden_ready"), st.sem("silu_ready")
        rounds = [st.sem(f"expert_rounds{n}") for n in range(2)]
        block = st.block()

        def produced(eng, i, u, name):
            b, n = place[u, name]
            eng.wait_ge(full[b], i * per_round + (n + 1))

        def load(eng, dst, array, i, u, done):
            one = array[ds(i * 2 + u, 1), :, :].rearrange("a (k p) n -> p (a k) n", p=P)
            eng.dma_start(dst, one).then_inc(done, 16)

        @block.sync
        def _(sp):
            with sp.Fori(0, E // 2) as i:
                for u in range(2):
                    sp.wait_ge(rounds[0], i * 2 + (u + 1))
                    load(sp, wg[u], src["g"], i, u, up_ready[u])
                    load(sp, wu[u], src["u"], i, u, up_ready[u])
                for u in range(2):
                    sp.wait_ge(rounds[1], i * 2 + (u + 1))
                    load(sp, wd[u], src["d"], i, u, down_ready[u])
                    sp.dma_start(cw[u], c.comb[ds(i * 2 + u, 1), :].to_broadcast([P, NT])).then_inc(comb_ready[u], 16)

        @block.tensor
        def _(pe):
            def product(i, u, name, steps):
                b, n = place[u, name]
                pe.wait_ge(taken[b], i * per_round + (n + 1))
                for k, (w, a) in enumerate(steps):
                    for s in range(2):
                        last = nc.tensor.matmul(c.pair[b][:, s, :], w, a[:, HALF * s:HALF * s + HALF],
                                                start=(k == 0), stop=(k == len(steps) - 1))
                last.then_inc(full[b], 1)

            for r in rounds:
                pe.sem_inc(r, 2)
            with pe.Fori(0, E // 2) as i:
                for u in range(2):
                    pe.wait_ge(up_ready[u], i * 32 + 32)
                    for f in range(FT):
                        for name, w in (("G", wg), ("U", wu)):
                            product(i, u, f"{name}{f}", [(w[u][:, k, P * f:P * f + P], x[:, k, :]) for k in range(KT)])
                    pe.drain().then_inc(rounds[0], 1)
                for u in range(2):
                    pe.wait_ge(down_ready[u], i * 16 + 16)
                    pe.wait_ge(hid_ready, i * 4 + (2 * u + 4))
                    for m in range(KT):
                        product(i, u, f"D{m}", [(wd[u][:, f, P * m:P * m + P], hid[u][:, f, :]) for f in range(FT)])
                    pe.drain().then_inc(rounds[1], 1)

        @block.scalar
        def _(act):
            with act.Fori(0, E // 2) as i:
                for u in range(2):
                    for f in range(FT):
                        b, _ = place[u, f"G{f}"]
                        produced(act, i, u, f"G{f}")
                        act.wait_ge(hid_ready, i * 4 + (2 * u + f + 1))
                        nc.scalar.activation(halves(act_out[f]), c.pair[b], ACT.Silu).then_inc(taken[b], 1)

        @block.vector
        def _(dve):
            dve.sem_inc(hid_ready, 2)
            with dve.Fori(0, E // 2) as i:
                for u in range(2):
                    dve.wait_ge(comb_ready[u], i * 16 + 16)
                    for f in range(FT):
                        g, n = place[u, f"G{f}"]
                        dve.wait_ge(taken[g], i * per_round + (n + 2))
                        b, _ = place[u, f"U{f}"]
                        produced(dve, i, u, f"U{f}")
                        nc.vector.tensor_tensor(halves(act_out[f]), halves(act_out[f]), c.pair[b], ALU.mult)
                        dve.drain().then_inc(taken[b], 1)
                        nc.vector.tensor_tensor(hid[u][:, f, :], act_out[f], cw[u], ALU.mult).then_inc(hid_ready, 1)
                for u in range(2):
                    for m in range(KT):
                        b, _ = place[u, f"D{m}"]
                        produced(dve, i, u, f"D{m}")
                        nc.vector.tensor_tensor(halves(h[:, m, :]), halves(h[:, m, :]), c.pair[b],
                                                ALU.add).then_inc(taken[b], 1)


def mixture(c, layer):
    rms_norm(c, c.slot(0), f"ffn{layer}", c.slot(1), c.slot(3))
    route(c, layer)
    experts(c, layer)



NSTR = 6
KVW = NSTR * KVH * HD
KVT = KVW // P
RW = KVH * HD


def rotate(c, name, src, dst, tiles):
    nc, io = c.nc, c.io
    cos, sin = c.work[:, 0:NT], c.work[:, NT:2 * NT]
    swap = c.work[:, 2 * NT:2 * NT + P]
    parts = [c.work[:, 1200 + NT * n:1200 + NT * (n + 1)] for n in range(2)]
    halves = lambda a: a.rearrange("p (s t) -> p s t", s=2)
    with c.stage(name) as st:
        loaded, full, taken = st.sem("tables_loaded"), st.sem("partners_in_psum"), st.sem("partners_taken")
        block = st.block()

        @block.sync
        def _(sp):
            for dst_, n in ((cos, "cos"), (sin, "sin"), (swap, "swap")):
                sp.dma_start(dst_, io["consts"][:, CCOL[n][0]:CCOL[n][1]]).then_inc(loaded, 16)

        @block.tensor
        def _(pe):
            pe.wait_ge(loaded, 48)
            for x, m in enumerate(tiles):
                if x >= 4:
                    pe.wait_ge(taken, x - 3)
                for s in range(2):
                    last = nc.tensor.matmul(c.pair[x % 4][:, s, :], swap, src[:, m, HALF * s:HALF * s + HALF],
                                            start=True, stop=True)
                last.then_inc(full, 1)

        @block.vector
        def _(dve):
            dve.wait_ge(loaded, 48)
            for x, m in enumerate(tiles):
                dve.wait_ge(full, x + 1)
                part = parts[x % 2]
                nc.vector.tensor_tensor(halves(part), c.pair[x % 4], halves(sin), ALU.mult).then_inc(taken, 1)
                nc.vector.tensor_tensor(dst[:, m, :], src[:, m, :], cos, ALU.mult)
                dve.drain()
                nc.vector.tensor_tensor(dst[:, m, :], dst[:, m, :], part, ALU.add)


def kv_rows(c):
    nc, io = c.nc, c.io
    kv = c.flat(2, 2)[:, 0:KVT * NT].rearrange("p (k t) -> p k t", t=NT)
    rows = c.flat(4, 2)[:, 0:(TT + 1) * KVW].rearrange("p (n e) -> p n e", e=KVW)
    with c.stage("kv_rows") as st:
        turned, moved, stored = st.sem("rows_in_psum"), st.sem("rows_moved"), st.sem("rows_stored")
        block = st.block()
        jobs = [(n, a) for n in range(TT + 1) for a in range(3)]

        @block.tensor
        def _(pe):
            for x, (n, a) in enumerate(jobs):
                m = P if n < TT else NB
                if x >= 8:
                    pe.wait_ge(moved, x - 7)
                for k in range(4):
                    last = nc.tensor.transpose(c.bank[x % 8][0:m, P * k:P * k + P],
                                               kv[:, 4 * a + k, P * n:P * n + m], c.ident)
                last.then_inc(turned, 1)

        @block.vector
        def _(dve):
            nc.vector.tensor_copy(c.kv_sample, kv[:, :, TP:NT])
            for x, (n, a) in enumerate(jobs):
                m = P if n < TT else NB
                dve.wait_ge(turned, x + 1)
                nc.vector.tensor_copy(rows[0:m, n, 512 * a:512 * a + 512], c.bank[x % 8][0:m, :]).then_inc(moved, 1)

        @block.sync
        def _(sp):
            stores = 0
            sp.dma_start(io["o_sample_win"][:, 0:WIN - 1].rearrange("b t s g d -> b (t s g d)"),
                         io["cache_win"][:, 1:WIN].rearrange("b t s g d -> b (t s g d)")).then_inc(stored, 16)
            stores += 1
            for n in range(TT):
                sp.wait_ge(moved, 3 * (n + 1))
                sp.dma_start(io["o_prompt_rows"][0, P * n:P * n + P].rearrange("t s g d -> t (s g d)"),
                             rows[:, n, 0:4 * RW]).then_inc(stored, 16)
                sp.dma_start(io["o_prompt_win"][0, P * n:P * n + P].rearrange("t s g d -> t (s g d)"),
                             rows[:, n, 4 * RW:KVW]).then_inc(stored, 16)
                stores += 2
            sp.wait_ge(moved, len(jobs))
            sp.dma_start(io["o_sample_rows"][:, 0].rearrange("b s g d -> b (s g d)"),
                         rows[0:NB, TT, 0:4 * RW]).then_inc(stored, 16)
            sp.dma_start(io["o_sample_win"][:, WIN - 1].rearrange("b s g d -> b (s g d)"),
                         rows[0:NB, TT, 4 * RW:KVW]).then_inc(stored, 16)
            for a, stream in ((0, 2), (1, 4)):
                for q in range(2):
                    sp.dma_start(c.prompt_keys[0:HD, a, q:KVH:2, :],
                                 kv[HD * q:HD * q + HD, 2 * stream:2 * stream + 2, 0:TP]).then_inc(stored, 16)
            sp.wait_ge(stored, 16 * (stores + 2 + 4))


def load_compression(c, st, sp, w1, w2, pe_rows, b1, done):
    io = c.io
    for kv in range(2):
        sp.dma_start(w1[:, kv], io["cmp_w1"][kv].rearrange("(j p) n -> p j n", p=P)).then_inc(done, 16)
        sp.dma_start(w2[:, kv, :], io["cmp_w2"][kv]).then_inc(done, 16)
        sp.dma_start(pe_rows[:, kv, :], io["cmp_pe"][kv].rearrange("(j a) d -> j (a d)", a=2)).then_inc(done, 16)
        sp.dma_start(b1[:, kv:kv + 1], io["cmp_b1"][kv].rearrange("(c a) -> c a", a=1)).then_inc(done, 16)
    return 16 * 8


def by_parity(copy, dst, src, done):
    for q in range(2):
        for par in range(2):
            s = src[HD * q:HD * q + HD].rearrange("p v (n j a) -> p v j n a", j=8, a=2)[:, :, :, :, par]
            copy(dst[HD * par:HD * par + HD, q:2 * KVH:2, :, :], s).then_inc(done, 1)


def compress_prompt(c):
    nc, io = c.nc, c.io
    w1 = c.flat(6)[:, 0:4096].rearrange("p (a j n) -> p a j n", a=2, j=16)
    w2 = c.work[:, 0:2 * HD].rearrange("p (a d) -> p a d", a=2)
    pe_rows = c.work[0:16, 128:384].rearrange("p (a d) -> p a d", a=2)
    b1, pe_cols = c.work[:, 384:386], c.work[:, 386:418].rearrange("p (a j) -> p a j", a=2)
    kv_t = c.flat(2, 2)[:, 0:KVT * NT].rearrange("p (k t) -> p k t", t=NT)
    NS = TP // SUB
    XT = c.work[:, 2560:2560 + 2048].rearrange("p (v x n) -> p v x n", v=2 * KVH, x=8)
    XV = [c.work[:, 2560 + 1024 * v:2560 + 1024 * (v + 1)].rearrange("p (g j n) -> p g j n", g=KVH, j=8)
          for v in range(2)]
    G = [c.work[:, 4608 + 128 * v:4608 + 128 * v + KVH * NCMP_P].rearrange("p (g n) -> p g n", g=KVH)
         for v in range(2)]
    with c.stage("compress_prompt") as st:
        loaded, pe_in, pe_out, bias_in, bias_out = (st.sem(n) for n in (
            "weights_loaded", "encoding_turned", "encoding_moved", "bias_in_psum", "bias_ready"))
        moved, hid_in, hid_out, out_in = (st.sem(n) for n in (
            "pairs_moved", "hidden_in_psum", "hidden_ready", "outputs_in_psum"))
        block = st.block()

        @block.sync
        def _(sp):
            load_compression(c, st, sp, w1, w2, pe_rows, b1, loaded)

        @block.tensor
        def _(pe):
            pe.wait_ge(loaded, 16 * 8)
            for v in range(2):
                last = nc.tensor.transpose(c.bank[0][:, 16 * v:16 * v + 16], pe_rows[:, v, :], c.ident[0:16, 0:16])
            last.then_inc(pe_in, 1)
            pe.wait_ge(pe_out, 1)
            for v in range(2):
                for j in range(16):
                    last = nc.tensor.matmul(c.bank[5][:, v:v + 1], w1[:, v, j, :], pe_cols[:, v, j:j + 1],
                                            start=(j == 0), stop=(j == 15))
            last.then_inc(bias_in, 1)
            pe.wait_ge(moved, 4)
            for v in range(2):
                for j in range(16):
                    first = j // 8
                    last = nc.tensor.matmul(c.bank[6 + v][:, 0:KVH * NCMP_P], w1[:, v, j, :],
                                            XV[v][:, :, j % 8, first:first + NCMP_P], start=(j == 0), stop=(j == 15))
            last.then_inc(hid_in, 1)
            pe.wait_ge(hid_out, 2)
            nc.tensor.matmul(c.bank[0][0:HD, 0:KVH * NCMP_P], w2[:, 0, :], G[0], start=True, stop=True)
            for g in range(KVH):
                last = nc.tensor.matmul(c.bank[1][0:NCMP_P, HD * g:HD * g + HD], G[1][:, g, :], w2[:, 1, :],
                                        start=True, stop=True)
            last.then_inc(out_in, 1)

        @block.vector
        def _(dve):
            nc.vector.memset(c.cmp_keys, 0.0)
            nc.vector.memset(c.cmp_values, 0.0)
            dve.drain()
            dve.wait_ge(pe_in, 1)
            nc.vector.tensor_copy(pe_cols, c.bank[0][:, 0:32].rearrange("p (a j) -> p a j", a=2)).then_inc(pe_out, 1)
            by_parity(nc.vector.tensor_copy, XT, kv_t[:, 0:4, 0:TP], moved)
            dve.wait_ge(bias_in, 1)
            nc.vector.tensor_tensor(c.cmp_bias, c.bank[5][:, 0:2], b1, ALU.add).then_inc(bias_out, 1)
            dve.wait_ge(out_in, 1)
            nc.vector.tensor_copy(c.cmp_keys[0:HD], c.bank[0][0:HD, 0:KVH * NCMP_P].rearrange("p (g n) -> p g n", g=KVH))
            nc.vector.tensor_copy(c.cmp_values[0:NCMP_P, :], c.bank[1][0:NCMP_P, 0:RW])

        @block.scalar
        def _(act):
            act.wait_ge(hid_in, 1)
            act.wait_ge(bias_out, 1)
            for v in range(2):
                nc.scalar.activation(G[v], c.bank[6 + v][:, 0:KVH * NCMP_P].rearrange("p (g n) -> p g n", g=KVH),
                                     ACT.Gelu_apprx_tanh, bias=c.cmp_bias[:, v:v + 1]).then_inc(hid_out, 1)



def gates(c):
    nc, io = c.nc, c.io
    x, NGATE = c.slot(1), 3 * NH
    w = c.work[:, 0:KT * NGATE].rearrange("p (k n) -> p k n", n=NGATE)
    with c.stage("gates") as st:
        loaded, full, ready, stored = (st.sem(n) for n in ("weight_loaded", "gates_in_psum", "gates_ready", "stored"))
        cleared = st.sem("rows_cleared")
        block = st.block()

        @block.gpsimd
        def _(pool):
            nc.gpsimd.memset(c.gate, 0.0).then_inc(cleared, 1)

        @block.sync
        def _(sp):
            sp.dma_start(w, io["nsa_wqg"][0][:, D:D + NGATE].rearrange("(k p) n -> p k n", p=P)).then_inc(loaded, 16)
            sp.wait_ge(ready, 1)
            sp.dma_start(c.gate_rows, c.gate[0:NB, TT, :]).then_inc(stored, 16)
            sp.wait_ge(stored, 16)

        @block.tensor
        def _(pe):
            pe.wait_ge(loaded, 16)
            for n in range(TT + 1):
                m = P if n < TT else NB
                for k in range(KT):
                    last = nc.tensor.matmul(c.bank[0][0:m, NGATE * n:NGATE * n + NGATE], x[:, k, P * n:P * n + m],
                                            w[:, k, :], start=(k == 0), stop=(k == KT - 1))
            last.then_inc(full, 1)

        @block.scalar
        def _(act):
            act.wait_ge(cleared, 1)
            act.wait_ge(full, 1)
            nc.scalar.activation(c.gate[:, 0:TT, :], c.bank[0][:, 0:TT * NGATE].rearrange("p (a b) -> p a b", b=NGATE),
                                 ACT.Sigmoid)
            nc.scalar.activation(c.gate[0:NB, TT, :], c.bank[0][0:NB, TT * NGATE:(TT + 1) * NGATE], ACT.Sigmoid)
            act.drain().then_inc(ready, 1)


def prompt_attention(c):
    nc, io = c.nc, c.io
    q_plain, q_rot = c.slot(6), c.slot(7)
    rows = c.flat(4, 2)[:, 0:(TT + 1) * KVW].rearrange("p (n e) -> p n e", e=KVW)
    out = c.flat(1)[:, 0:TT * D].rearrange("p (n e) -> p n e", e=D)
    lo, hi = CCOL["cmpneg"][0], CCOL["cmpone"][1]
    NK = NCMP_P
    work, at = c.work, [0]

    def area(n):
        at[0] += n
        return work[:, at[0] - n:at[0]]

    masks, causal = area(hi - lo), area(P)
    neg, one = (masks[:, x * TT * NK:(x + 1) * TT * NK].rearrange("p (n k) -> p n k", k=NK) for x in range(2))
    queries = [area(4 * TP).rearrange("p (r t) -> p r t", t=TP)[0:HD] for _ in range(2)]
    prob = [area(TP) for _ in range(3)]
    turned_sb = [area(TP) for _ in range(3)]
    top, total, coef = area(64), area(64), area(64)
    CMP, SEL, WINB = range(3)
    jobs = [(r, b, n) for r in range(4) for n in range(TT) for b in (SEL, WINB, CMP)]
    NJ = len(jobs)
    width = lambda b, n: NK if b == CMP else P * (n + 1)
    STREAM = {SEL: 3, WINB: 5}
    with c.stage("prompt_attention") as st:
        loaded, q_ready = st.sem("tables_loaded"), st.sem("queries_ready")
        topped, score_free = st.sem("maximum_ready"), st.sem("scores_used")
        scored, expd, p_in, p_out, mixed, added = (st.sem(n, 1) for n in (
            "scores_in_psum", "probabilities_ready", "turned_in_psum", "turned_ready", "output_in_psum",
            "output_added"))
        block = st.block()
        S = [c.bank[x] for x in range(3)]
        Tb = [c.bank[3], c.bank[4]]
        O = [c.bank[5], c.bank[6]]

        @block.sync
        def _(sp):
            sp.dma_start(masks, io["consts"][:, lo:hi]).then_inc(loaded, 16)
            sp.dma_start(causal, io["consts"][:, CCOL["causal"][0]:CCOL["causal"][1]]).then_inc(loaded, 16)

        @block.gpsimd
        def _(pool):
            with pool.Fori(0, KVH) as i:
                pool.wait_ge(scored, i * NJ + 1)
                for dst, src in zip(queries, (q_plain, q_rot)):
                    for odd in range(2):
                        nc.gpsimd.tensor_copy(dst[:, odd:4:2, :],
                                              src[HD * odd:HD * odd + HD, ds(i * 2, 2), 0:TP]).then_inc(q_ready, 1)

        @block.tensor
        def _(pe):
            with pe.Fori(0, KVH) as i:
                pe.wait_ge(q_ready, i * 4 + 4)
                for x in range(NJ + 3):
                    if x < NJ:
                        r, b, n = jobs[x]
                        q = queries[0 if b == CMP else 1][:, r, P * n:P * n + P]
                        keys = (c.cmp_keys[0:HD, ds(i, 1), :] if b == CMP else
                                c.prompt_keys[0:HD, b - 1, ds(i, 1), 0:P * (n + 1)])
                        pe.wait_ge(expd, i * NJ + max(0, x - 2) + 1)
                        pe.nop(nofuse=True)
                        nc.tensor.matmul(S[x % 3][:, 0:width(b, n)], q, keys.rearrange("p a t -> p (a t)"),
                                         start=True, stop=True).then_inc(scored, 1)
                    if 2 <= x < NJ + 2:
                        y = x - 2
                        r, b, n = jobs[y]
                        pe.wait_ge(expd, i * NJ + y + 2)
                        pe.wait_ge(p_out, i * NJ + max(0, y - 1) + 1)
                        if b == CMP:
                            last = nc.tensor.transpose(Tb[y % 2][0:NK, 0:P], prob[y % 3][:, 0:NK], c.ident)
                        else:
                            for s in range(n + 1):
                                last = nc.tensor.transpose(Tb[y % 2][:, P * s:P * s + P],
                                                           prob[y % 3][:, P * s:P * s + P], c.ident)
                        last.then_inc(p_in, 1)
                    if x >= 3:
                        y = x - 3
                        r, b, n = jobs[y]
                        pe.wait_ge(p_out, i * NJ + y + 2)
                        pe.wait_ge(added, i * NJ + max(0, y - 1) + 1)
                        pe.nop(nofuse=True)
                        if b == CMP:
                            last = nc.tensor.matmul(O[y % 2][:, 0:HD], turned_sb[y % 3][0:NK, 0:P],
                                                    c.cmp_values[0:NK, ds(i * HD, HD)], start=True, stop=True)
                        else:
                            for s in range(n + 1):
                                v = rows[:, s, ds(i * HD + STREAM[b] * RW, HD)]
                                last = nc.tensor.matmul(O[y % 2][:, 0:HD], turned_sb[y % 3][:, P * s:P * s + P], v,
                                                        start=(s == 0), stop=(s == n))
                        last.then_inc(mixed, 1)

        @block.scalar
        def _(act):
            with act.Fori(0, KVH) as i:
                for x in range(NJ + 1):
                    if x < NJ:
                        r, b, n = jobs[x]
                        w = width(b, n)
                        act.wait_ge(topped, i * NJ + x + 1)
                        act.wait_ge(p_in, i * NJ + max(0, x - 2) + 1)
                        nc.scalar.activation(prob[x % 3][:, 0:w], S[x % 3][:, 0:w], ACT.Exp, bias=top[:, x:x + 1],
                                             scale=SCALE, accum_out=total[:, x:x + 1])
                        act.drain().then_inc(expd if b != CMP else score_free, 1)
                    if x >= 1:
                        y = x - 1
                        r, b, n = jobs[y]
                        rows_, w = (NK, P) if b == CMP else (P, P * (n + 1))
                        act.wait_ge(p_in, i * NJ + y + 2)
                        act.wait_ge(mixed, i * NJ + max(0, y - 2) + 1)
                        nc.scalar.copy(turned_sb[y % 3][0:rows_, 0:w], Tb[y % 2][0:rows_, 0:w]).then_inc(p_out, 1)

        @block.vector
        def _(dve):
            nc.vector.memset(out, 0.0)
            dve.wait_ge(loaded, 32)
            with dve.Fori(0, KVH) as i:
                ncmp = 0
                for x in range(NJ + 3):
                    if x < NJ:
                        r, b, n = jobs[x]
                        w = width(b, n)
                        dve.wait_ge(scored, i * NJ + x + 2)
                        part, mask = ((S[x % 3][:, 0:NK], neg[:, n, :]) if b == CMP
                                      else (S[x % 3][:, P * n:P * n + P], causal))
                        nc.vector.tensor_tensor(part, part, mask, ALU.add)
                        dve.drain()
                        nc.vector.tensor_reduce(top[:, x:x + 1], S[x % 3][:, 0:w], AX.X, ALU.max)
                        dve.drain()
                        nc.vector.tensor_scalar(top[:, x:x + 1], top[:, x:x + 1], -SCALE, None, ALU.mult)
                        dve.drain().then_inc(topped, 1)
                        if b == CMP:
                            ncmp += 1
                            dve.wait_ge(score_free, i * (NJ // 3) + ncmp)
                            nc.vector.tensor_tensor(prob[x % 3][:, 0:NK], prob[x % 3][:, 0:NK], one[:, n, :], ALU.mult)
                            dve.drain()
                            nc.vector.tensor_reduce(total[:, x:x + 1], prob[x % 3][:, 0:NK], AX.X, ALU.add)
                            dve.drain()
                            nc.vector.tensor_scalar(total[:, x:x + 1], total[:, x:x + 1], 1e-30, None, ALU.max)
                            dve.drain().then_inc(expd, 1)
                    if x >= 3:
                        y = x - 3
                        r, b, n = jobs[y]
                        cf = coef[:, y:y + 1]
                        nc.vector.reciprocal(cf, total[:, y:y + 1])
                        dve.drain()
                        nc.vector.tensor_tensor(cf, cf, c.gate[:, n, ds(i * 12 + (3 * r + b), 1)], ALU.mult)
                        dve.drain()
                        dve.wait_ge(mixed, i * NJ + y + 2)
                        o = out[:, n, ds(i * (4 * HD) + r * HD, HD)]
                        nc.vector.scalar_tensor_tensor(o, O[y % 2][:, 0:HD], cf, o, ALU.mult, ALU.add)
                        dve.drain().then_inc(added, 1)

    with c.stage("prompt_mixed") as st:
        turned, moved = st.sem("columns_in_psum"), st.sem("columns_moved")
        block = st.block()

        @block.tensor
        def _(pe):
            for k in range(KT):
                for n in range(TT):
                    last = nc.tensor.transpose(c.bank[k][:, P * n:P * n + P], out[:, n, P * k:P * k + P], c.ident)
                last.then_inc(turned, 1)

        @block.vector
        def _(dve):
            for k in range(KT):
                dve.wait_ge(turned, k + 1)
                nc.vector.tensor_copy(c.slot(9)[:, k, 0:TP], c.bank[k])


def sample_prepare(c):
    nc, io = c.nc, c.io
    rows = c.slot(1)[0:NB, :, :].rearrange("b k t -> b (k t)")[:, 0:2 * D].rearrange("b (a e) -> b a e", a=2)
    s = c.sample
    pages_i = c.flat(8)[:, 0:NB * NPG].bitcast(I32)
    pages_f = c.flat(8)[:, 128:128 + NB * NPG]
    tok = c.flat(8)[:, 256:257]
    with c.stage("sample_prepare") as st:
        loaded, turned, moved, stored = (st.sem(n) for n in ("loaded", "queries_turned", "queries_moved", "stored"))
        weights = st.sem("weights_loaded")
        block = st.block()

        @block.sync
        def _(sp):
            table = io["page_table"].rearrange("(a b) p -> a (b p)", a=1).to_broadcast([P, NB * NPG])
            sp.dma_start(pages_i, table).then_inc(loaded, 16)
            sp.dma_start(tok, io["consts"][:, CCOL["tokrow"][0]:CCOL["tokrow"][1]], allow_slow_non_contiguous=True).then_inc(loaded, 16)
            sp.wait_ge(turned, 1)
            n = load_compression(c, st, sp, s["w1"], s["w2"], c.flat(8)[0:16, 300:556].rearrange("p (a d) -> p a d", a=2),
                                 c.flat(8)[:, 556:558], weights)
            for name in ("overlap", "samegroup", "notforced", "forced", "earlier", "ownkv", "ownquery"):
                sp.dma_start(s[name], io["consts"][0:s[name].shape[0], CCOL[name][0]:CCOL[name][1]]).then_inc(weights, 16)
                n += 16
            sp.dma_start(s["gate"], c.gate_rows.rearrange("b (h r) -> h b r", r=3)).then_inc(weights, 16)
            sp.wait_ge(weights, n + 16)
            sp.wait_ge(moved, 4)
            sp.dma_start(c.query_rows.rearrange("a b e -> b a e"), rows).then_inc(stored, 16)
            sp.wait_ge(stored, 16)

        @block.tensor
        def _(pe):
            for a in range(2):
                for k in range(KT):
                    last = nc.tensor.transpose(c.bank[2 * a + k // 4][0:NB, P * (k % 4):P * (k % 4) + P],
                                               c.slot(6 + a)[:, k, TP:NT], c.ident)
            last.then_inc(turned, 1)

        @block.vector
        def _(dve):
            dve.wait_ge(loaded, 32)
            nc.vector.tensor_copy(pages_f, pages_i)
            dve.drain()
            nc.vector.tensor_scalar(pages_f, pages_f, float(2 * PAGE), tok, ALU.mult, ALU.add)
            dve.drain()
            nc.vector.tensor_copy(s["index"][:, 1, :], pages_f)
            nc.vector.tensor_scalar(pages_f, pages_f, -1.0, None, ALU.add)
            dve.drain()
            nc.vector.tensor_copy(s["index"][:, 0, :], pages_f)
            dve.wait_ge(turned, 1)
            for a in range(2):
                for k in range(2):
                    nc.vector.tensor_copy(rows[:, a, 512 * k:512 * k + 512], c.bank[2 * a + k][0:NB, :]).then_inc(moved, 1)


def sample_memory(c):
    f, w, at = c.flat, c.work, [0]

    def area(n, rows=P):
        at[0] += n
        assert at[0] <= 8320
        return w[0:rows, at[0] - n:at[0]]

    NSC = NCMP_S + PAST + 1 + WIN
    c.sample = {
        "sel": f(1, 2)[:, 0:NPG * 512].rearrange("p (n e) -> p n e", e=512),
        "xt": f(3, 2)[:, 0:8192].rearrange("p (v j n) -> p v j n", v=2 * KVH, j=8),
        "kt": f(5)[:, 0:2 * PAST].rearrange("p (g t) -> p g t", g=2),
        "w1": f(6)[:, 0:4096].rearrange("p (a j n) -> p a j n", a=2, j=16),
        "cmp": f(7)[:, 0:2048].rearrange("p (n e) -> p n e", e=512),
        "win": f(7)[:, 2048:4096].rearrange("p (n e) -> p n e", e=512),
        "kwt": f(8)[:, 0:1024].rearrange("p (g t) -> p g t", g=2),
        "score": f(8)[0:NH, 1024:1024 + NSC],
        "w2": area(2 * HD).rearrange("p (a d) -> p a d", a=2),
        "index": area(2 * NB * NPG).rearrange("p (a n) -> p a n", a=2).bitcast(U32),
        "now": area(2 * NPG).rearrange("p (a n) -> p a n", a=2).bitcast(U32),
        "hidden": area(2 * KVH * NCMP_S).rearrange("p (a g n) -> p a g n", a=2, g=KVH),
        "kc": area(2 * NCMP_S).rearrange("p (g n) -> p g n", g=2),
        "vc": area(RW, NCMP_S),
        "overlap": area(NSB, NCMP_S), "samegroup": area(NH, NH), "notforced": area(NSB, NH), "forced": area(NSB, NH),
        "earlier": area(NSB * NSB, NH), "ownkv": area(RW, NH), "ownquery": area(2 * NH),
        "gate": area(3 * NB, NH).rearrange("p (b r) -> p b r", r=3),
        "qrow": area(4 * HD, NH).rearrange("p (a x d) -> p a x d", a=2, x=2),
        "vnew": area(RW, 1),
        "rank": area(NSB * NSB, NH), "tie": area(NSB * NSB, NH),
        "imp": area(NSB, NH), "pick": area(NSB, NH),
        "pct": area(NH, NCMP_S), "pt": area((NPG + 1) * NH), "wt": area(4 * NH),
        "acc": area(RW, NH), "head": area(HD, NH), "col": area(16, NH),
    }


def sample_attention(c):
    nc, io = c.nc, c.io
    s = c.sample
    cache = io["cache_kv"].rearrange("n t (a s) g d -> (n t a) (s g d)", a=2)
    sc_cmp, sc_sel = s["score"][:, 0:NCMP_S], s["score"][:, NCMP_S:NCMP_S + PAST + 1]
    sc_win = s["score"][:, NCMP_S + PAST + 1:]
    col = lambda n: s["col"][:, n:n + 1]
    out_rows = nc.dram_tensor("sample_attended", [NB, D], F32).ap()
    CAP = 4
    RING = NPG + NPG // 2 + 2
    with c.stage("sample_attention") as st:
        cmp_in = [st.sem(f"cmp_page_loaded{n}") for n in range(CAP)]
        sel_in = [st.sem(f"sel_pages_loaded{n}") for n in range(4)]
        win_in, row_in, stored = st.sem("window_loaded"), st.sem("query_rows_loaded"), st.sem("head_rows_stored", 16)
        turned = [st.sem(f"tile_turned{n}", 1) for n in range(2)]
        taken = [st.sem(f"tile_taken{n}", 1) for n in range(2)]
        ev = {n: st.sem(n, 1) for n in (
            "hidden_in_psum", "hidden_ready", "compressed_in_psum", "compressed_ready",
            "queries_in_psum", "queries_ready", "small_scores_in_psum", "small_scores_ready", "sel_scores_in_psum",
            "maxima_ready", "exp_ready", "cmp_prob_ready", "cmp_turned_in_psum", "cmp_turned_ready",
            "importance_in_psum", "importance_ready", "group_importance_in_psum", "sel_maximum_ready",
            "sel_exp_ready", "turned_in_psum", "turned_ready", "output_in_psum", "head_ready")}
        block = st.block()

        def now(eng, i, *names):
            for n in names:
                eng.wait_ge(ev[n], i + 2)

        def before(eng, i, *names):
            for n in names:
                eng.wait_ge(ev[n], i + 1)

        @block.gpsimd
        def _(pool):
            def gather(dst, a, p, done):
                pool.nop(nofuse=True)
                nc.gpsimd.indirect_dma_start(
                    out=dst, out_offset=None, in_=cache,
                    in_offset=bass.IndirectOffsetOnAxis(ap=s["now"][:, a, p:p + 1], axis=0),
                    bounds_check=NPHYS * PAGE * 2 - 1, oob_is_err=True).then_inc(done, 16)

            with pool.Fori(0, NB) as i:
                before(pool, i, "sel_scores_in_psum")
                nc.gpsimd.tensor_copy(s["now"], s["index"][:, :, ds(i * NPG, NPG)])
                pool.drain()
                for p in range(NPG):
                    if p >= CAP:
                        pool.wait_ge(turned[p % 2], i * (RING // 2) + (p - CAP) // 2 + 2)
                    else:
                        pool.wait_ge(turned[p % 2], i * (RING // 2) + 1)
                    gather(s["cmp"][:, p % CAP, :], 0, p, cmp_in[p % CAP])
                    if p == 0:
                        before(pool, i, "output_in_psum")
                    gather(s["sel"][:, p, :], 1, p, sel_in[p // 4])

        @block.sync
        def _(sp):
            with sp.Fori(0, NB) as i:
                before(sp, i, "output_in_psum")
                window = io["o_sample_win"][ds(i, 1)].rearrange("b (n p) s g d -> p (b n) (s g d)", p=P)
                sp.dma_start(s["win"], window).then_inc(win_in, 16)
                sp.dma_start(s["vnew"], io["o_sample_rows"][ds(i, 1), 0, 3].rearrange("b g d -> b (g d)")).then_inc(win_in, 16)
                for x in range(2):
                    q = c.query_rows[:, ds(i, 1), :].rearrange("a b (h d) -> h (a b) d", d=HD)
                    sp.dma_start(s["qrow"][:, :, x, :], q).then_inc(row_in, 16)
                now(sp, i, "head_ready")
                sp.dma_start(out_rows[ds(i, 1), :].rearrange("b (h d) -> (b h) d", d=HD), s["head"]).then_inc(stored, 16)
            sp.wait_ge(stored, 16 * NB + 16)

        @block.tensor
        def _(pe):
            mm, tr = nc.tensor.matmul, nc.tensor.transpose

            def tile(i, x, sources):
                pe.wait_ge(taken[x % 2], i * (RING // 2) + x // 2 + 1)
                for at, src in sources:
                    last = tr(c.bank[x % 2][:, at:at + P], src, c.ident)
                last.then_inc(turned[x % 2], 1)

            with pe.Fori(0, NB) as i:
                for p in range(NPG):
                    pe.wait_ge(cmp_in[p % CAP], i * (16 * NPG // CAP) + 16 * (p // CAP + 1))
                    tile(i, p, [(P * v, s["cmp"][:, p % CAP, P * v:P * v + P]) for v in range(4)])
                for n in range(2):
                    pe.wait_ge(taken[n], i * (RING // 2) + NPG // 2 + 1)
                for v in range(2):
                    for j in range(16):
                        first = j // 8
                        last = mm(c.bank[2 + v][:, 0:KVH * NCMP_S], s["w1"][:, v, j, :],
                                  s["xt"][:, KVH * v:KVH * v + KVH, j % 8, first:first + NCMP_S],
                                  start=(j == 0), stop=(j == 15))
                last.then_inc(ev["hidden_in_psum"], 1)
                pe.wait_ge(row_in, i * 32 + 32)
                pe.nop(nofuse=True)
                for a in range(2):
                    last = tr(c.bank[4][:, NH * a:NH * a + NH], s["qrow"][:, a].rearrange("h x d -> h (x d)"),
                              c.ident[0:NH, 0:NH])
                last.then_inc(ev["queries_in_psum"], 1)
                for x in range(NPG // 2):
                    pe.wait_ge(sel_in[x // 2], i * (16 * NPG // 4) + 64)
                    tile(i, NPG + x, [(2 * P * g + P * y, s["sel"][:, 2 * x + y, P * g:P * g + P])
                                      for g in range(2) for y in range(2)])
                pe.wait_ge(win_in, i * 32 + 32)
                for g in range(2):
                    tile(i, NPG + NPG // 2 + g, [(P * y, s["win"][:, y, P * g:P * g + P]) for y in range(4)])
                now(pe, i, "hidden_ready")
                for q in range(2):
                    mm(c.bank[2][HD * q:HD * q + HD, 0:2 * NCMP_S], s["w2"][:, 0, :], s["hidden"][:, 0, q:KVH:2, :],
                       start=True, stop=True)
                for g in range(KVH):
                    last = mm(c.bank[3][0:NCMP_S, HD * g:HD * g + HD], s["hidden"][:, 1, g, :], s["w2"][:, 1, :],
                              start=True, stop=True)
                last.then_inc(ev["compressed_in_psum"], 1)
                for n in range(2):
                    pe.wait_ge(taken[n], i * (RING // 2) + RING // 2 + 1)
                now(pe, i, "compressed_ready", "queries_ready")
                Q = c.queries
                for g in range(2):
                    mm(c.bank[2][0:NH, 0:NCMP_S], Q[:, 0, g, :], s["kc"][:, g, :], start=(g == 0), stop=(g == 1))
                for g in range(2):
                    mm(c.bank[2][0:NH, 128:129], Q[:, 1, g, :], c.kv_sample[:, 4 + g, ds(i, 1)],
                       start=(g == 0), stop=(g == 1))
                for g in range(2):
                    last = mm(c.bank[3][0:NH, :], Q[:, 1, g, :], s["kwt"][:, g, :], start=(g == 0), stop=(g == 1))
                last.then_inc(ev["small_scores_in_psum"], 1)
                before(pe, i, "head_ready")
                for x in range(4):
                    for g in range(2):
                        last = mm(c.bank[4 + x][0:NH, :], Q[:, 1, g, :], s["kt"][:, g, 512 * x:512 * x + 512],
                                  start=(g == 0), stop=(g == 1))
                last.then_inc(ev["sel_scores_in_psum"], 1)
                now(pe, i, "cmp_prob_ready", "small_scores_ready")
                pe.nop(nofuse=True)
                tr(c.bank[2][0:NCMP_S, 0:NH], sc_cmp, c.ident[0:NH, 0:NH]).then_inc(ev["cmp_turned_in_psum"], 1)
                now(pe, i, "cmp_turned_ready")
                mm(c.bank[3][0:NH, 0:NSB], s["pct"], s["overlap"], start=True,
                   stop=True).then_inc(ev["importance_in_psum"], 1)
                now(pe, i, "importance_ready")
                pe.nop(nofuse=True)
                mm(c.bank[2][0:NH, 0:NSB], s["samegroup"], s["imp"], start=True,
                   stop=True).then_inc(ev["group_importance_in_psum"], 1)
                now(pe, i, "sel_exp_ready", "exp_ready")
                pe.nop(nofuse=True)
                for p in range(NPG):
                    tr(c.bank[4][:, NH * p:NH * p + NH], sc_sel[:, P * p:P * p + P], c.ident[0:NH, 0:NH])
                tr(c.bank[4][0:1, NH * NPG:NH * NPG + NH], sc_sel[:, PAST:PAST + 1], c.ident[0:NH, 0:NH])
                for y in range(4):
                    last = tr(c.bank[5][:, NH * y:NH * y + NH], sc_win[:, P * y:P * y + P], c.ident[0:NH, 0:NH])
                last.then_inc(ev["turned_in_psum"], 1)
                now(pe, i, "turned_ready")
                for p in range(NPG):
                    mm(c.bank[6][0:NH, 0:RW], s["pt"][:, NH * p:NH * p + NH], s["sel"][:, p, RW:2 * RW],
                       start=(p == 0), stop=False)
                mm(c.bank[6][0:NH, 0:RW], s["pt"][0:1, NH * NPG:NH * NPG + NH], s["vnew"], start=False, stop=True)
                for y in range(4):
                    mm(c.bank[6][0:NH, RW:2 * RW], s["wt"][:, NH * y:NH * y + NH], s["win"][:, y, RW:2 * RW],
                       start=(y == 0), stop=(y == 3))
                mm(c.bank[7][0:NH, 0:RW], s["pct"], s["vc"], start=True, stop=True).then_inc(ev["output_in_psum"], 1)

        def take_tile(eng, copy, i, x):
            b = x % 2
            eng.wait_ge(turned[b], i * (RING // 2) + x // 2 + 2)
            bank = c.bank[b]
            if x < NPG:
                src = bank.rearrange("p (v t) -> p v t", v=4)
                for q in range(2):
                    for par in range(2):
                        half = src[HD * q:HD * q + HD].rearrange("p v (n j a) -> p v j n a", j=8, a=2)[:, :, :, :, par]
                        last = copy(s["xt"][HD * par:HD * par + HD, q:2 * KVH:2, :, 8 * x:8 * x + 8], half)
            elif x < NPG + NPG // 2:
                y = x - NPG
                last = copy(s["kt"][:, :, 2 * P * y:2 * P * y + 2 * P], bank.rearrange("p (g t) -> p g t", g=2))
            else:
                last = copy(s["kwt"][:, x - NPG - NPG // 2, :], bank)
            eng.drain().then_inc(taken[b], 1)

        @block.scalar
        def _(act):
            with act.Fori(0, NB) as i:
                for x in range(1, NPG, 2):
                    take_tile(act, nc.scalar.copy, i, x)
                now(act, i, "hidden_in_psum")
                for v in range(2):
                    nc.scalar.activation(s["hidden"][:, v],
                                         c.bank[2 + v][:, 0:KVH * NCMP_S].rearrange("p (g n) -> p g n", g=KVH),
                                         ACT.Gelu_apprx_tanh, bias=c.cmp_bias[:, v:v + 1])
                act.drain().then_inc(ev["hidden_ready"], 1)
                for x in range(NPG + 1, RING, 2):
                    take_tile(act, nc.scalar.copy, i, x)
                now(act, i, "small_scores_in_psum")
                nc.scalar.copy(sc_cmp, c.bank[2][0:NH, 0:NCMP_S])
                nc.scalar.copy(sc_sel[:, PAST:PAST + 1], c.bank[2][0:NH, 128:129])
                nc.scalar.copy(sc_win, c.bank[3][0:NH, :])
                act.drain().then_inc(ev["small_scores_ready"], 1)
                now(act, i, "maxima_ready")
                nc.scalar.activation(sc_cmp, sc_cmp, ACT.Exp, bias=col(0), scale=SCALE, accum_out=col(1))
                nc.scalar.activation(sc_win, sc_win, ACT.Exp, bias=col(2), scale=SCALE, accum_out=col(3))
                act.drain().then_inc(ev["exp_ready"], 1)
                now(act, i, "sel_maximum_ready")
                nc.scalar.activation(sc_sel, sc_sel, ACT.Exp, bias=col(4), scale=SCALE, accum_out=col(5))
                act.drain().then_inc(ev["sel_exp_ready"], 1)

        @block.vector
        def _(dve):
            tt, ts, copy = nc.vector.tensor_tensor, nc.vector.tensor_scalar, nc.vector.tensor_copy
            reduce = nc.vector.tensor_reduce

            def scaled_maximum(dst, scores):
                reduce(dst, scores, AX.X, ALU.max)
                dve.drain()
                ts(dst, dst, -SCALE, None, ALU.mult)

            with dve.Fori(0, NB) as i:
                for x in range(0, NPG, 2):
                    take_tile(dve, copy, i, x)
                now(dve, i, "queries_in_psum")
                for a in range(2):
                    src = c.bank[4][:, NH * a:NH * a + NH].unsqueeze(1).to_broadcast([P, 2, NH])
                    tt(c.queries[:, a], src, s["ownquery"].rearrange("p (g h) -> p g h", g=2), ALU.mult)
                dve.drain().then_inc(ev["queries_ready"], 1)
                for x in range(NPG, RING, 2):
                    take_tile(dve, copy, i, x)
                now(dve, i, "compressed_in_psum")
                copy(s["kc"], c.bank[2][:, 0:2 * NCMP_S].rearrange("p (g n) -> p g n", g=2))
                copy(s["vc"], c.bank[3][0:NCMP_S, 0:RW])
                dve.drain().then_inc(ev["compressed_ready"], 1)
                now(dve, i, "small_scores_ready")
                scaled_maximum(col(0), sc_cmp)
                scaled_maximum(col(2), sc_win)
                dve.drain().then_inc(ev["maxima_ready"], 1)
                now(dve, i, "exp_ready")
                ts(col(1), col(1), 1e-30, None, ALU.max)
                dve.drain()
                nc.vector.reciprocal(col(1), col(1))
                nc.vector.reciprocal(col(3), col(3))
                dve.drain()
                ts(sc_cmp, sc_cmp, col(1), None, ALU.mult)
                dve.drain().then_inc(ev["cmp_prob_ready"], 1)
                now(dve, i, "cmp_turned_in_psum")
                copy(s["pct"], c.bank[2][0:NCMP_S, 0:NH]).then_inc(ev["cmp_turned_ready"], 1)
                now(dve, i, "importance_in_psum")
                copy(s["imp"], c.bank[3][0:NH, 0:NSB]).then_inc(ev["importance_ready"], 1)
                now(dve, i, "group_importance_in_psum")
                tt(s["pick"], c.bank[2][0:NH, 0:NSB], s["notforced"], ALU.mult)
                dve.drain()
                tt(s["pick"], s["pick"], s["forced"], ALU.add)
                dve.drain()
                theirs = s["pick"].unsqueeze(1).to_broadcast([NH, NSB, NSB])
                mine = s["pick"].unsqueeze(2).to_broadcast([NH, NSB, NSB])
                cube = lambda a: a.rearrange("p (i j) -> p i j", i=NSB)
                tt(cube(s["rank"]), theirs, mine, ALU.is_gt)
                tt(cube(s["tie"]), theirs, mine, ALU.is_equal)
                dve.drain()
                tt(s["tie"], s["tie"], s["earlier"], ALU.mult)
                dve.drain()
                tt(s["rank"], s["rank"], s["tie"], ALU.add)
                dve.drain()
                reduce(s["pick"], cube(s["rank"]), AX.X, ALU.add)
                dve.drain()
                ts(s["pick"], s["pick"], float(NSEL), NEG, ALU.is_ge, ALU.mult)
                dve.drain()
                now(dve, i, "sel_scores_in_psum")
                for x in range(4):
                    blocks = s["pick"][:, 8 * x:8 * x + 8].unsqueeze(2).to_broadcast([NH, 8, HD])
                    tt(sc_sel[:, 512 * x:512 * x + 512].rearrange("p (a t) -> p a t", t=HD),
                       c.bank[4 + x][0:NH, :].rearrange("p (a t) -> p a t", t=HD), blocks, ALU.add)
                tt(sc_sel[:, PAST:PAST + 1], sc_sel[:, PAST:PAST + 1], s["pick"][:, NSB - 1:NSB], ALU.add)
                dve.drain()
                scaled_maximum(col(4), sc_sel)
                dve.drain().then_inc(ev["sel_maximum_ready"], 1)
                now(dve, i, "turned_in_psum")
                copy(s["pt"][:, 0:NH * NPG], c.bank[4][:, 0:NH * NPG])
                copy(s["pt"][0:1, NH * NPG:], c.bank[4][0:1, NH * NPG:NH * NPG + NH])
                copy(s["wt"], c.bank[5][:, 0:4 * NH])
                nc.vector.reciprocal(col(5), col(5))
                dve.drain().then_inc(ev["turned_ready"], 1)
                g = s["gate"]
                tt(col(5), col(5), g[:, ds(i, 1), 1], ALU.mult)
                tt(col(3), col(3), g[:, ds(i, 1), 2], ALU.mult)
                copy(col(1), g[:, ds(i, 1), 0])
                dve.drain()
                now(dve, i, "output_in_psum")
                acc = s["acc"]
                ts(acc, c.bank[7][0:NH, 0:RW], col(1), None, ALU.mult)
                for cf, at in ((5, 0), (3, RW)):
                    dve.drain()
                    nc.vector.scalar_tensor_tensor(acc, c.bank[6][0:NH, at:at + RW], col(cf), acc, ALU.mult, ALU.add)
                dve.drain()
                tt(acc, acc, s["ownkv"], ALU.mult)
                dve.drain()
                dve.wait_ge(stored, i * 16 + 16)
                reduce(s["head"], acc.rearrange("p (g d) -> p d g", g=KVH), AX.X, ALU.add).then_inc(ev["head_ready"], 1)

    back = c.work[0:NB, 0:D]
    with c.stage("sample_mixed") as st:
        loaded, turned2 = st.sem("rows_loaded"), st.sem("columns_in_psum")
        block = st.block()

        @block.sync
        def _(sp):
            sp.dma_start(back, out_rows).then_inc(loaded, 16)

        @block.tensor
        def _(pe):
            pe.wait_ge(loaded, 16)
            for k in range(KT):
                last = nc.tensor.transpose(c.bank[0][:, NB * k:NB * k + NB], back[:, P * k:P * k + P],
                                           c.ident[0:NB, 0:NB])
            last.then_inc(turned2, 1)

        @block.vector
        def _(dve):
            dve.wait_ge(turned2, 1)
            nc.vector.tensor_copy(c.slot(9)[:, :, TP:NT], c.bank[0][:, 0:NB * KT].rearrange("p (k b) -> p k b", b=NB))


def hybrid_step(nc, io):
    c = Core(nc, io)
    load_parameters(c)
    load_tokens(c)
    rms_norm(c, c.slot(0), "mix0", c.slot(1), c.slot(3))
    transpose_out(c, "shift_out", c.slot(1), TP - 1, [(TP - 1, TP, io["o_prompt_shift"][0, :, :]),
                                                      (TP, NT, io["o_sample_shift"][0, :, :])])
    rwkv_inputs(c)
    rwkv_prepare(c)
    sample_state(c)
    rwkv_chunks(c)
    rwkv_state_out(c)
    rwkv_finish(c)
    project(c, "rw_wo", c.slot(4), KT, io["rw_wo"][0, :, :], KT, add_to(c, c.slot(0)), "dve")
    mixture(c, 0)

    kv = c.flat(2, 2)[:, 0:KVT * NT].rearrange("p (k t) -> p k t", t=NT)
    rms_norm(c, c.slot(0), "kv", c.slot(1), c.slot(4))
    project(c, "w_kv", c.slot(1), KT, io["w_kv"], KVT, copy_to(c, kv), "act")
    rotate(c, "rotate_keys", kv, kv, (4, 5, 8, 9))
    kv_rows(c)
    compress_prompt(c)

    rms_norm(c, c.slot(0), "mix1", c.slot(1), c.slot(2))
    project(c, "nsa_wq", c.slot(1), KT, io["nsa_wqg"][0][:, 0:D], KT, copy_to(c, c.slot(6)), "act")
    rotate(c, "rotate_queries", c.slot(6), c.slot(7), range(KT))
    gates(c)
    prompt_attention(c)

    sample_memory(c)
    sample_prepare(c)
    sample_attention(c)
    project(c, "nsa_wo", c.slot(9), KT, io["nsa_wo"][0], KT, add_to(c, c.slot(0)), "dve")
    mixture(c, 1)

    rms_norm(c, c.slot(0), "out", c.slot(1), c.slot(2))
    transpose_out(c, "outputs", c.slot(1), 0,
                  [(P * n, P * n + P, io["o_y_prompt"][0, P * n:P * n + P, :]) for n in range(TT)]
                  + [(TP, NT, io["o_y_sample"][:, 0, :])])


_INS = ["x_prompt", "x_sample", "state_wkv", "state_shift", "cache_kv", "cache_win", "page_table",
        "ln_mix", "ln_ffn", "ln_kv", "ln_out", "rw_mu", "rw_wr", "rw_wk", "rw_wv", "rw_wo", "rw_w0", "rw_w1", "rw_w2",
        "rw_a0", "rw_a1", "rw_a2", "rw_g1", "rw_g2", "rw_kk", "rw_ka", "rw_rk", "rw_lnw", "rw_lnb",
        "w_kv", "cmp_pe", "cmp_w1", "cmp_b1", "cmp_w2", "nsa_wqg", "nsa_wo",
        "moe_wrg", "moe_brg", "moe_wre", "moe_bre", "moe_wgate", "moe_wup", "moe_wdown"]
_OUTS = [("o_y_prompt", (1, TP, D)), ("o_y_sample", (NB, 1, D)), ("o_prompt_wkv", (1, 1, NH, HD, HD)),
         ("o_prompt_shift", (1, 1, D)), ("o_prompt_rows", (1, TP, 4, KVH, HD)), ("o_prompt_win", (1, WIN, 2, KVH, HD)),
         ("o_sample_wkv", (1, NB, NH, HD, HD)), ("o_sample_shift", (1, NB, D)),
         ("o_sample_rows", (NB, 1, 4, KVH, HD)), ("o_sample_win", (NB, WIN, 2, KVH, HD))]


def _lay_out(inputs):
    arrays = {name: np.ascontiguousarray(inputs[name]) for name in _INS}
    arrays["consts"] = CONSTS
    return arrays


def kernel(**inputs):
    import concourse.bacc as _bacc
    from concourse.bass_utils import run_bass_kernel_spmd as _run

    nc = _bacc.Bacc("TRN2", target_bir_lowering=False, num_devices=1)
    arrays, io = _lay_out(inputs), {}
    for name, a in arrays.items():
        io[name] = nc.dram_tensor(f"in_{name}", a.shape, mybir.dt.from_np(a.dtype), kind="ExternalInput").ap()
    for name, shape in _OUTS:
        io[name] = nc.dram_tensor(name, shape, F32, kind="ExternalOutput").ap()
    hybrid_step(nc, io)
    r = _run(nc, [{f"in_{name}": a for name, a in arrays.items()}], core_ids=[0])
    return tuple(r.results[0][name] for name, _ in _OUTS)
```

```python
from contextlib import ExitStack

import numpy as np
import concourse.bass as bass
from concourse import mybir

F32 = mybir.dt.float32
I32 = mybir.dt.int32
U32 = mybir.dt.uint32
ALU = mybir.AluOpType
ACT = mybir.ActivationFunctionType
AX = mybir.AxisListType
ds = bass.ds

P = 128
D = 1024
KT = D // P
TP = 512
NB = 8
NT = TP + NB
HALF = NT // 2
TT = TP // P
HD = 64
NH = 16
KVH = 4
CH = 64
NCH = TP // CH
PAST = 2048
PAGE = 128
NPG = PAST // PAGE
NPHYS = 160
WIN = 512
SUB = 16
NSUB = PAST // SUB
NCMP_S = NSUB - 1
NCMP_P = TP // SUB - 1
CH_HID = 128
NSB = PAST // HD + 1
NSEL = 16
E = 32
JOBS = E + 2 * NT // P
FE = 256
SCALE = HD ** -0.5
EPS = 1e-6
GN_EPS = 64e-5
NEG = -1.0e30

PVEC = ["mu0", "mu1", "mu2", "mu3", "mu4", "mu5", "mix0", "mix1", "ffn0", "ffn1", "kv", "out",
        "w0", "a0", "kk", "ka", "rk", "lnw", "lnb"]

def build_constants():
    cols, parts, at = {}, [], 0

    def put(name, a):
        nonlocal at
        a = np.asarray(a, np.float32)
        full = np.zeros((P, a.shape[1]), np.float32)
        full[:a.shape[0]] = a
        cols[name] = (at, at + a.shape[1])
        at += a.shape[1]
        parts.append(full)

    i, j = np.arange(P)[:, None], np.arange(P)[None, :]
    put("ident", i == j)
    put("ones", np.ones((P, P)))
    put("headones", (i // HD) == (j // HD))
    s, t = np.arange(P)[:, None] % HD, np.arange(HD)[None, :]
    put("ident64", s == t)
    put("before", s < t)
    put("upto", s <= t)
    for lvl in range(6):
        b = 1 << lvl
        put(f"join{lvl}", (s < t) & ((s ^ t) >= b) & ((s ^ t) < 2 * b))
    put("joinT0", ((t < s) & ((s ^ t) >= 1) & ((s ^ t) < 2)))
    put("keep", np.tile((np.arange(TP)[None, :] % CH != 0), (P, 1)))
    put("causal", np.where(j <= i, 0.0, NEG))
    half = 8
    inv = np.power(np.float32(500000.0), -np.arange(half, dtype=np.float32) * np.float32(2.0 / 16))
    pos = np.concatenate([np.arange(TP), np.full(NB, PAST)]).astype(np.float32)
    ang = pos[None, :] * inv[:, None].astype(np.float32)
    cs, sn = np.cos(ang), np.sin(ang)
    c64 = np.ones((HD, NT)); s64 = np.zeros((HD, NT))
    c64[:half] = cs; c64[half:16] = cs
    s64[:half] = -sn; s64[half:16] = sn
    put("cos", np.tile(c64, (2, 1)))
    put("sin", np.tile(s64, (2, 1)))
    perm = np.zeros((P, P))
    for q in range(2):
        for c in range(half):
            perm[q * HD + half + c, q * HD + c] = 1
            perm[q * HD + c, q * HD + half + c] = 1
    put("swap", perm)
    tok = np.arange(TP).reshape(TT, P).T[:, :, None]
    end = (np.arange(NCMP_P) * SUB + 31)[None, None, :]
    put("cmpneg", np.where(end <= tok, 0.0, NEG).reshape(P, -1))
    put("cmpone", (end <= tok).astype(np.float32).reshape(P, -1))
    st = np.arange(NCMP_S)[:, None] * SUB
    bl = np.arange(NSB)[None, :] * HD
    put("overlap", (st < bl + HD) & (st + 31 >= bl))
    hh = np.arange(NH)
    put("samegroup", (hh[:, None] // 4) == (hh[None, :] // 4))
    forced = np.zeros(NSB); forced[[0, NSB - 2, NSB - 1]] = 1
    put("notforced", np.tile(1 - forced, (NH, 1)))
    put("forced", np.tile(forced * 1.0e4, (NH, 1)))
    e = (np.arange(NSB)[None, :] < np.arange(NSB)[:, None]).astype(np.float32).reshape(1, -1)
    put("earlier", np.tile(e, (NH, 1)))
    own = (hh[:, None, None] // 4 == np.arange(KVH)[None, :, None]) * np.ones((1, 1, HD))
    put("ownkv", own.reshape(NH, -1))
    put("tokrow", np.arange(P)[:, None] * 2.0 + 1.0)
    oq = (hh[None, None, :] // 4 % 2 == (np.arange(P) // HD)[:, None, None]) & (hh[None, None, :] // 8 == np.arange(2)[None, :, None])
    put("ownquery", oq.reshape(P, -1))
    col = np.arange(TT + 1)[None, :] * P + np.arange(P)[:, None]
    put("valid", col < NT)
    put("token", col)
    put("triangle", i < j)
    put("jobid", np.tile(np.arange(JOBS + 1)[None, :], (P, 1)))
    put("rank4", np.tile(4.0 - np.arange(4)[None, :], (P, 1)))
    put("rank8", np.tile(8.0 - np.arange(8)[None, :], (P, 1)))
    return cols, np.concatenate(parts, 1)


CCOL, CONSTS = build_constants()
NCONST = CONSTS.shape[1]



class Core:

    def __init__(self, nc, io):
        self.nc, self.io = nc, io
        self.n, self.last_sems = 0, []
        self.lists = nc.dram_tensor("expert_lists", [(JOBS + 1) * P, 4], U32).ap()
        self.token_rows = nc.dram_tensor("expert_token_rows", [NT, D], F32).ap()
        self.expert_rows = nc.dram_tensor("expert_result_rows", [2 * NT, D], F32).ap()
        lists = nc.alloc_sbuf_tensor("job_lists", [P, (JOBS + 1) * 4], U32)
        self.job_lists = lists[:, :].rearrange("p (j w) -> p j w", w=4)
        self.job_expert = nc.alloc_sbuf_tensor("job_expert", [1, JOBS + 1], I32)[:, :]
        self.slots = nc.alloc_sbuf_tensor("slots", [P, 10 * KT * NT], F32)
        self.work = nc.alloc_sbuf_tensor("work", [P, 8320], F32)
        self.base = nc.alloc_sbuf_tensor("base_constants", [P, 384], F32)
        self.par = nc.alloc_sbuf_tensor("parameters", [P, 8 * len(PVEC)], F32)
        self.small = nc.alloc_sbuf_tensor("small", [P, 704], F32)
        self.z_state = nc.alloc_sbuf_tensor("z_state", [P, KT * HD], F32)
        psum = nc.alloc_psum_tensor("banks", [P, 8, 512], F32)
        self.bank = [psum[:, b, :] for b in range(8)]
        self.pair = [psum[:, 2 * b:2 * b + 2, 0:NT // 2] for b in range(4)]
        self.ident, self.ones, self.headones = (self.base[:, 128 * n:128 * n + 128] for n in range(3))

        keep = nc.alloc_sbuf_tensor("keep", [P, 840], F32)
        self.gate = keep[:, 0:240].rearrange("p (n g) -> p n g", n=TT + 1)
        self.kv_sample = keep[:, 240:336].rearrange("p (k b) -> p k b", b=NB)
        self.cmp_keys = keep[:, 336:336 + 4 * NCMP_P].rearrange("p (g n) -> p g n", g=KVH)
        self.cmp_values = keep[:, 464:464 + KVH * HD]
        self.cmp_bias = keep[:, 720:722]
        self.query_mask = keep[:, 724:756]
        self.queries = keep[:, 756:820].rearrange("p (a g h) -> p a g h", a=2, g=2)
        self.gate_rows = nc.dram_tensor("sample_gates", [NB, 3 * NH], F32).ap()
        self.query_rows = nc.dram_tensor("sample_queries", [2, NB, D], F32).ap()
        self.prompt_keys = self.slots[:, 8 * KT * NT:8 * KT * NT + 4096].rearrange("p (a g t) -> p a g t", a=2, g=KVH)

    def slot(self, n):
        return self.slots[:, n * KT * NT:(n + 1) * KT * NT].rearrange("p (k t) -> p k t", t=NT)

    def flat(self, n, count=1):
        return self.slots[:, n * KT * NT:(n + count) * KT * NT]

    def vec(self, name, k):
        c = 8 * PVEC.index(name) + k
        return self.par[:, c:c + 1]

    def stage(self, name):
        self.n += 1
        return Stage(self, f"{self.n}_{name}")


class Stage:

    def __init__(self, core, name):
        self.nc, self.core, self.name = core.nc, core, name

    def __enter__(self):
        self.ctx, self.sems, self.last, self.starts = ExitStack(), [], self.core.last_sems, []
        return self

    def sem(self, name, start=0):
        self.sems.append(self.nc.alloc_semaphore(f"{name}_{self.name}"))
        if start:
            self.starts.append((self.sems[-1], start))
        return self.sems[-1]

    def block(self):
        self.nc.clear_and_free_semaphores(self.last)
        for sem, start in self.starts:
            self.nc.gpsimd.sem_inc(sem, start)
        if self.starts:
            self.nc.all_engine_barrier()
        return self.ctx.enter_context(self.nc.Block())

    def __exit__(self, *a):
        self.ctx.close()
        self.core.last_sems = self.sems


def load_parameters(c):
    nc, io = c.nc, c.io
    nv = len(PVEC) * 8
    rows = c.work[:, 0:256]
    src = [io["rw_mu"][0, n, :] for n in range(6)] + [
        io["ln_mix"][0, :], io["ln_mix"][1, :], io["ln_ffn"][0, :], io["ln_ffn"][1, :], io["ln_kv"][:],
        io["ln_out"][:], io["rw_w0"][0, :], io["rw_a0"][0, :], io["rw_kk"][0, :], io["rw_ka"][0, :],
        io["rw_rk"][0, :, :].rearrange("h d -> (h d)"), io["rw_lnw"][0, :], io["rw_lnb"][0, :]]
    with c.stage("parameters") as st:
        loaded, cleared, turned = st.sem("vectors_loaded"), st.sem("rows_cleared"), st.sem("columns_in_psum")
        block = st.block()

        @block.sync
        def _(sp):
            sp.dma_start(c.base[:, :], io["consts"][:, 0:384]).then_inc(loaded, 16)
            sp.wait_ge(cleared, 1)
            for n, v in enumerate(src):
                r, half = (8 * n) % P, (8 * n) // P
                sp.dma_start(rows[r:r + 8, half * P:half * P + P],
                             v.rearrange("(k p) -> k p", p=P)).then_inc(loaded, 16)

        @block.vector
        def _(dve):
            nc.vector.memset(rows, 0.0).then_inc(cleared, 1)
            dve.wait_ge(turned, 1)
            nc.vector.tensor_copy(c.par[:, 0:nv], c.bank[0][:, 0:nv])

        @block.tensor
        def _(pe):
            pe.wait_ge(loaded, 16 * (len(src) + 1))
            nc.tensor.transpose(c.bank[0][:, 0:P], rows[:, 0:P], c.ident)
            nc.tensor.transpose(c.bank[0][:, P:2 * P], rows[:, P:2 * P], c.ident).then_inc(turned, 1)


def load_tokens(c):
    nc, io = c.nc, c.io
    h, prev = c.slot(0), c.slot(2)
    tiles = [(io["x_prompt"][0, P * n:P * n + P, :], h, P * n, P) for n in range(TT)]
    tiles += [(io["x_sample"][:, 0, :], h, TP, NB), (io["state_shift"][0, :, :], prev, TP, NB)]
    with c.stage("tokens") as st:
        loaded, turned, moved = st.sem("rows_loaded"), st.sem("tile_in_psum"), st.sem("tile_moved")
        block = st.block()
        rows = [c.work[:, D * n:D * n + D] for n in range(len(tiles))]

        @block.sync
        def _(sp):
            for n, (src, _, _, m) in enumerate(tiles):
                sp.dma_start(rows[n][0:m, :], src).then_inc(loaded, 16)

        @block.tensor
        def _(pe):
            pe.wait_ge(loaded, 16 * len(tiles))
            for n, (_, _, _, m) in enumerate(tiles):
                if n >= 2:
                    pe.wait_ge(moved, 2 * (n - 1))
                for k in range(KT):
                    out = c.bank[2 * (n % 2) + k // 4][:, P * (k % 4):P * (k % 4) + m]
                    last = nc.tensor.transpose(out, rows[n][0:m, P * k:P * k + P], c.ident[0:m, 0:m])
                last.then_inc(turned, 1)

        @block.vector
        def _(dve):
            for n, (_, dst, t0, m) in enumerate(tiles):
                dve.wait_ge(turned, n + 1)
                for a in range(2):
                    src = c.bank[2 * (n % 2) + a][:, :].rearrange("p (k t) -> p k t", t=P)
                    nc.vector.tensor_copy(dst[:, 4 * a:4 * a + 4, t0:t0 + m], src[:, :, 0:m]).then_inc(moved, 1)


def rms_norm(c, src, gain, dst, square):
    nc = c.nc
    rstd = c.work[:, 0:NT]
    with c.stage("norm_" + gain) as st:
        squared, summed = st.sem("squares_ready"), st.sem("sums_in_psum")
        means, roots = st.sem("means_ready"), st.sem("roots_ready")
        block = st.block()

        @block.scalar
        def _(act):
            for k in range(KT):
                nc.scalar.activation(square[:, k, :], src[:, k, :], ACT.Square).then_inc(squared, 1)
            act.wait_ge(means, 1)
            nc.scalar.activation(rstd, rstd, ACT.Sqrt).then_inc(roots, 1)

        @block.tensor
        def _(pe):
            for k in range(KT):
                pe.wait_ge(squared, k + 1)
                nc.tensor.matmul(c.bank[0][:, :], c.ones, square[:, k, 0:TP], start=(k == 0), stop=(k == KT - 1))
                last = nc.tensor.matmul(c.bank[1][:, 0:NB], c.ones, square[:, k, TP:NT],
                                        start=(k == 0), stop=(k == KT - 1))
            last.then_inc(summed, 1)

        @block.vector
        def _(dve):
            dve.wait_ge(summed, 1)
            for bank, a, b in ((0, 0, TP), (1, TP, NT)):
                nc.vector.tensor_scalar(rstd[:, a:b], c.bank[bank][:, 0:b - a], 1.0 / D, EPS, ALU.mult, ALU.add)
            dve.drain().then_inc(means, 1)
            dve.wait_ge(roots, 1)
            nc.vector.reciprocal(rstd, rstd)
            dve.drain()
            for k in range(KT):
                nc.vector.scalar_tensor_tensor(dst[:, k, :], src[:, k, :], c.vec(gain, k), rstd, ALU.mult, ALU.mult)


def project(c, name, x, kt, weight, tiles, evacuate, engine, out_rows=P):
    nc = c.nc
    U = 4 if tiles % 4 == 0 else 1
    ring = [c.work[:, kt * out_rows * u:kt * out_rows * (u + 1)].rearrange("p (k n) -> p k n", n=out_rows)
            for u in range(U)]
    wv = weight.rearrange("(k p) n -> p k n", p=P)
    with c.stage(name) as st:
        ready = [st.sem(f"weight_ready{u}") for u in range(U)]
        done, free = st.sem("tiles_done"), st.sem("bank_free")
        block = st.block()

        @block.sync
        def _(sp):
            with sp.Fori(0, tiles // U) as i:
                for u in range(U):
                    sp.wait_ge(done, i * U + (u + 1))
                    sp.dma_start(ring[u], wv[:, :, ds((i * U + u) * out_rows, out_rows)]).then_inc(ready[u], 16)

        @block.tensor
        def _(pe):
            pe.sem_inc(done, U)
            with pe.Fori(0, tiles // U) as i:
                for u in range(U):
                    pe.wait_ge(ready[u], i * 16 + 16)
                    pe.wait_ge(free, i * U + (u + 1))
                    for k in range(kt):
                        for s in range(2):
                            last = nc.tensor.matmul(c.pair[u][0:out_rows, s, :], ring[u][:, k, :],
                                                    x[:, k, HALF * s:HALF * s + HALF],
                                                    start=(k == 0), stop=(k == kt - 1))
                    last.then_inc(done, 1)

        def copies(eng):
            eng.sem_inc(free, U)
            with eng.Fori(0, tiles // U) as i:
                for u in range(U):
                    eng.wait_ge(done, i * U + (U + u + 1))
                    evacuate(eng, i * U + u, c.pair[u][0:out_rows]).then_inc(free, 1)

        if engine == "act":
            block.scalar(copies)
        else:
            block.vector(copies)


def copy_to(c, dst, rows=P):
    def evacuate(eng, m, tile):
        return c.nc.scalar.activation(dst[0:rows, ds(m, 1), :].rearrange("p a (s t) -> p (a s) t", s=2), tile,
                                      ACT.Copy)
    return evacuate


def add_to(c, dst):
    def evacuate(eng, m, tile):
        o = dst[:, ds(m, 1), :].rearrange("p a (s t) -> p (a s) t", s=2)
        return c.nc.vector.tensor_tensor(o, o, tile, ALU.add)
    return evacuate


def elementwise(c, name, body):
    with c.stage(name) as st:
        block = st.block()

        @block.vector
        def _(dve):
            body(dve)


def transpose_out(c, name, src, cols, stores):
    nc = c.nc
    with c.stage(name) as st:
        turned, moved, stored = st.sem("rows_in_psum"), st.sem("rows_moved"), st.sem("rows_stored")
        block = st.block()

        @block.tensor
        def _(pe):
            for n, (a, b, _) in enumerate(stores):
                if n >= 2:
                    pe.wait_ge(moved, 2 * (n - 1))
                for k in range(KT):
                    last = nc.tensor.transpose(c.bank[2 * (n % 2) + k // 4][0:b - a, P * (k % 4):P * (k % 4) + P],
                                               src[:, k, a:b], c.ident)
                last.then_inc(turned, 1)

        @block.vector
        def _(dve):
            for n, (a, b, _) in enumerate(stores):
                dve.wait_ge(turned, n + 1)
                for k in range(2):
                    nc.vector.tensor_copy(c.work[0:b - a, D * n + 512 * k:D * n + 512 * k + 512],
                                          c.bank[2 * (n % 2) + k][0:b - a, :]).then_inc(moved, 1)

        @block.sync
        def _(sp):
            for n, (a, b, dst) in enumerate(stores):
                sp.wait_ge(moved, 2 * (n + 1))
                sp.dma_start(dst, c.work[0:b - a, D * n:D * n + D]).then_inc(stored, 16)
            sp.wait_ge(stored, 16 * len(stores))



def rwkv_inputs(c):
    nc, io = c.nc, c.io
    xn, xx, xi = c.slot(1), c.slot(2), c.slot(3)

    def differences(dve):
        nc.vector.tensor_tensor(xx[:, :, 1:TP], xn[:, :, 0:TP - 1], xn[:, :, 1:TP], ALU.subtract)
        nc.vector.tensor_scalar(xx[:, :, 0:1], xn[:, :, 0:1], -1.0, None, ALU.mult)
        nc.vector.tensor_tensor(xx[:, :, TP:NT], xx[:, :, TP:NT], xn[:, :, TP:NT], ALU.subtract)

    elementwise(c, "shift", differences)

    def mixed(n):
        def body(dve):
            for k in range(KT):
                nc.vector.scalar_tensor_tensor(xi[:, k, :], xx[:, k, :], c.vec(f"mu{n}", k), xn[:, k, :],
                                               ALU.mult, ALU.add)
        elementwise(c, f"mix{n}", body)

    hidden = c.slots[:, 4160 * 9:4160 * 9 + NT].rearrange("p (a t) -> p a t", a=1)

    def squash(func, rows):
        def evacuate(eng, m, tile):
            return nc.scalar.activation(hidden[0:rows, 0, :].rearrange("p (s t) -> p s t", s=2), tile, func)
        return evacuate

    def second(name, weight, rows, dst, bias):
        w2 = c.work[0:rows, 4096:4096 + D]
        with c.stage(name) as st:
            ready, full, free = st.sem("weight_ready"), st.sem("bank_full"), st.sem("bank_free")
            block = st.block()

            @block.sync
            def _(sp):
                sp.dma_start(w2, weight).then_inc(ready, 16)

            @block.tensor
            def _(pe):
                pe.wait_ge(ready, 16)
                for m in range(KT):
                    if m >= 4:
                        pe.wait_ge(free, m - 3)
                    for s in range(2):
                        last = nc.tensor.matmul(c.pair[m % 4][:, s, :], w2[:, P * m:P * m + P],
                                                hidden[0:rows, 0, HALF * s:HALF * s + HALF], start=True, stop=True)
                    last.then_inc(full, 1)

            @block.scalar
            def _(act):
                for m in range(KT):
                    act.wait_ge(full, m + 1)
                    o = dst[:, m, :].rearrange("p (s t) -> p s t", s=2)
                    if bias:
                        nc.scalar.activation(o, c.pair[m % 4], ACT.Sigmoid, bias=c.vec(bias, m)).then_inc(free, 1)
                    else:
                        nc.scalar.activation(o, c.pair[m % 4], ACT.Copy).then_inc(free, 1)

    for n, w, dst in ((0, "rw_wr", 4), (2, "rw_wk", 5), (3, "rw_wv", 6)):
        mixed(n)
        project(c, w, xi, KT, io[w][0, :, :], KT, copy_to(c, c.slot(dst)), "act")
    mixed(1)
    project(c, "rw_w1", xi, KT, io["rw_w1"][0, :, :], 1, squash(ACT.Tanh, 64), "act", 64)
    second("rw_w2", io["rw_w2"][0, :, :], 64, c.slot(7), "w0")
    mixed(4)
    project(c, "rw_a1", xi, KT, io["rw_a1"][0, :, :], 1, squash(ACT.Copy, 64), "act", 64)
    second("rw_a2", io["rw_a2"][0, :, :], 64, c.slot(8), "a0")
    mixed(5)
    project(c, "rw_g1", xi, KT, io["rw_g1"][0, :, :], 1, squash(ACT.Sigmoid, P), "act")
    second("rw_g2", io["rw_g2"][0, :, :], P, c.slot(1), None)
    elementwise(c, "gate_home", lambda dve: nc.vector.tensor_copy(c.flat(9), c.flat(1)))


def rwkv_prepare(c):
    nc, io = c.nc, c.io
    r, k_, v, w, a = (c.slot(n) for n in range(4, 9))
    kk, tmp, bonus = c.slot(1), c.slot(2), c.slot(3)
    keep = c.work[:, 0:TP]
    norm = [c.work[:, TP + NT * n:TP + NT * (n + 1)] for n in range(2)]
    ends = c.small[:, 0:KT * NCH].rearrange("p (k n) -> p k n", n=NCH)
    NLOG = -float(np.exp(-0.5))
    with c.stage("rwkv_prepare") as st:
        keep_in = st.sem("keep_loaded")
        sq, nrm, nfree = st.sem("squares_ready"), st.sem("norms_in_psum"), st.sem("norms_used")
        rk, bon, bfree = st.sem("rk_ready"), st.sem("bonus_in_psum"), st.sem("bonus_used")
        g_ready, ex, done = st.sem("decay_sums_ready"), st.sem("factors_ready"), st.sem("tile_done")
        roots = st.sem("norms_inverted")
        block = st.block()

        @block.sync
        def _(sp):
            lo, hi = CCOL["keep"]
            sp.dma_start(keep, io["consts"][:, lo:hi]).then_inc(keep_in, 16)

        @block.vector
        def _(dve):
            dve.wait_ge(keep_in, 16)
            for k in range(KT):
                nc.vector.tensor_scalar(kk[:, k, :], k_[:, k, :], c.vec("kk", k), None, ALU.mult)
                dve.drain()
                nc.vector.tensor_tensor(tmp[:, k, :], kk[:, k, :], kk[:, k, :], ALU.mult).then_inc(sq, 1)
                nc.vector.tensor_scalar(bonus[:, k, :], a[:, k, :], -1.0, c.vec("ka", k), ALU.add, ALU.mult)
                dve.drain()
                nc.vector.scalar_tensor_tensor(k_[:, k, :], bonus[:, k, :], 1.0, k_[:, k, :], ALU.add, ALU.mult)
                dve.drain()
                nc.vector.scalar_tensor_tensor(bonus[:, k, :], r[:, k, :], c.vec("rk", k), k_[:, k, :],
                                               ALU.mult, ALU.mult).then_inc(rk, 1)
                dve.wait_ge(nrm, k + 1)
                rn = norm[k % 2]
                for bank, lo, hi in ((0, 0, TP), (1, TP, NT)):
                    nc.vector.tensor_scalar(rn[:, lo:hi], c.bank[bank][:, 0:hi - lo], 1e-24, None, ALU.max)
                dve.drain().then_inc(nfree, 1)
                dve.wait_ge(roots, k + 1)
                nc.vector.reciprocal(rn, rn)
                dve.drain()
                nc.vector.tensor_tensor(kk[:, k, :], kk[:, k, :], rn, ALU.mult)
                dve.drain()
                nc.vector.tensor_tensor(a[:, k, :], a[:, k, :], kk[:, k, :], ALU.mult)
                dve.wait_ge(bon, k + 1)
                for bank, lo, hi in ((2, 0, TP), (3, TP, NT)):
                    last = nc.vector.tensor_tensor(bonus[:, k, lo:hi], c.bank[bank][:, 0:hi - lo], v[:, k, lo:hi],
                                                   ALU.mult)
                last.then_inc(bfree, 1)
                nc.vector.tensor_scalar(w[:, k, :], w[:, k, :], NLOG, None, ALU.mult)
                dve.drain()
                nc.vector.tensor_tensor_scan(tmp[:, k, 0:TP], keep, w[:, k, 0:TP], 0.0, ALU.mult, ALU.add)
                dve.drain()
                nc.vector.tensor_copy(ends[:, k, :], tmp[:, k, CH - 1:TP:CH])
                nc.vector.tensor_tensor(w[:, k, 0:TP], tmp[:, k, 0:TP], w[:, k, 0:TP],
                                        ALU.subtract).then_inc(g_ready, 1)

        @block.tensor
        def _(pe):
            for k in range(KT):
                if k >= 1:
                    pe.wait_ge(nfree, k)
                pe.wait_ge(sq, k + 1)
                nc.tensor.matmul(c.bank[0][:, :], c.headones, tmp[:, k, 0:TP], start=True, stop=True)
                nc.tensor.matmul(c.bank[1][:, 0:NB], c.headones, tmp[:, k, TP:NT], start=True,
                                 stop=True).then_inc(nrm, 1)
                if k >= 1:
                    pe.wait_ge(bfree, k)
                pe.wait_ge(rk, k + 1)
                nc.tensor.matmul(c.bank[2][:, :], c.headones, bonus[:, k, 0:TP], start=True, stop=True)
                nc.tensor.matmul(c.bank[3][:, 0:NB], c.headones, bonus[:, k, TP:NT], start=True,
                                 stop=True).then_inc(bon, 1)

        @block.scalar
        def _(act):
            for k in range(KT):
                act.wait_ge(nfree, k + 1)
                nc.scalar.activation(norm[k % 2], norm[k % 2], ACT.Sqrt).then_inc(roots, 1)
                act.wait_ge(g_ready, k + 1)
                nc.scalar.activation(ends[:, k, :], ends[:, k, :], ACT.Exp)
                nc.scalar.activation(w[:, k, :], w[:, k, :], ACT.Exp)

    prompt = slice(0, TP)
    with c.stage("rwkv_scale") as st:
        up, down = st.sem("growth_ready"), st.sem("shrink_ready")
        used = st.sem("growth_used")
        block = st.block()
        bufs = [c.work[:, 2048 + TP * n:2048 + TP * (n + 1)] for n in range(4)]

        @block.scalar
        def _(act):
            for k in range(KT):
                if k >= 2:
                    act.wait_ge(used, k - 1)
                nc.scalar.activation(bufs[k % 2], tmp[:, k, prompt], ACT.Exp)
                nc.scalar.activation(bufs[2 + k % 2], tmp[:, k, prompt], ACT.Exp, scale=-1.0).then_inc(up, 1)

        @block.vector
        def _(dve):
            for k in range(KT):
                nc.vector.scalar_tensor_tensor(w[:, k, prompt], kk[:, k, prompt], -1.0, w[:, k, prompt],
                                               ALU.mult, ALU.mult)
                dve.wait_ge(up, k + 1)
                nc.vector.tensor_tensor(r[:, k, prompt], r[:, k, prompt], bufs[k % 2], ALU.mult)
                nc.vector.tensor_tensor(k_[:, k, prompt], k_[:, k, prompt], bufs[2 + k % 2], ALU.mult)
                nc.vector.tensor_tensor(a[:, k, prompt], a[:, k, prompt], bufs[2 + k % 2], ALU.mult).then_inc(used, 1)


def sample_state(c):
    nc, io = c.nc, c.io
    arrays = [c.slot(4), c.slot(5), c.slot(6), c.slot(7), c.slot(1), c.slot(8)]
    scratch = nc.dram_tensor("sample_vectors", [6, NB, D], F32).ap()
    out_scratch = nc.dram_tensor("sample_mixed", [NB, D], F32).ap()
    rows = c.work[0:NB, 0:6 * D].rearrange("b (n e) -> b n e", e=D)
    with c.stage("sample_vectors") as st:
        turned, moved, stored = st.sem("rows_in_psum"), st.sem("rows_moved"), st.sem("rows_stored")
        block = st.block()

        @block.tensor
        def _(pe):
            for n, a in enumerate(arrays):
                if n >= 2:
                    pe.wait_ge(moved, 2 * (n - 1))
                for k in range(KT):
                    last = nc.tensor.transpose(c.bank[2 * (n % 2) + k // 4][0:NB, P * (k % 4):P * (k % 4) + P],
                                               a[:, k, TP:NT], c.ident)
                last.then_inc(turned, 1)

        @block.vector
        def _(dve):
            for n in range(6):
                dve.wait_ge(turned, n + 1)
                for k in range(2):
                    nc.vector.tensor_copy(rows[:, n, 512 * k:512 * k + 512],
                                          c.bank[2 * (n % 2) + k][0:NB, :]).then_inc(moved, 1)

        @block.sync
        def _(sp):
            sp.wait_ge(moved, 12)
            sp.dma_start(scratch.rearrange("n b e -> b n e"), rows).then_inc(stored, 16)
            sp.wait_ge(stored, 16)

    S = c.flat(1)[:, 0:HD * HD].rearrange("p (i j) -> p i j", j=HD)
    t1 = c.flat(2)[:, 0:HD * HD].rearrange("p (i j) -> p i j", j=HD)
    t2 = c.work[:, 0:HD * HD].rearrange("p (i j) -> p i j", j=HD)
    vec = c.work[:, 4096:4096 + 6 * HD].rearrange("p (n d) -> p n d", d=HD)
    sa, o = c.work[:, 4608:4608 + HD], c.work[:, 4672:4672 + HD]
    key = lambda n: vec[:, n, :].unsqueeze(1).to_broadcast([P, HD, HD])
    val = lambda a: a.unsqueeze(2).to_broadcast([P, HD, HD])
    with c.stage("sample_state") as st:
        loaded, stepped, mixed, stored = (st.sem(n) for n in ("state_loaded", "state_stepped", "output_ready",
                                                              "stored"))
        block = st.block()

        @block.sync
        def _(sp):
            sp.dma_start(vec, scratch.rearrange("n b (h d) -> (b h) n d", d=HD)).then_inc(loaded, 16)
            sp.dma_start(S, io["state_wkv"][0].rearrange("b h i j -> (b h) i j")).then_inc(loaded, 16)
            sp.wait_ge(stepped, 1)
            sp.dma_start(io["o_sample_wkv"][0].rearrange("b h i j -> (b h) i j"), S).then_inc(stored, 16)
            sp.wait_ge(mixed, 1)
            sp.dma_start(out_scratch.rearrange("b (h d) -> (b h) d", d=HD), o).then_inc(stored, 16)
            sp.wait_ge(stored, 32)

        @block.vector
        def _(dve):
            tt = nc.vector.tensor_tensor
            dve.wait_ge(loaded, 32)
            tt(t1, S, key(4), ALU.mult)
            tt(t2, key(1), val(vec[:, 2, :]), ALU.mult)
            dve.drain()
            nc.vector.tensor_reduce(sa, t1, AX.X, ALU.add)
            tt(S, S, key(3), ALU.mult)
            dve.drain()
            tt(t1, key(5), val(sa), ALU.mult)
            tt(S, S, t2, ALU.add)
            dve.drain()
            tt(S, S, t1, ALU.subtract)
            dve.drain().then_inc(stepped, 1)
            tt(t1, S, key(0), ALU.mult)
            dve.drain()
            nc.vector.tensor_reduce(o, t1, AX.X, ALU.add).then_inc(mixed, 1)

    back = c.work[0:NB, 0:D]
    with c.stage("sample_output") as st:
        loaded, turned = st.sem("rows_loaded"), st.sem("columns_in_psum")
        block = st.block()

        @block.sync
        def _(sp):
            sp.dma_start(back, out_scratch).then_inc(loaded, 16)

        @block.tensor
        def _(pe):
            pe.wait_ge(loaded, 16)
            for k in range(KT):
                last = nc.tensor.transpose(c.bank[0][:, NB * k:NB * k + NB], back[:, P * k:P * k + P],
                                           c.ident[0:NB, 0:NB])
            last.then_inc(turned, 1)

        @block.vector
        def _(dve):
            dve.wait_ge(turned, 1)
            nc.vector.tensor_copy(c.slot(4)[:, :, TP:NT], c.bank[0][:, 0:NB * KT].rearrange("p (k b) -> p k b", b=NB))


def rwkv_chunks(c):
    nc, io = c.nc, c.io
    lo, hi = CCOL["ident64"][0], CCOL["joinT0"][1]
    table = c.small[:, 64:64 + hi - lo]
    const = lambda name: table[:, CCOL[name][0] - lo:CCOL[name][1] - lo]
    wide = lambda a: a.unsqueeze(1).to_broadcast([P, KT, CH])
    ends = c.small[:, 0:KT * NCH].rearrange("p (k n) -> p k n", n=NCH)
    area = [c.flat(1, 2), c.work[:, :]]
    names = ["r", "k", "a", "b", "v", "LT", "join", "T", "TT", "X", "MT", "AB", "AK", "Bt", "Kt", "Vt"]
    buf = [{n: area[u][:, 512 * x:512 * x + 512].rearrange("p (k t) -> p k t", t=CH)
            for x, n in enumerate(names)} for u in range(2)]
    for u in range(2):
        buf[u]["RHS"], buf[u]["U"] = buf[u]["X"], buf[u]["T"]
    Z = c.z_state[:, :].rearrange("p (k i) -> p k i", i=HD)
    src = {"r": c.slot(4), "k": c.slot(5), "v": c.slot(6), "a": c.slot(7), "b": c.slot(8)}

    order = [(u, n) for u in range(2) for n in ("LT", "L")]
    filler = {1: ["MT", "AB"], 2: ["AK"], 3: ["Bt"], 4: ["Kt"], 5: ["Vt"]}
    for lvl in range(1, 6):
        order += [(u, f"X{lvl}") for u in range(2)]
        order += [(u, n) for n in filler[lvl] for u in range(2)]
        order += [(u, f"{n}{lvl}") for u in range(2) for n in (("T", "TT") if lvl < 5 else ("TT",))]
    order += [(u, n) for u in range(2) for n in ("RHS", "U", "O", "Z")]
    place, per_round = {}, [0] * 8
    for u in range(2):
        for x, n in enumerate([n for v, n in order if v == u]):
            b = 4 * u + x % 4
            place[u, n] = (b, per_round[b])
            per_round[b] += 1

    with c.stage("rwkv_chunks") as st:
        table_in = st.sem("masks_loaded")
        chunk_ready = [st.sem(f"chunk_ready{u}") for u in range(2)]
        joins = [st.sem(f"join_ready{u}") for u in range(2)]
        state_ready = st.sem("state_ready", 1)
        full = [st.sem(f"product_in_bank{b}") for b in range(8)]
        taken = [st.sem(f"product_taken{b}", 1) for b in range(8)]
        block = st.block()

        def produced(eng, i, u, name):
            b, n = place[u, name]
            eng.wait_ge(full[b], i * per_round[b] + (n + 1))

        def in_sbuf(eng, i, u, names, before=None):
            least = {}
            for name in names:
                b, n = place[u, name]
                least[b] = max(least.get(b, 0), n + 1)
            if before:
                b, n = place[u, before]
                least[b] = max(least.get(b, 0), n)
            for b, n in least.items():
                eng.wait_ge(taken[b], i * per_round[b] + (n + 1))

        def bank(u, name):
            return c.bank[place[u, name][0]][:, :].rearrange("p (k t) -> p k t", t=CH)

        @block.sync
        def _(sp):
            sp.dma_start(table, io["consts"][:, lo:hi]).then_inc(table_in, 16)

        @block.tensor
        def _(pe):
            pe.wait_ge(table_in, 16)

            def product(i, u, name, terms, needs=()):
                b = place[u, name][0]
                in_sbuf(pe, i, u, needs, before=name)
                pe.nop(nofuse=True)
                out = bank(u, name)
                for k in range(KT):
                    for q in range(2):
                        half = slice(HD * q, HD * q + HD)
                        for x, (lhsT, rhs) in enumerate(terms):
                            right = const("ident64")[half, :] if rhs is None else rhs[half, k, :]
                            last = nc.tensor.matmul(out[half, k, :], lhsT[half, k, :], right,
                                                    start=(x == 0), stop=(x == len(terms) - 1))
                return last.then_inc(full[b], 1)

            with pe.Fori(0, NCH // 2) as i:
                for u in range(2):
                    w = buf[u]
                    pe.wait_ge(chunk_ready[u], i * 5 + 5)
                    product(i, u, "LT", [(w["b"], w["a"])])
                    product(i, u, "L", [(w["a"], w["b"])])
                for lvl in range(1, 6):
                    for u in range(2):
                        w = buf[u]
                        pe.wait_ge(joins[u], i * 5 + lvl)
                        product(i, u, f"X{lvl}", [(w["join"], w["T"])], ["L" if lvl == 1 else f"T{lvl - 1}"])
                    for name in filler[lvl]:
                        for u in range(2):
                            w = buf[u]
                            product(i, u, name, {
                                "MT": [(w["k"], w["a"])], "AB": [(w["b"], w["r"])], "AK": [(w["k"], w["r"])],
                                "Bt": [(w["b"], None)], "Kt": [(w["k"], None)], "Vt": [(w["v"], None)]}[name])
                    for u in range(2):
                        w = buf[u]
                        needs = [f"X{lvl}", "LT" if lvl == 1 else f"TT{lvl - 1}"]
                        if lvl < 5:
                            product(i, u, f"T{lvl}", [(w["TT"], w["X"])], needs)
                        product(i, u, f"TT{lvl}", [(w["X"], w["TT"])], needs)
                for u in range(2):
                    w = buf[u]
                    pe.wait_ge(state_ready, i * 2 + (u + 2))
                    product(i, u, "RHS", [(w["a"], Z), (w["MT"], w["Vt"])], ["MT", "Vt"])
                    product(i, u, "U", [(w["TT"], w["RHS"])], ["TT5", "RHS"])
                    product(i, u, "O", [(Z, w["r"]), (w["U"], w["AB"]), (w["Vt"], w["AK"])], ["U", "AB", "AK"])
                    product(i, u, "Z", [(w["Bt"], w["U"]), (w["Kt"], w["Vt"])], ["Bt", "Kt"])

        def take(eng, i, u, name, op):
            produced(eng, i, u, name)
            op(bank(u, name)).then_inc(taken[place[u, name][0]], 1)

        @block.scalar
        def _(act):
            with act.Fori(0, NCH // 2) as i:
                for u in range(2):
                    act.wait_ge(state_ready, i * 2 + (u + 1))
                    for n in ("a", "v"):
                        nc.scalar.copy(buf[u][n], src[n][:, :, ds(i * 2 * CH + u * CH, CH)]).then_inc(chunk_ready[u], 1)
                for u, name in order:
                    stem = name.rstrip("0123456789")
                    if stem in ("X", "Bt", "Kt", "Vt", "RHS", "U"):
                        take(act, i, u, name, lambda p: nc.scalar.copy(buf[u][stem], p))
                    if stem == "O":
                        take(act, i, u, name,
                             lambda p: nc.scalar.copy(c.slot(4)[:, :, ds(i * 2 * CH + u * CH, CH)], p))

        @block.gpsimd
        def _(pool):
            pool.wait_ge(table_in, 16)
            with pool.Fori(0, NCH // 2) as i:
                for u in range(2):
                    pool.wait_ge(state_ready, i * 2 + (u + 1))
                    for n in ("b", "r", "k"):
                        nc.gpsimd.tensor_copy(buf[u][n],
                                              src[n][:, :, ds(i * 2 * CH + u * CH, CH)]).then_inc(chunk_ready[u], 1)
                for lvl in range(1, 6):
                    for u in range(2):
                        if lvl == 1:
                            in_sbuf(pool, i, u, ["LT"])
                        else:
                            produced(pool, i, u, f"X{lvl - 1}")
                        nc.gpsimd.tensor_tensor(buf[u]["join"], buf[u]["LT"], wide(const(f"join{lvl}")),
                                                ALU.mult).then_inc(joins[u], 1)

        @block.vector
        def _(dve):
            nc.vector.memset(Z, 0.0).then_inc(state_ready, 1)
            dve.wait_ge(table_in, 16)
            tt = nc.vector.tensor_tensor
            with dve.Fori(0, NCH // 2) as i:
                for u, name in order:
                    w = buf[u]
                    stem = name.rstrip("0123456789")
                    if name == "LT":
                        produced(dve, i, u, name)
                        nc.vector.tensor_copy(w["LT"], bank(u, name))
                        tt(w["TT"], bank(u, name), wide(const("join0")), ALU.mult)
                        dve.drain()
                        tt(w["TT"], w["TT"], wide(const("ident64")), ALU.add).then_inc(taken[place[u, name][0]], 1)
                    if name == "L":
                        produced(dve, i, u, name)
                        tt(w["T"], bank(u, name), wide(const("joinT0")), ALU.mult)
                        dve.drain()
                        tt(w["T"], w["T"], wide(const("ident64")), ALU.add).then_inc(taken[place[u, name][0]], 1)
                    if name in ("MT", "AB", "AK"):
                        mask = const("before" if name == "MT" else "upto")
                        take(dve, i, u, name, lambda p: tt(w[name], p, wide(mask), ALU.mult))
                    if stem in ("T", "TT"):
                        take(dve, i, u, name, lambda p: tt(w[stem], w[stem], p, ALU.add))
                    if name == "Z":
                        take(dve, i, u, name, lambda p: tt(Z, Z, p, ALU.add))
                        dve.drain()
                        end = ends[:, :, ds(i * 2 + u, 1)].to_broadcast([P, KT, HD])
                        tt(Z, Z, end, ALU.mult).then_inc(state_ready, 1)


def rwkv_state_out(c):
    nc, io = c.nc, c.io
    Z = c.z_state[:, :].rearrange("p (k i) -> p k i", i=HD)
    rows = c.work[0:HD, 0:D]
    with c.stage("rwkv_state_out") as st:
        turned, moved, stored = st.sem("state_in_psum"), st.sem("state_moved"), st.sem("state_stored")
        block = st.block()

        @block.tensor
        def _(pe):
            for k in range(KT):
                last = nc.tensor.transpose(c.bank[k // 4][0:HD, P * (k % 4):P * (k % 4) + P], Z[:, k, :], c.ident)
            last.then_inc(turned, 1)

        @block.vector
        def _(dve):
            dve.wait_ge(turned, 1)
            for a in range(2):
                nc.vector.tensor_copy(rows[:, 512 * a:512 * a + 512], c.bank[a][0:HD, :]).then_inc(moved, 1)

        @block.sync
        def _(sp):
            sp.wait_ge(moved, 2)
            sp.dma_start(io["o_prompt_wkv"][0, 0].rearrange("h i j -> i h j"),
                         rows.rearrange("i (h j) -> i h j", j=HD)).then_inc(stored, 16)
            sp.wait_ge(stored, 16)


def rwkv_finish(c):
    nc = c.nc
    o, bonus, g, sq = c.slot(4), c.slot(3), c.slot(9), c.slot(1)
    rn = c.work[:, 0:NT]
    cols = ((0, 0, TP), (1, TP, NT))
    with c.stage("rwkv_finish") as st:
        mean, centred, var, used = (st.sem(n) for n in ("mean_in_psum", "squares_ready", "variance_in_psum",
                                                        "banks_used"))
        roots = st.sem("deviation_inverted")
        block = st.block()

        @block.scalar
        def _(act):
            for k in range(KT):
                act.wait_ge(used, 2 * k + 2)
                nc.scalar.activation(rn, rn, ACT.Sqrt).then_inc(roots, 1)

        @block.tensor
        def _(pe):
            for k in range(KT):
                if k >= 1:
                    pe.wait_ge(used, 2 * k)
                nc.tensor.matmul(c.bank[0][:, :], c.headones, o[:, k, 0:TP], start=True, stop=True)
                nc.tensor.matmul(c.bank[1][:, 0:NB], c.headones, o[:, k, TP:NT], start=True,
                                 stop=True).then_inc(mean, 1)
                pe.wait_ge(centred, k + 1)
                nc.tensor.matmul(c.bank[2][:, :], c.headones, sq[:, k, 0:TP], start=True, stop=True)
                nc.tensor.matmul(c.bank[3][:, 0:NB], c.headones, sq[:, k, TP:NT], start=True,
                                 stop=True).then_inc(var, 1)

        @block.vector
        def _(dve):
            for k in range(KT):
                dve.wait_ge(mean, k + 1)
                for b, lo, hi in cols:
                    nc.vector.scalar_tensor_tensor(sq[:, k, lo:hi], c.bank[b][:, 0:hi - lo], -1.0 / HD, o[:, k, lo:hi],
                                                   ALU.mult, ALU.add)
                dve.drain()
                nc.vector.tensor_copy(o[:, k, :], sq[:, k, :])
                dve.drain().then_inc(used, 1)
                nc.vector.tensor_tensor(sq[:, k, :], sq[:, k, :], o[:, k, :], ALU.mult).then_inc(centred, 1)
                dve.wait_ge(var, k + 1)
                for b, lo, hi in cols:
                    nc.vector.tensor_scalar(rn[:, lo:hi], c.bank[2 + b][:, 0:hi - lo], 1.0 / HD, GN_EPS,
                                            ALU.mult, ALU.add)
                dve.drain().then_inc(used, 1)
                dve.wait_ge(roots, k + 1)
                nc.vector.reciprocal(rn, rn)
                dve.drain()
                nc.vector.scalar_tensor_tensor(o[:, k, :], o[:, k, :], c.vec("lnw", k), rn, ALU.mult, ALU.mult)
                dve.drain()
                nc.vector.scalar_tensor_tensor(o[:, k, :], o[:, k, :], c.vec("lnb", k), bonus[:, k, :],
                                               ALU.add, ALU.add)
                dve.drain()
                nc.vector.tensor_tensor(o[:, k, :], o[:, k, :], g[:, k, :], ALU.mult)



def route(c, layer):
    nc, io = c.nc, c.io
    x = c.slot(1)
    NTILE, NL, NG, EG = TT + 1, 36, 4, 8
    wr = c.work[:, 0:KT * NL].rearrange("p (k n) -> p k n", n=NL)
    bias = c.work[0:1, 300:300 + NL]
    at = [400]

    def area(*shape):
        n = int(np.prod(shape))
        a = c.work[:, at[0]:at[0] + n]
        at[0] += n
        return a if len(shape) == 1 else a.rearrange("p (a b) -> p a b", b=shape[1])

    rank4, rank8 = area(NG), area(EG)
    L = area(NTILE, NL)
    gmax, gexp, gsum, gkey, gtop = area(NTILE, 1), area(NTILE, NG), area(NTILE, 1), area(NTILE, NG), area(NTILE, 1)
    ghot, picked, part = area(NTILE, NG), area(NTILE, EG), area(NTILE, EG)
    m1, m2, k1, h1, h2 = area(NTILE, 1), area(NTILE, 1), area(NTILE, EG), area(NTILE, EG), area(NTILE, EG)
    e2, w1 = area(NTILE, 1), area(NTILE, 1)
    hot = [area(NTILE, E) for _ in range(2)]
    both, place = area(NTILE, E), area(NTILE, E)
    valid, token, before = area(NTILE, 1), area(NTILE, 1), area(P)
    count, jobs_of, start, more = area(E), area(E), area(E), area(E)
    ones = area(E)
    job_id, owner = area(JOBS + 1), area(JOBS + 1)
    cube = area((JOBS + 1) * E)[0:1].rearrange("p (j e) -> p j e", e=E)
    row = area(2, NTILE)
    row_u = area(2, NTILE).bitcast(U32)
    entry = area(2 * NTILE * 4).rearrange("p (a n w) -> p a n w", a=2, w=4)
    entry_u = entry.bitcast(U32)
    blank = c.flat(4)[:, 0:(JOBS + 1) * 4].rearrange("p (j w) -> p j w", w=4)
    rows = c.flat(2, 2)[:, 0:NTILE * D].rearrange("p (n e) -> p n e", e=D)
    job_float = area(JOBS + 1)
    lists = c.lists.rearrange("(j p) w -> p j w", p=P)
    wide = lambda a, n: a.to_broadcast([P, NTILE, n])
    with c.stage(f"route{layer}") as st:
        loaded, logits, differences, exps, ready = (st.sem(n) for n in (
            "router_loaded", "logits_in_psum", "differences_ready", "exponentials_ready", "weights_ready"))
        turned, moved, stored, blanked = (st.sem(n) for n in ("tokens_turned", "tokens_moved", "rows_stored",
                                                              "lists_blank"))
        chosen, counted, placed, listed = (st.sem(n) for n in ("choices_ready", "places_in_psum", "entries_ready",
                                                               "entries_listed"))
        block = st.block()

        @block.sync
        def _(sp):
            sp.dma_start(wr[:, :, 0:NG], io["moe_wrg"][layer].rearrange("(k p) n -> p k n", p=P)).then_inc(loaded, 16)
            sp.dma_start(wr[:, :, NG:NL], io["moe_wre"][layer].rearrange("(k p) n -> p k n", p=P)).then_inc(loaded, 16)
            sp.dma_start(bias[:, 0:NG], io["moe_brg"][layer:layer + 1, :]).then_inc(loaded, 16)
            sp.dma_start(bias[:, NG:NL], io["moe_bre"][layer:layer + 1, :]).then_inc(loaded, 16)
            for dst, name in ((rank4, "rank4"), (rank8, "rank8"), (valid, "valid"), (token, "token"),
                              (before, "triangle"), (job_id, "jobid")):
                sp.dma_start(dst, io["consts"][:, CCOL[name][0]:CCOL[name][1]]).then_inc(loaded, 16)
            sp.wait_ge(blanked, 1)
            sp.dma_start(lists, blank.bitcast(U32)).then_inc(stored, 16)
            sp.wait_ge(moved, 2 * NTILE)
            sp.dma_start(c.token_rows[0:TP].rearrange("(n p) e -> p n e", p=P), rows[:, 0:TT]).then_inc(stored, 16)
            sp.dma_start(c.token_rows[TP:NT], rows[0:NB, TT]).then_inc(stored, 16)
            sp.wait_ge(listed, 16 * 2 * NTILE)
            sp.dma_start(c.job_lists, lists).then_inc(stored, 16)
            sp.wait_ge(stored, 64)

        @block.gpsimd
        def _(pool):
            pool.wait_ge(placed, 1)
            pool.wait_ge(stored, 16 * 3)
            for n in range(NTILE):
                m = P if n < TT else NB
                for a in range(2):
                    nc.gpsimd.indirect_dma_start(
                        out=c.lists, out_offset=bass.IndirectOffsetOnAxis(ap=row_u[0:m, a, n:n + 1], axis=0),
                        in_=entry_u[0:m, a, n, :], in_offset=None,
                        bounds_check=(JOBS + 1) * P - 1, oob_is_err=True).then_inc(listed, 16)

        @block.tensor
        def _(pe):
            pe.wait_ge(loaded, 16 * 10)
            for n in range(NTILE):
                m = P if n < TT else NB
                out = c.bank[0][0:m, NL * n:NL * n + NL]
                for k in range(KT):
                    nc.tensor.matmul(out, x[:, k, P * n:P * n + m], wr[:, k, :], start=(k == 0), stop=False)
                last = nc.tensor.matmul(out, c.ones[0:1, 0:m], bias, start=False, stop=True)
            last.then_inc(logits, 1)
            for n in range(NTILE):
                m = P if n < TT else NB
                if n:
                    pe.wait_ge(moved, 2 * n)
                for k in range(KT):
                    last = nc.tensor.transpose(c.bank[1 + k // 4][0:m, P * (k % 4):P * (k % 4) + P],
                                               x[:, k, P * n:P * n + m], c.ident)
                last.then_inc(turned, 1)
            pe.wait_ge(chosen, 1)
            for n in range(NTILE):
                for m in range(n + 1):
                    nc.tensor.matmul(c.bank[3][:, E * n:E * n + E], c.ones if m < n else before, both[:, m, :],
                                     start=(m == 0), stop=(m == n))
            for n in range(NTILE):
                last = nc.tensor.matmul(c.bank[4][:, 0:E], c.ones, both[:, n, :], start=(n == 0),
                                        stop=(n == NTILE - 1))
            last.then_inc(counted, 1)

        @block.scalar
        def _(act):
            act.wait_ge(differences, 1)
            nc.scalar.activation(gexp, gkey, ACT.Exp).then_inc(exps, 1)
            act.wait_ge(differences, 2)
            nc.scalar.activation(e2, m2, ACT.Exp).then_inc(exps, 1)

        @block.vector
        def _(dve):
            tt, ts = nc.vector.tensor_tensor, nc.vector.tensor_scalar
            reduce = nc.vector.tensor_reduce
            nc.vector.memset(L, 0.0)
            blank_u = blank.bitcast(U32)
            nc.vector.memset(blank, 0.0)
            nc.vector.memset(job_float, float(1 << 20))
            dve.drain()
            for w in range(2):
                nc.vector.tensor_copy(blank_u[:, :, w], job_float)
            dve.drain().then_inc(blanked, 1)
            for n in range(NTILE):
                m = P if n < TT else NB
                dve.wait_ge(turned, n + 1)
                for a in range(2):
                    nc.vector.tensor_copy(rows[0:m, n, 512 * a:512 * a + 512], c.bank[1 + a][0:m, :]).then_inc(moved, 1)
            dve.wait_ge(logits, 1)
            dve.drain()
            nc.vector.tensor_copy(L[:, 0:TT, :], c.bank[0][:, 0:TT * NL].rearrange("p (a b) -> p a b", b=NL))
            nc.vector.tensor_copy(L[0:NB, TT, :], c.bank[0][0:NB, TT * NL:NTILE * NL])
            dve.drain()
            lg = L[:, :, 0:NG]
            reduce(gmax, lg, AX.X, ALU.max)
            dve.drain()
            tt(gkey, lg, wide(gmax, NG), ALU.subtract)
            dve.drain().then_inc(differences, 1)
            dve.wait_ge(exps, 1)
            reduce(gsum, gexp, AX.X, ALU.add)

            def first_of(hot, values, top, rank, n, key):
                tt(key, values, wide(top, n), ALU.is_equal)
                dve.drain()
                tt(key, key, rank.unsqueeze(1).to_broadcast([P, NTILE, n]), ALU.mult)
                dve.drain()
                reduce(gtop, key, AX.X, ALU.max)
                dve.drain()
                tt(hot, key, wide(gtop, n), ALU.is_equal)
                dve.drain()

            first_of(ghot, lg, gmax, rank4, NG, gkey)
            for g in range(NG):
                dst = picked if g == 0 else part
                tt(dst, L[:, :, NG + EG * g:NG + EG * g + EG], wide(ghot[:, :, g:g + 1], EG), ALU.mult)
                dve.drain()
                if g:
                    tt(picked, picked, part, ALU.add)
                    dve.drain()
            reduce(m1, picked, AX.X, ALU.max)
            dve.drain()
            first_of(h1, picked, m1, rank8, EG, k1)
            nc.vector.scalar_tensor_tensor(part, h1, NEG, picked, ALU.mult, ALU.add)
            dve.drain()
            reduce(m2, part, AX.X, ALU.max)
            dve.drain()
            first_of(h2, part, m2, rank8, EG, k1)
            tt(m2, m2, m1, ALU.subtract)
            dve.drain().then_inc(differences, 1)
            dve.wait_ge(exps, 2)
            ts(w1, e2, 1.0, None, ALU.add)
            dve.drain()
            tt(w1, w1, gsum, ALU.mult)
            dve.drain()
            nc.vector.reciprocal(w1, w1)
            dve.drain()
            tt(e2, e2, w1, ALU.mult)
            dve.drain()
            for a, h in ((0, h1), (1, h2)):
                for g in range(NG):
                    tt(hot[a][:, :, EG * g:EG * g + EG], h, wide(ghot[:, :, g:g + 1], EG), ALU.mult)
                dve.drain()
                tt(hot[a], hot[a], wide(valid, E), ALU.mult)
            dve.drain()
            tt(both, hot[0], hot[1], ALU.add)
            dve.drain().then_inc(chosen, 1)
            for a, w in ((0, w1), (1, e2)):
                nc.vector.tensor_copy(entry_u[:, a, :, 0:1], token)
                ts(row[:, a, :].unsqueeze(2), token, 2.0, float(a), ALU.mult, ALU.add)
                nc.vector.tensor_copy(entry[:, a, :, 2:3], w)
                nc.vector.memset(entry[:, a, :, 3:4], 0.0)
                dve.drain()
                nc.vector.tensor_copy(entry_u[:, a, :, 1:2], row[:, a, :].unsqueeze(2))
            nc.vector.memset(ones, 1.0)
            dve.wait_ge(counted, 1)
            nc.vector.tensor_copy(count, c.bank[4][:, 0:E])
            dve.drain()
            ts(jobs_of, count, 0.0, None, ALU.is_gt)
            for m in range(1, NTILE):
                ts(more, count, float(P * m), None, ALU.is_gt)
                dve.drain()
                tt(jobs_of, jobs_of, more, ALU.add)
                dve.drain()
            nc.vector.tensor_tensor_scan(start, ones, jobs_of, 0.0, ALU.mult, ALU.add)
            dve.drain()
            tt(start, start, jobs_of, ALU.subtract)
            dve.drain()
            tt(cube, start[0:1].unsqueeze(1).to_broadcast([1, JOBS + 1, E]),
               job_id[0:1].unsqueeze(2).to_broadcast([1, JOBS + 1, E]), ALU.is_le)
            ts(more, start, float(P), None, ALU.mult)
            dve.drain()
            reduce(owner[0:1], cube, AX.X, ALU.add)
            tt(place, c.bank[3][:, 0:NTILE * E].rearrange("p (n e) -> p n e", e=E),
               more.unsqueeze(1).to_broadcast([P, NTILE, E]), ALU.add)
            dve.drain()
            ts(owner[0:1], owner[0:1], -1.0, None, ALU.add)
            for a in range(2):
                tt(both, place, hot[a], ALU.mult)
                dve.drain()
                reduce(row[:, a, :].unsqueeze(2), both, AX.X, ALU.add)
                dve.drain()
            nc.vector.tensor_copy(c.job_expert, owner[0:1])
            nc.vector.tensor_copy(row_u, row)
            dve.drain().then_inc(placed, 1)



def experts(c, layer):
    nc, io = c.nc, c.io
    U = 4
    FT = FE // P
    wbuf = [c.flat(4, 6)[:, 6144 * u:6144 * (u + 1)] for u in range(U)]
    wgu = [b[:, 0:4096].rearrange("p (k n) -> p k n", n=2 * FE) for b in wbuf]
    wd = [b[:, 4096:6144].rearrange("p (f n) -> p f n", n=D) for b in wbuf]
    at = [0]

    def two(n):
        at[0] += 2 * n
        assert at[0] <= 8320
        return [c.work[:, at[0] - n * (2 - v):at[0] - n * (1 - v)] for v in range(2)]

    xg, xt = two(D), [a.rearrange("p (k t) -> p k t", t=P) for a in two(D)]
    y = [c.flat(2)[:, D * u:D * u + D] for u in range(U)]
    silu, hid, ht = two(FE), two(FE), [a.rearrange("p (f t) -> p f t", t=P) for a in two(FE)]
    now = two(4) + two(4)
    now_u = [a.bitcast(U32) for a in now]
    src = {"g": io["moe_wgate"][layer].rearrange("g e d f -> (g e) d f"),
           "u": io["moe_wup"][layer].rearrange("g e d f -> (g e) d f"),
           "d": io["moe_wdown"][layer].rearrange("g e f d -> (g e) f d")}

    with c.stage(f"experts{layer}") as st:
        up_ready = [st.sem(f"gate_up_loaded{u}") for u in range(U)]
        down_ready = [st.sem(f"down_loaded{u}") for u in range(U)]
        gathered = [st.sem(f"tokens_gathered{v}") for v in range(2)]
        scattered = [st.sem(f"rows_scattered{u}") for u in range(U)]
        cleared, staged, silu_ready = st.sem("token_buffers_cleared"), st.sem("list_staged"), st.sem("silu_ready")
        start = {"tokens_turned": 2, "tokens_ready": 1, "gate_up_in_psum": 2, "hidden_ready": 2,
                 "hidden_turned": 2, "hidden_turned_ready": 1, "rows_in_psum": U, "rows_ready": 1}
        sems = {n: st.sem(n, s) for n, s in start.items()}
        block = st.block()

        def done(eng, name, i, w, back=0):
            eng.wait_ge(sems[name], i * U + (w + 1 - back + start[name]))

        @block.sync
        def _(sp):
            def load(i, w):
                u = w % U
                e = sp.value_load(c.job_expert[0:1, ds(i * U + w, 1)], min_val=0, max_val=E - 1)
                done(sp, "rows_in_psum", i, w, U)
                for n, a in enumerate("gu"):
                    sp.dma_start(wgu[u][:, :, FE * n:FE * n + FE],
                                 src[a][ds(e, 1)].rearrange("a (k p) n -> p (a k) n", p=P)).then_inc(up_ready[u], 16)
                sp.dma_start(wd[u], src["d"][ds(e, 1)].rearrange("a (k p) n -> p (a k) n",
                                                                 p=P)).then_inc(down_ready[u], 16)

            load(0, 0)
            with sp.Fori(0, JOBS // U) as i:
                for u in range(U):
                    load(i, u + 1)
            sp.wait_ge(up_ready[0], 32 * (JOBS // U + 1))
            sp.wait_ge(down_ready[0], 16 * (JOBS // U + 1))

        @block.gpsimd
        def _(pool):
            def fetch(i, w):
                u, v = w % U, w % 2
                scatters = i + w // U - 1
                if not isinstance(scatters, int) or scatters >= 0:
                    pool.wait_ge(scattered[u], scatters * 16 + 16)
                nc.gpsimd.tensor_copy(now_u[u], c.job_lists[:, ds(i * U + w, 1), :].rearrange(
                    "p a w -> p (a w)")).then_inc(staged, 1)
                pool.wait_ge(staged, i * U + (w + 1))
                done(pool, "tokens_turned", i, w, 2)
                pool.nop(nofuse=True)
                nc.gpsimd.indirect_dma_start(
                    out=xg[v], out_offset=None, in_=c.token_rows,
                    in_offset=bass.IndirectOffsetOnAxis(ap=now_u[u][:, 0:1], axis=0),
                    bounds_check=NT - 1, oob_is_err=False).then_inc(gathered[v], 16)

            def send(i, w):
                u = w % U
                done(pool, "rows_ready", i, w)
                pool.nop(nofuse=True)
                nc.gpsimd.indirect_dma_start(
                    out=c.expert_rows, out_offset=bass.IndirectOffsetOnAxis(ap=now_u[u][:, 1:2], axis=0),
                    in_=y[u], in_offset=None,
                    bounds_check=2 * NT - 1, oob_is_err=False).then_inc(scattered[u], 16)

            pool.wait_ge(cleared, 1)
            fetch(0, 0)
            fetch(0, 1)
            for u in range(U):
                fetch(0, u + 2)
                send(0, u)
            with pool.Fori(1, JOBS // U - 1) as i:
                for u in range(U):
                    fetch(i, u + 2)
                    send(i, u)
            last = JOBS // U - 1
            for u in range(U):
                if last * U + u + 2 <= JOBS:
                    fetch(last, u + 2)
                send(last, u)
            for u in range(U):
                pool.wait_ge(scattered[u], 16 * JOBS // U)
            pool.wait_ge(gathered[0], 16 * (JOBS // 2 + 1))
            pool.wait_ge(gathered[1], 16 * (JOBS // 2))

        @block.tensor
        def _(pe):
            mm, tr = nc.tensor.matmul, nc.tensor.transpose

            def turn_tokens(i, w):
                v = w % 2
                pe.wait_ge(gathered[v], (i * (U // 2) + (w // 2 + 1)) * 16)
                done(pe, "tokens_ready", i, w, 1)
                for k in range(KT):
                    last = tr(c.bank[2 + k // 4][:, P * (k % 4):P * (k % 4) + P], xg[v][:, P * k:P * k + P], c.ident)
                last.then_inc(sems["tokens_turned"], 1)

            def gate_up(i, w):
                u, v = w % U, w % 2
                pe.wait_ge(up_ready[u], (i + (w // U + 1)) * 32)
                done(pe, "tokens_ready", i, w)
                done(pe, "hidden_ready", i, w, 2)
                for k in range(KT):
                    last = mm(c.bank[v], xt[v][:, k, :], wgu[u][:, k, :], start=(k == 0), stop=(k == KT - 1))
                last.then_inc(sems["gate_up_in_psum"], 1)

            turn_tokens(0, 0)
            gate_up(0, 0)
            with pe.Fori(0, JOBS // U) as i:
                for u in range(U):
                    v = u % 2
                    turn_tokens(i, u + 1)
                    done(pe, "hidden_ready", i, u)
                    done(pe, "hidden_turned_ready", i, u, 1)
                    for f in range(FT):
                        last = tr(c.bank[4][:, P * f:P * f + P], hid[v][:, P * f:P * f + P], c.ident)
                    last.then_inc(sems["hidden_turned"], 1)
                    gate_up(i, u + 1)
                    pe.wait_ge(down_ready[u], i * 16 + 16)
                    done(pe, "hidden_turned_ready", i, u)
                    done(pe, "rows_ready", i, u, 1)
                    for a in range(2):
                        for f in range(FT):
                            last = mm(c.bank[5 + a], ht[v][:, f, :], wd[u][:, f, 512 * a:512 * a + 512],
                                      start=(f == 0), stop=(f == FT - 1))
                    last.then_inc(sems["rows_in_psum"], 1)

        @block.scalar
        def _(act):
            def tokens(i, w):
                v = w % 2
                done(act, "tokens_turned", i, w)
                done(act, "gate_up_in_psum", i, w, 2)
                for a in range(2):
                    nc.scalar.copy(xt[v][:, 4 * a:4 * a + 4, :], c.bank[2 + a].rearrange("p (k t) -> p k t", t=P))
                act.drain().then_inc(sems["tokens_ready"], 1)

            def gate(i, w):
                v = w % 2
                done(act, "gate_up_in_psum", i, w)
                done(act, "hidden_ready", i, w, 2)
                nc.scalar.activation(silu[v], c.bank[v][:, 0:FE], ACT.Silu).then_inc(silu_ready, 1)

            tokens(0, 0)
            gate(0, 0)
            with act.Fori(0, JOBS // U) as i:
                for u in range(U):
                    tokens(i, u + 1)
                    gate(i, u + 1)

        @block.vector
        def _(dve):
            def hidden(i, w):
                v = w % 2
                dve.wait_ge(silu_ready, i * U + (w + 1))
                done(dve, "hidden_turned", i, w, 2)
                nc.vector.tensor_tensor(hid[v], silu[v], c.bank[v][:, FE:2 * FE],
                                        ALU.mult).then_inc(sems["hidden_ready"], 1)

            for v in range(2):
                nc.vector.memset(xg[v], 0.0)
            dve.drain().then_inc(cleared, 1)
            hidden(0, 0)
            with dve.Fori(0, JOBS // U) as i:
                for u in range(U):
                    v = u % 2
                    done(dve, "hidden_turned", i, u)
                    done(dve, "rows_in_psum", i, u, 2)
                    nc.vector.tensor_copy(ht[v], c.bank[4][:, 0:FE].rearrange("p (f t) -> p f t", t=P)).then_inc(
                        sems["hidden_turned_ready"], 1)
                    hidden(i, u + 1)
                    done(dve, "rows_in_psum", i, u)
                    dve.wait_ge(staged, i * U + (u + 1))
                    for a in range(2):
                        nc.vector.tensor_scalar(y[u][:, 512 * a:512 * a + 512], c.bank[5 + a], now[u][:, 2:3], None,
                                                ALU.mult)
                    dve.drain().then_inc(sems["rows_ready"], 1)


def combine(c, layer):
    nc = c.nc
    h, NTILE = c.slot(0), TT + 1
    rows = c.flat(2, 3)[:, 0:NTILE * 2 * D].rearrange("p (n a e) -> p n a e", a=2, e=D)
    with c.stage(f"combine{layer}") as st:
        loaded = [st.sem(f"rows_loaded{n}") for n in range(NTILE)]
        summed, turned, added = st.sem("rows_summed"), st.sem("sums_turned"), st.sem("sums_added")
        block = st.block()

        @block.sync
        def _(sp):
            for n in range(NTILE):
                m = P if n < TT else NB
                two = c.expert_rows[2 * P * n:2 * P * n + 2 * m].rearrange("(p a) e -> p a e", a=2)
                sp.dma_start(rows[0:m, n], two).then_inc(loaded[n], 16)

        @block.tensor
        def _(pe):
            for n in range(NTILE):
                m = P if n < TT else NB
                pe.wait_ge(summed, n + 1)
                if n >= 2:
                    pe.wait_ge(added, 2 * (n - 1))
                for k in range(KT):
                    last = nc.tensor.transpose(c.bank[2 * (n % 2) + k // 4][:, P * (k % 4):P * (k % 4) + m],
                                               rows[0:m, n, 0, P * k:P * k + P], c.ident[0:m, 0:m])
                last.then_inc(turned, 1)

        @block.gpsimd
        def _(pool):
            for n in range(NTILE):
                m = P if n < TT else NB
                pool.wait_ge(loaded[n], 16)
                nc.gpsimd.tensor_tensor(rows[0:m, n, 0, :], rows[0:m, n, 0, :], rows[0:m, n, 1, :],
                                        ALU.add).then_inc(summed, 1)

        @block.vector
        def _(dve):
            for n in range(NTILE):
                m = P if n < TT else NB
                dve.wait_ge(turned, n + 1)
                for a in range(2):
                    o = h[:, 4 * a:4 * a + 4, P * n:P * n + m]
                    src = c.bank[2 * (n % 2) + a].rearrange("p (k t) -> p k t", t=P)[:, :, 0:m]
                    nc.vector.tensor_tensor(o, o, src, ALU.add).then_inc(added, 1)


def mixture(c, layer):
    rms_norm(c, c.slot(0), f"ffn{layer}", c.slot(1), c.slot(3))
    route(c, layer)
    experts(c, layer)
    combine(c, layer)



NSTR = 6
KVW = NSTR * KVH * HD
KVT = KVW // P
RW = KVH * HD


def rotate(c, name, src, dst, tiles):
    nc, io = c.nc, c.io
    cos, sin = c.work[:, 0:NT], c.work[:, NT:2 * NT]
    swap = c.work[:, 2 * NT:2 * NT + P]
    parts = [c.work[:, 1200 + NT * n:1200 + NT * (n + 1)] for n in range(2)]
    halves = lambda a: a.rearrange("p (s t) -> p s t", s=2)
    with c.stage(name) as st:
        loaded, full, taken = st.sem("tables_loaded"), st.sem("partners_in_psum"), st.sem("partners_taken")
        block = st.block()

        @block.sync
        def _(sp):
            for dst_, n in ((cos, "cos"), (sin, "sin"), (swap, "swap")):
                sp.dma_start(dst_, io["consts"][:, CCOL[n][0]:CCOL[n][1]]).then_inc(loaded, 16)

        @block.tensor
        def _(pe):
            pe.wait_ge(loaded, 48)
            for x, m in enumerate(tiles):
                if x >= 4:
                    pe.wait_ge(taken, x - 3)
                for s in range(2):
                    last = nc.tensor.matmul(c.pair[x % 4][:, s, :], swap, src[:, m, HALF * s:HALF * s + HALF],
                                            start=True, stop=True)
                last.then_inc(full, 1)

        @block.vector
        def _(dve):
            dve.wait_ge(loaded, 48)
            for x, m in enumerate(tiles):
                dve.wait_ge(full, x + 1)
                part = parts[x % 2]
                nc.vector.tensor_tensor(halves(part), c.pair[x % 4], halves(sin), ALU.mult).then_inc(taken, 1)
                nc.vector.tensor_tensor(dst[:, m, :], src[:, m, :], cos, ALU.mult)
                dve.drain()
                nc.vector.tensor_tensor(dst[:, m, :], dst[:, m, :], part, ALU.add)


def kv_rows(c):
    nc, io = c.nc, c.io
    kv = c.flat(2, 2)[:, 0:KVT * NT].rearrange("p (k t) -> p k t", t=NT)
    rows = c.flat(4, 2)[:, 0:(TT + 1) * KVW].rearrange("p (n e) -> p n e", e=KVW)
    with c.stage("kv_rows") as st:
        turned, moved, stored = st.sem("rows_in_psum"), st.sem("rows_moved"), st.sem("rows_stored")
        block = st.block()
        jobs = [(n, a) for n in range(TT + 1) for a in range(3)]

        @block.tensor
        def _(pe):
            for x, (n, a) in enumerate(jobs):
                m = P if n < TT else NB
                if x >= 8:
                    pe.wait_ge(moved, x - 7)
                for k in range(4):
                    last = nc.tensor.transpose(c.bank[x % 8][0:m, P * k:P * k + P],
                                               kv[:, 4 * a + k, P * n:P * n + m], c.ident)
                last.then_inc(turned, 1)

        @block.vector
        def _(dve):
            nc.vector.tensor_copy(c.kv_sample, kv[:, :, TP:NT])
            for x, (n, a) in enumerate(jobs):
                m = P if n < TT else NB
                dve.wait_ge(turned, x + 1)
                nc.vector.tensor_copy(rows[0:m, n, 512 * a:512 * a + 512], c.bank[x % 8][0:m, :]).then_inc(moved, 1)

        @block.sync
        def _(sp):
            stores = 0
            sp.dma_start(io["o_sample_win"][:, 0:WIN - 1].rearrange("b t s g d -> b (t s g d)"),
                         io["cache_win"][:, 1:WIN].rearrange("b t s g d -> b (t s g d)")).then_inc(stored, 16)
            stores += 1
            for n in range(TT):
                sp.wait_ge(moved, 3 * (n + 1))
                sp.dma_start(io["o_prompt_rows"][0, P * n:P * n + P].rearrange("t s g d -> t (s g d)"),
                             rows[:, n, 0:4 * RW]).then_inc(stored, 16)
                sp.dma_start(io["o_prompt_win"][0, P * n:P * n + P].rearrange("t s g d -> t (s g d)"),
                             rows[:, n, 4 * RW:KVW]).then_inc(stored, 16)
                stores += 2
            sp.wait_ge(moved, len(jobs))
            sp.dma_start(io["o_sample_rows"][:, 0].rearrange("b s g d -> b (s g d)"),
                         rows[0:NB, TT, 0:4 * RW]).then_inc(stored, 16)
            sp.dma_start(io["o_sample_win"][:, WIN - 1].rearrange("b s g d -> b (s g d)"),
                         rows[0:NB, TT, 4 * RW:KVW]).then_inc(stored, 16)
            for a, stream in ((0, 2), (1, 4)):
                for q in range(2):
                    sp.dma_start(c.prompt_keys[0:HD, a, q:KVH:2, :],
                                 kv[HD * q:HD * q + HD, 2 * stream:2 * stream + 2, 0:TP]).then_inc(stored, 16)
            sp.wait_ge(stored, 16 * (stores + 2 + 4))


def load_compression(c, st, sp, w1, w2, pe_rows, b1, done):
    io = c.io
    for kv in range(2):
        sp.dma_start(w1[:, kv], io["cmp_w1"][kv].rearrange("(j p) n -> p j n", p=P)).then_inc(done, 16)
        sp.dma_start(w2[:, kv, :], io["cmp_w2"][kv]).then_inc(done, 16)
        sp.dma_start(pe_rows[:, kv, :], io["cmp_pe"][kv].rearrange("(j a) d -> j (a d)", a=2)).then_inc(done, 16)
        sp.dma_start(b1[:, kv:kv + 1], io["cmp_b1"][kv].rearrange("(c a) -> c a", a=1)).then_inc(done, 16)
    return 16 * 8


def by_parity(copy, dst, src, done):
    for q in range(2):
        for par in range(2):
            s = src[HD * q:HD * q + HD].rearrange("p v (n j a) -> p v j n a", j=8, a=2)[:, :, :, :, par]
            copy(dst[HD * par:HD * par + HD, q:2 * KVH:2, :, :], s).then_inc(done, 1)


def compress_prompt(c):
    nc, io = c.nc, c.io
    w1 = c.flat(6)[:, 0:4096].rearrange("p (a j n) -> p a j n", a=2, j=16)
    w2 = c.work[:, 0:2 * HD].rearrange("p (a d) -> p a d", a=2)
    pe_rows = c.work[0:16, 128:384].rearrange("p (a d) -> p a d", a=2)
    b1, pe_cols = c.work[:, 384:386], c.work[:, 386:418].rearrange("p (a j) -> p a j", a=2)
    kv_t = c.flat(2, 2)[:, 0:KVT * NT].rearrange("p (k t) -> p k t", t=NT)
    NS = TP // SUB
    XT = c.work[:, 2560:2560 + 2048].rearrange("p (v x n) -> p v x n", v=2 * KVH, x=8)
    XV = [c.work[:, 2560 + 1024 * v:2560 + 1024 * (v + 1)].rearrange("p (g j n) -> p g j n", g=KVH, j=8)
          for v in range(2)]
    G = [c.work[:, 4608 + 128 * v:4608 + 128 * v + KVH * NCMP_P].rearrange("p (g n) -> p g n", g=KVH)
         for v in range(2)]
    with c.stage("compress_prompt") as st:
        loaded, pe_in, pe_out, bias_in, bias_out = (st.sem(n) for n in (
            "weights_loaded", "encoding_turned", "encoding_moved", "bias_in_psum", "bias_ready"))
        moved, hid_in, hid_out, out_in = (st.sem(n) for n in (
            "pairs_moved", "hidden_in_psum", "hidden_ready", "outputs_in_psum"))
        block = st.block()

        @block.sync
        def _(sp):
            load_compression(c, st, sp, w1, w2, pe_rows, b1, loaded)

        @block.tensor
        def _(pe):
            pe.wait_ge(loaded, 16 * 8)
            for v in range(2):
                last = nc.tensor.transpose(c.bank[0][:, 16 * v:16 * v + 16], pe_rows[:, v, :], c.ident[0:16, 0:16])
            last.then_inc(pe_in, 1)
            pe.wait_ge(pe_out, 1)
            for v in range(2):
                for j in range(16):
                    last = nc.tensor.matmul(c.bank[5][:, v:v + 1], w1[:, v, j, :], pe_cols[:, v, j:j + 1],
                                            start=(j == 0), stop=(j == 15))
            last.then_inc(bias_in, 1)
            pe.wait_ge(moved, 4)
            for v in range(2):
                for j in range(16):
                    first = j // 8
                    last = nc.tensor.matmul(c.bank[6 + v][:, 0:KVH * NCMP_P], w1[:, v, j, :],
                                            XV[v][:, :, j % 8, first:first + NCMP_P], start=(j == 0), stop=(j == 15))
            last.then_inc(hid_in, 1)
            pe.wait_ge(hid_out, 2)
            nc.tensor.matmul(c.bank[0][0:HD, 0:KVH * NCMP_P], w2[:, 0, :], G[0], start=True, stop=True)
            for g in range(KVH):
                last = nc.tensor.matmul(c.bank[1][0:NCMP_P, HD * g:HD * g + HD], G[1][:, g, :], w2[:, 1, :],
                                        start=True, stop=True)
            last.then_inc(out_in, 1)

        @block.vector
        def _(dve):
            nc.vector.memset(c.cmp_keys, 0.0)
            nc.vector.memset(c.cmp_values, 0.0)
            dve.drain()
            dve.wait_ge(pe_in, 1)
            nc.vector.tensor_copy(pe_cols, c.bank[0][:, 0:32].rearrange("p (a j) -> p a j", a=2)).then_inc(pe_out, 1)
            by_parity(nc.vector.tensor_copy, XT, kv_t[:, 0:4, 0:TP], moved)
            dve.wait_ge(bias_in, 1)
            nc.vector.tensor_tensor(c.cmp_bias, c.bank[5][:, 0:2], b1, ALU.add).then_inc(bias_out, 1)
            dve.wait_ge(out_in, 1)
            nc.vector.tensor_copy(c.cmp_keys[0:HD], c.bank[0][0:HD, 0:KVH * NCMP_P].rearrange("p (g n) -> p g n", g=KVH))
            nc.vector.tensor_copy(c.cmp_values[0:NCMP_P, :], c.bank[1][0:NCMP_P, 0:RW])

        @block.scalar
        def _(act):
            act.wait_ge(hid_in, 1)
            act.wait_ge(bias_out, 1)
            for v in range(2):
                nc.scalar.activation(G[v], c.bank[6 + v][:, 0:KVH * NCMP_P].rearrange("p (g n) -> p g n", g=KVH),
                                     ACT.Gelu_apprx_tanh, bias=c.cmp_bias[:, v:v + 1]).then_inc(hid_out, 1)



def gates(c):
    nc, io = c.nc, c.io
    x, NGATE = c.slot(1), 3 * NH
    w = c.work[:, 0:KT * NGATE].rearrange("p (k n) -> p k n", n=NGATE)
    with c.stage("gates") as st:
        loaded, full, ready, stored = (st.sem(n) for n in ("weight_loaded", "gates_in_psum", "gates_ready", "stored"))
        cleared = st.sem("rows_cleared")
        block = st.block()

        @block.gpsimd
        def _(pool):
            nc.gpsimd.memset(c.gate, 0.0).then_inc(cleared, 1)

        @block.sync
        def _(sp):
            sp.dma_start(w, io["nsa_wqg"][0][:, D:D + NGATE].rearrange("(k p) n -> p k n", p=P)).then_inc(loaded, 16)
            sp.wait_ge(ready, 1)
            sp.dma_start(c.gate_rows, c.gate[0:NB, TT, :]).then_inc(stored, 16)
            sp.wait_ge(stored, 16)

        @block.tensor
        def _(pe):
            pe.wait_ge(loaded, 16)
            for n in range(TT + 1):
                m = P if n < TT else NB
                for k in range(KT):
                    last = nc.tensor.matmul(c.bank[0][0:m, NGATE * n:NGATE * n + NGATE], x[:, k, P * n:P * n + m],
                                            w[:, k, :], start=(k == 0), stop=(k == KT - 1))
            last.then_inc(full, 1)

        @block.scalar
        def _(act):
            act.wait_ge(cleared, 1)
            act.wait_ge(full, 1)
            nc.scalar.activation(c.gate[:, 0:TT, :], c.bank[0][:, 0:TT * NGATE].rearrange("p (a b) -> p a b", b=NGATE),
                                 ACT.Sigmoid)
            nc.scalar.activation(c.gate[0:NB, TT, :], c.bank[0][0:NB, TT * NGATE:(TT + 1) * NGATE], ACT.Sigmoid)
            act.drain().then_inc(ready, 1)


def prompt_attention(c):
    nc, io = c.nc, c.io
    q_plain, q_rot = c.slot(6), c.slot(7)
    rows = c.flat(4, 2)[:, 0:(TT + 1) * KVW].rearrange("p (n e) -> p n e", e=KVW)
    out = c.flat(1)[:, 0:TT * D].rearrange("p (n e) -> p n e", e=D)
    lo, hi = CCOL["cmpneg"][0], CCOL["cmpone"][1]
    NK = NCMP_P
    work, at = c.work, [0]

    def area(n):
        at[0] += n
        return work[:, at[0] - n:at[0]]

    masks, causal = area(hi - lo), area(P)
    neg, one = (masks[:, x * TT * NK:(x + 1) * TT * NK].rearrange("p (n k) -> p n k", k=NK) for x in range(2))
    queries = [area(4 * TP).rearrange("p (r t) -> p r t", t=TP)[0:HD] for _ in range(2)]
    prob = [area(TP) for _ in range(3)]
    turned_sb = [area(TP) for _ in range(3)]
    top, total, coef = area(64), area(64), area(64)
    CMP, SEL, WINB = range(3)
    jobs = [(r, b, n) for r in range(4) for n in range(TT) for b in (SEL, WINB, CMP)]
    NJ = len(jobs)
    width = lambda b, n: NK if b == CMP else P * (n + 1)
    STREAM = {SEL: 3, WINB: 5}
    with c.stage("prompt_attention") as st:
        loaded, q_ready = st.sem("tables_loaded"), st.sem("queries_ready")
        topped, score_free = st.sem("maximum_ready"), st.sem("scores_used")
        scored, expd, p_in, p_out, mixed, added = (st.sem(n, 1) for n in (
            "scores_in_psum", "probabilities_ready", "turned_in_psum", "turned_ready", "output_in_psum",
            "output_added"))
        block = st.block()
        S = [c.bank[x] for x in range(3)]
        Tb = [c.bank[3], c.bank[4]]
        O = [c.bank[5], c.bank[6]]

        @block.sync
        def _(sp):
            sp.dma_start(masks, io["consts"][:, lo:hi]).then_inc(loaded, 16)
            sp.dma_start(causal, io["consts"][:, CCOL["causal"][0]:CCOL["causal"][1]]).then_inc(loaded, 16)

        @block.gpsimd
        def _(pool):
            with pool.Fori(0, KVH) as i:
                pool.wait_ge(scored, i * NJ + 1)
                for dst, src in zip(queries, (q_plain, q_rot)):
                    for odd in range(2):
                        nc.gpsimd.tensor_copy(dst[:, odd:4:2, :],
                                              src[HD * odd:HD * odd + HD, ds(i * 2, 2), 0:TP]).then_inc(q_ready, 1)

        @block.tensor
        def _(pe):
            with pe.Fori(0, KVH) as i:
                pe.wait_ge(q_ready, i * 4 + 4)
                for x in range(NJ + 3):
                    if x < NJ:
                        r, b, n = jobs[x]
                        q = queries[0 if b == CMP else 1][:, r, P * n:P * n + P]
                        keys = (c.cmp_keys[0:HD, ds(i, 1), :] if b == CMP else
                                c.prompt_keys[0:HD, b - 1, ds(i, 1), 0:P * (n + 1)])
                        pe.wait_ge(expd, i * NJ + max(0, x - 2) + 1)
                        pe.nop(nofuse=True)
                        nc.tensor.matmul(S[x % 3][:, 0:width(b, n)], q, keys.rearrange("p a t -> p (a t)"),
                                         start=True, stop=True).then_inc(scored, 1)
                    if 2 <= x < NJ + 2:
                        y = x - 2
                        r, b, n = jobs[y]
                        pe.wait_ge(expd, i * NJ + y + 2)
                        pe.wait_ge(p_out, i * NJ + max(0, y - 1) + 1)
                        if b == CMP:
                            last = nc.tensor.transpose(Tb[y % 2][0:NK, 0:P], prob[y % 3][:, 0:NK], c.ident)
                        else:
                            for s in range(n + 1):
                                last = nc.tensor.transpose(Tb[y % 2][:, P * s:P * s + P],
                                                           prob[y % 3][:, P * s:P * s + P], c.ident)
                        last.then_inc(p_in, 1)
                    if x >= 3:
                        y = x - 3
                        r, b, n = jobs[y]
                        pe.wait_ge(p_out, i * NJ + y + 2)
                        pe.wait_ge(added, i * NJ + max(0, y - 1) + 1)
                        pe.nop(nofuse=True)
                        if b == CMP:
                            last = nc.tensor.matmul(O[y % 2][:, 0:HD], turned_sb[y % 3][0:NK, 0:P],
                                                    c.cmp_values[0:NK, ds(i * HD, HD)], start=True, stop=True)
                        else:
                            for s in range(n + 1):
                                v = rows[:, s, ds(i * HD + STREAM[b] * RW, HD)]
                                last = nc.tensor.matmul(O[y % 2][:, 0:HD], turned_sb[y % 3][:, P * s:P * s + P], v,
                                                        start=(s == 0), stop=(s == n))
                        last.then_inc(mixed, 1)

        @block.scalar
        def _(act):
            with act.Fori(0, KVH) as i:
                for x in range(NJ + 1):
                    if x < NJ:
                        r, b, n = jobs[x]
                        w = width(b, n)
                        act.wait_ge(topped, i * NJ + x + 1)
                        act.wait_ge(p_in, i * NJ + max(0, x - 2) + 1)
                        nc.scalar.activation(prob[x % 3][:, 0:w], S[x % 3][:, 0:w], ACT.Exp, bias=top[:, x:x + 1],
                                             scale=SCALE, accum_out=total[:, x:x + 1])
                        act.drain().then_inc(expd if b != CMP else score_free, 1)
                    if x >= 1:
                        y = x - 1
                        r, b, n = jobs[y]
                        rows_, w = (NK, P) if b == CMP else (P, P * (n + 1))
                        act.wait_ge(p_in, i * NJ + y + 2)
                        act.wait_ge(mixed, i * NJ + max(0, y - 2) + 1)
                        nc.scalar.copy(turned_sb[y % 3][0:rows_, 0:w], Tb[y % 2][0:rows_, 0:w]).then_inc(p_out, 1)

        @block.vector
        def _(dve):
            nc.vector.memset(out, 0.0)
            dve.wait_ge(loaded, 32)
            with dve.Fori(0, KVH) as i:
                ncmp = 0
                for x in range(NJ + 3):
                    if x < NJ:
                        r, b, n = jobs[x]
                        w = width(b, n)
                        dve.wait_ge(scored, i * NJ + x + 2)
                        part, mask = ((S[x % 3][:, 0:NK], neg[:, n, :]) if b == CMP
                                      else (S[x % 3][:, P * n:P * n + P], causal))
                        nc.vector.tensor_tensor(part, part, mask, ALU.add)
                        dve.drain()
                        nc.vector.tensor_reduce(top[:, x:x + 1], S[x % 3][:, 0:w], AX.X, ALU.max)
                        dve.drain()
                        nc.vector.tensor_scalar(top[:, x:x + 1], top[:, x:x + 1], -SCALE, None, ALU.mult)
                        dve.drain().then_inc(topped, 1)
                        if b == CMP:
                            ncmp += 1
                            dve.wait_ge(score_free, i * (NJ // 3) + ncmp)
                            nc.vector.tensor_tensor(prob[x % 3][:, 0:NK], prob[x % 3][:, 0:NK], one[:, n, :], ALU.mult)
                            dve.drain()
                            nc.vector.tensor_reduce(total[:, x:x + 1], prob[x % 3][:, 0:NK], AX.X, ALU.add)
                            dve.drain()
                            nc.vector.tensor_scalar(total[:, x:x + 1], total[:, x:x + 1], 1e-30, None, ALU.max)
                            dve.drain().then_inc(expd, 1)
                    if x >= 3:
                        y = x - 3
                        r, b, n = jobs[y]
                        cf = coef[:, y:y + 1]
                        nc.vector.reciprocal(cf, total[:, y:y + 1])
                        dve.drain()
                        nc.vector.tensor_tensor(cf, cf, c.gate[:, n, ds(i * 12 + (3 * r + b), 1)], ALU.mult)
                        dve.drain()
                        dve.wait_ge(mixed, i * NJ + y + 2)
                        o = out[:, n, ds(i * (4 * HD) + r * HD, HD)]
                        nc.vector.scalar_tensor_tensor(o, O[y % 2][:, 0:HD], cf, o, ALU.mult, ALU.add)
                        dve.drain().then_inc(added, 1)

    with c.stage("prompt_mixed") as st:
        turned, moved = st.sem("columns_in_psum"), st.sem("columns_moved")
        block = st.block()

        @block.tensor
        def _(pe):
            for k in range(KT):
                for n in range(TT):
                    last = nc.tensor.transpose(c.bank[k][:, P * n:P * n + P], out[:, n, P * k:P * k + P], c.ident)
                last.then_inc(turned, 1)

        @block.vector
        def _(dve):
            for k in range(KT):
                dve.wait_ge(turned, k + 1)
                nc.vector.tensor_copy(c.slot(9)[:, k, 0:TP], c.bank[k])


def sample_prepare(c):
    nc, io = c.nc, c.io
    rows = c.slot(1)[0:NB, :, :].rearrange("b k t -> b (k t)")[:, 0:2 * D].rearrange("b (a e) -> b a e", a=2)
    s = c.sample
    pages_i = c.flat(8)[:, 0:NB * NPG].bitcast(I32)
    pages_f = c.flat(8)[:, 128:128 + NB * NPG]
    tok = c.flat(8)[:, 256:257]
    with c.stage("sample_prepare") as st:
        loaded, turned, moved, stored = (st.sem(n) for n in ("loaded", "queries_turned", "queries_moved", "stored"))
        weights = st.sem("weights_loaded")
        block = st.block()

        @block.sync
        def _(sp):
            table = io["page_table"].rearrange("(a b) p -> a (b p)", a=1).to_broadcast([P, NB * NPG])
            sp.dma_start(pages_i, table).then_inc(loaded, 16)
            sp.dma_start(tok, io["consts"][:, CCOL["tokrow"][0]:CCOL["tokrow"][1]], allow_slow_non_contiguous=True).then_inc(loaded, 16)
            sp.wait_ge(turned, 1)
            n = load_compression(c, st, sp, s["w1"], s["w2"], c.flat(8)[0:16, 300:556].rearrange("p (a d) -> p a d", a=2),
                                 c.flat(8)[:, 556:558], weights)
            for name in ("overlap", "samegroup", "notforced", "forced", "earlier", "ownkv", "ownquery"):
                sp.dma_start(s[name], io["consts"][0:s[name].shape[0], CCOL[name][0]:CCOL[name][1]]).then_inc(weights, 16)
                n += 16
            sp.dma_start(s["gate"], c.gate_rows.rearrange("b (h r) -> h b r", r=3)).then_inc(weights, 16)
            sp.wait_ge(weights, n + 16)
            sp.wait_ge(moved, 4)
            sp.dma_start(c.query_rows.rearrange("a b e -> b a e"), rows).then_inc(stored, 16)
            sp.wait_ge(stored, 16)

        @block.tensor
        def _(pe):
            for a in range(2):
                for k in range(KT):
                    last = nc.tensor.transpose(c.bank[2 * a + k // 4][0:NB, P * (k % 4):P * (k % 4) + P],
                                               c.slot(6 + a)[:, k, TP:NT], c.ident)
            last.then_inc(turned, 1)

        @block.vector
        def _(dve):
            dve.wait_ge(loaded, 32)
            nc.vector.tensor_copy(pages_f, pages_i)
            dve.drain()
            nc.vector.tensor_scalar(pages_f, pages_f, float(2 * PAGE), tok, ALU.mult, ALU.add)
            dve.drain()
            nc.vector.tensor_copy(s["index"][:, 1, :], pages_f)
            nc.vector.tensor_scalar(pages_f, pages_f, -1.0, None, ALU.add)
            dve.drain()
            nc.vector.tensor_copy(s["index"][:, 0, :], pages_f)
            dve.wait_ge(turned, 1)
            for a in range(2):
                for k in range(2):
                    nc.vector.tensor_copy(rows[:, a, 512 * k:512 * k + 512], c.bank[2 * a + k][0:NB, :]).then_inc(moved, 1)


def sample_memory(c):
    f, w, at = c.flat, c.work, [0]

    def area(n, rows=P):
        at[0] += n
        assert at[0] <= 8320
        return w[0:rows, at[0] - n:at[0]]

    NSC = NCMP_S + PAST + 1 + WIN
    c.sample = {
        "sel": f(1, 2)[:, 0:NPG * 512].rearrange("p (n e) -> p n e", e=512),
        "xt": f(3, 2)[:, 0:8192].rearrange("p (v j n) -> p v j n", v=2 * KVH, j=8),
        "kt": f(5)[:, 0:2 * PAST].rearrange("p (g t) -> p g t", g=2),
        "w1": f(6)[:, 0:4096].rearrange("p (a j n) -> p a j n", a=2, j=16),
        "cmp": f(7)[:, 0:2048].rearrange("p (n e) -> p n e", e=512),
        "win": f(7)[:, 2048:4096].rearrange("p (n e) -> p n e", e=512),
        "kwt": f(8)[:, 0:1024].rearrange("p (g t) -> p g t", g=2),
        "score": f(8)[0:NH, 1024:1024 + NSC],
        "w2": area(2 * HD).rearrange("p (a d) -> p a d", a=2),
        "index": area(2 * NB * NPG).rearrange("p (a n) -> p a n", a=2).bitcast(U32),
        "now": area(2 * NPG).rearrange("p (a n) -> p a n", a=2).bitcast(U32),
        "hidden": area(2 * KVH * NCMP_S).rearrange("p (a g n) -> p a g n", a=2, g=KVH),
        "kc": area(2 * NCMP_S).rearrange("p (g n) -> p g n", g=2),
        "vc": area(RW, NCMP_S),
        "overlap": area(NSB, NCMP_S), "samegroup": area(NH, NH), "notforced": area(NSB, NH), "forced": area(NSB, NH),
        "earlier": area(NSB * NSB, NH), "ownkv": area(RW, NH), "ownquery": area(2 * NH),
        "gate": area(3 * NB, NH).rearrange("p (b r) -> p b r", r=3),
        "qrow": area(4 * HD, NH).rearrange("p (a x d) -> p a x d", a=2, x=2),
        "vnew": area(RW, 1),
        "rank": area(NSB * NSB, NH), "tie": area(NSB * NSB, NH),
        "imp": area(NSB, NH), "pick": area(NSB, NH),
        "pct": area(NH, NCMP_S), "pt": area((NPG + 1) * NH), "wt": area(4 * NH),
        "acc": area(RW, NH), "head": area(HD, NH), "col": area(16, NH),
    }


def sample_attention(c):
    nc, io = c.nc, c.io
    s = c.sample
    cache = io["cache_kv"].rearrange("n t (a s) g d -> (n t a) (s g d)", a=2)
    sc_cmp, sc_sel = s["score"][:, 0:NCMP_S], s["score"][:, NCMP_S:NCMP_S + PAST + 1]
    sc_win = s["score"][:, NCMP_S + PAST + 1:]
    col = lambda n: s["col"][:, n:n + 1]
    out_rows = nc.dram_tensor("sample_attended", [NB, D], F32).ap()
    CAP = 4
    RING = NPG + NPG // 2 + 2
    with c.stage("sample_attention") as st:
        cmp_in = [st.sem(f"cmp_page_loaded{n}") for n in range(CAP)]
        sel_in = [st.sem(f"sel_pages_loaded{n}") for n in range(4)]
        win_in, row_in, stored = st.sem("window_loaded"), st.sem("query_rows_loaded"), st.sem("head_rows_stored", 16)
        turned = [st.sem(f"tile_turned{n}", 1) for n in range(2)]
        taken = [st.sem(f"tile_taken{n}", 1) for n in range(2)]
        ev = {n: st.sem(n, 1) for n in (
            "hidden_in_psum", "hidden_ready", "compressed_in_psum", "compressed_ready",
            "queries_in_psum", "queries_ready", "small_scores_in_psum", "small_scores_ready", "sel_scores_in_psum",
            "maxima_ready", "exp_ready", "cmp_prob_ready", "cmp_turned_in_psum", "cmp_turned_ready",
            "importance_in_psum", "importance_ready", "group_importance_in_psum", "sel_maximum_ready",
            "sel_exp_ready", "turned_in_psum", "turned_ready", "output_in_psum", "head_ready")}
        block = st.block()

        def now(eng, i, *names):
            for n in names:
                eng.wait_ge(ev[n], i + 2)

        def before(eng, i, *names):
            for n in names:
                eng.wait_ge(ev[n], i + 1)

        @block.gpsimd
        def _(pool):
            def gather(dst, a, p, done):
                pool.nop(nofuse=True)
                nc.gpsimd.indirect_dma_start(
                    out=dst, out_offset=None, in_=cache,
                    in_offset=bass.IndirectOffsetOnAxis(ap=s["now"][:, a, p:p + 1], axis=0),
                    bounds_check=NPHYS * PAGE * 2 - 1, oob_is_err=True).then_inc(done, 16)

            with pool.Fori(0, NB) as i:
                before(pool, i, "sel_scores_in_psum")
                nc.gpsimd.tensor_copy(s["now"], s["index"][:, :, ds(i * NPG, NPG)])
                pool.drain()
                for p in range(NPG):
                    if p >= CAP:
                        pool.wait_ge(turned[p % 2], i * (RING // 2) + (p - CAP) // 2 + 2)
                    else:
                        pool.wait_ge(turned[p % 2], i * (RING // 2) + 1)
                    gather(s["cmp"][:, p % CAP, :], 0, p, cmp_in[p % CAP])
                    if p == 0:
                        before(pool, i, "output_in_psum")
                    gather(s["sel"][:, p, :], 1, p, sel_in[p // 4])

        @block.sync
        def _(sp):
            with sp.Fori(0, NB) as i:
                before(sp, i, "output_in_psum")
                window = io["o_sample_win"][ds(i, 1)].rearrange("b (n p) s g d -> p (b n) (s g d)", p=P)
                sp.dma_start(s["win"], window).then_inc(win_in, 16)
                sp.dma_start(s["vnew"], io["o_sample_rows"][ds(i, 1), 0, 3].rearrange("b g d -> b (g d)")).then_inc(win_in, 16)
                for x in range(2):
                    q = c.query_rows[:, ds(i, 1), :].rearrange("a b (h d) -> h (a b) d", d=HD)
                    sp.dma_start(s["qrow"][:, :, x, :], q).then_inc(row_in, 16)
                now(sp, i, "head_ready")
                sp.dma_start(out_rows[ds(i, 1), :].rearrange("b (h d) -> (b h) d", d=HD), s["head"]).then_inc(stored, 16)
            sp.wait_ge(stored, 16 * NB + 16)

        @block.tensor
        def _(pe):
            mm, tr = nc.tensor.matmul, nc.tensor.transpose

            def tile(i, x, sources):
                pe.wait_ge(taken[x % 2], i * (RING // 2) + x // 2 + 1)
                for at, src in sources:
                    last = tr(c.bank[x % 2][:, at:at + P], src, c.ident)
                last.then_inc(turned[x % 2], 1)

            with pe.Fori(0, NB) as i:
                for p in range(NPG):
                    pe.wait_ge(cmp_in[p % CAP], i * (16 * NPG // CAP) + 16 * (p // CAP + 1))
                    tile(i, p, [(P * v, s["cmp"][:, p % CAP, P * v:P * v + P]) for v in range(4)])
                for n in range(2):
                    pe.wait_ge(taken[n], i * (RING // 2) + NPG // 2 + 1)
                for v in range(2):
                    for j in range(16):
                        first = j // 8
                        last = mm(c.bank[2 + v][:, 0:KVH * NCMP_S], s["w1"][:, v, j, :],
                                  s["xt"][:, KVH * v:KVH * v + KVH, j % 8, first:first + NCMP_S],
                                  start=(j == 0), stop=(j == 15))
                last.then_inc(ev["hidden_in_psum"], 1)
                pe.wait_ge(row_in, i * 32 + 32)
                pe.nop(nofuse=True)
                for a in range(2):
                    last = tr(c.bank[4][:, NH * a:NH * a + NH], s["qrow"][:, a].rearrange("h x d -> h (x d)"),
                              c.ident[0:NH, 0:NH])
                last.then_inc(ev["queries_in_psum"], 1)
                for x in range(NPG // 2):
                    pe.wait_ge(sel_in[x // 2], i * (16 * NPG // 4) + 64)
                    tile(i, NPG + x, [(2 * P * g + P * y, s["sel"][:, 2 * x + y, P * g:P * g + P])
                                      for g in range(2) for y in range(2)])
                pe.wait_ge(win_in, i * 32 + 32)
                for g in range(2):
                    tile(i, NPG + NPG // 2 + g, [(P * y, s["win"][:, y, P * g:P * g + P]) for y in range(4)])
                now(pe, i, "hidden_ready")
                for q in range(2):
                    mm(c.bank[2][HD * q:HD * q + HD, 0:2 * NCMP_S], s["w2"][:, 0, :], s["hidden"][:, 0, q:KVH:2, :],
                       start=True, stop=True)
                for g in range(KVH):
                    last = mm(c.bank[3][0:NCMP_S, HD * g:HD * g + HD], s["hidden"][:, 1, g, :], s["w2"][:, 1, :],
                              start=True, stop=True)
                last.then_inc(ev["compressed_in_psum"], 1)
                for n in range(2):
                    pe.wait_ge(taken[n], i * (RING // 2) + RING // 2 + 1)
                now(pe, i, "compressed_ready", "queries_ready")
                Q = c.queries
                for g in range(2):
                    mm(c.bank[2][0:NH, 0:NCMP_S], Q[:, 0, g, :], s["kc"][:, g, :], start=(g == 0), stop=(g == 1))
                for g in range(2):
                    mm(c.bank[2][0:NH, 128:129], Q[:, 1, g, :], c.kv_sample[:, 4 + g, ds(i, 1)],
                       start=(g == 0), stop=(g == 1))
                for g in range(2):
                    last = mm(c.bank[3][0:NH, :], Q[:, 1, g, :], s["kwt"][:, g, :], start=(g == 0), stop=(g == 1))
                last.then_inc(ev["small_scores_in_psum"], 1)
                before(pe, i, "head_ready")
                for x in range(4):
                    for g in range(2):
                        last = mm(c.bank[4 + x][0:NH, :], Q[:, 1, g, :], s["kt"][:, g, 512 * x:512 * x + 512],
                                  start=(g == 0), stop=(g == 1))
                last.then_inc(ev["sel_scores_in_psum"], 1)
                now(pe, i, "cmp_prob_ready", "small_scores_ready")
                pe.nop(nofuse=True)
                tr(c.bank[2][0:NCMP_S, 0:NH], sc_cmp, c.ident[0:NH, 0:NH]).then_inc(ev["cmp_turned_in_psum"], 1)
                now(pe, i, "cmp_turned_ready")
                mm(c.bank[3][0:NH, 0:NSB], s["pct"], s["overlap"], start=True,
                   stop=True).then_inc(ev["importance_in_psum"], 1)
                now(pe, i, "importance_ready")
                pe.nop(nofuse=True)
                mm(c.bank[2][0:NH, 0:NSB], s["samegroup"], s["imp"], start=True,
                   stop=True).then_inc(ev["group_importance_in_psum"], 1)
                now(pe, i, "sel_exp_ready", "exp_ready")
                pe.nop(nofuse=True)
                for p in range(NPG):
                    tr(c.bank[4][:, NH * p:NH * p + NH], sc_sel[:, P * p:P * p + P], c.ident[0:NH, 0:NH])
                tr(c.bank[4][0:1, NH * NPG:NH * NPG + NH], sc_sel[:, PAST:PAST + 1], c.ident[0:NH, 0:NH])
                for y in range(4):
                    last = tr(c.bank[5][:, NH * y:NH * y + NH], sc_win[:, P * y:P * y + P], c.ident[0:NH, 0:NH])
                last.then_inc(ev["turned_in_psum"], 1)
                now(pe, i, "turned_ready")
                for p in range(NPG):
                    mm(c.bank[6][0:NH, 0:RW], s["pt"][:, NH * p:NH * p + NH], s["sel"][:, p, RW:2 * RW],
                       start=(p == 0), stop=False)
                mm(c.bank[6][0:NH, 0:RW], s["pt"][0:1, NH * NPG:NH * NPG + NH], s["vnew"], start=False, stop=True)
                for y in range(4):
                    mm(c.bank[6][0:NH, RW:2 * RW], s["wt"][:, NH * y:NH * y + NH], s["win"][:, y, RW:2 * RW],
                       start=(y == 0), stop=(y == 3))
                mm(c.bank[7][0:NH, 0:RW], s["pct"], s["vc"], start=True, stop=True).then_inc(ev["output_in_psum"], 1)

        def take_tile(eng, copy, i, x):
            b = x % 2
            eng.wait_ge(turned[b], i * (RING // 2) + x // 2 + 2)
            bank = c.bank[b]
            if x < NPG:
                src = bank.rearrange("p (v t) -> p v t", v=4)
                for q in range(2):
                    for par in range(2):
                        half = src[HD * q:HD * q + HD].rearrange("p v (n j a) -> p v j n a", j=8, a=2)[:, :, :, :, par]
                        last = copy(s["xt"][HD * par:HD * par + HD, q:2 * KVH:2, :, 8 * x:8 * x + 8], half)
            elif x < NPG + NPG // 2:
                y = x - NPG
                last = copy(s["kt"][:, :, 2 * P * y:2 * P * y + 2 * P], bank.rearrange("p (g t) -> p g t", g=2))
            else:
                last = copy(s["kwt"][:, x - NPG - NPG // 2, :], bank)
            eng.drain().then_inc(taken[b], 1)

        @block.scalar
        def _(act):
            with act.Fori(0, NB) as i:
                for x in range(1, NPG, 2):
                    take_tile(act, nc.scalar.copy, i, x)
                now(act, i, "hidden_in_psum")
                for v in range(2):
                    nc.scalar.activation(s["hidden"][:, v],
                                         c.bank[2 + v][:, 0:KVH * NCMP_S].rearrange("p (g n) -> p g n", g=KVH),
                                         ACT.Gelu_apprx_tanh, bias=c.cmp_bias[:, v:v + 1])
                act.drain().then_inc(ev["hidden_ready"], 1)
                for x in range(NPG + 1, RING, 2):
                    take_tile(act, nc.scalar.copy, i, x)
                now(act, i, "small_scores_in_psum")
                nc.scalar.copy(sc_cmp, c.bank[2][0:NH, 0:NCMP_S])
                nc.scalar.copy(sc_sel[:, PAST:PAST + 1], c.bank[2][0:NH, 128:129])
                nc.scalar.copy(sc_win, c.bank[3][0:NH, :])
                act.drain().then_inc(ev["small_scores_ready"], 1)
                now(act, i, "maxima_ready")
                nc.scalar.activation(sc_cmp, sc_cmp, ACT.Exp, bias=col(0), scale=SCALE, accum_out=col(1))
                nc.scalar.activation(sc_win, sc_win, ACT.Exp, bias=col(2), scale=SCALE, accum_out=col(3))
                act.drain().then_inc(ev["exp_ready"], 1)
                now(act, i, "sel_maximum_ready")
                nc.scalar.activation(sc_sel, sc_sel, ACT.Exp, bias=col(4), scale=SCALE, accum_out=col(5))
                act.drain().then_inc(ev["sel_exp_ready"], 1)

        @block.vector
        def _(dve):
            tt, ts, copy = nc.vector.tensor_tensor, nc.vector.tensor_scalar, nc.vector.tensor_copy
            reduce = nc.vector.tensor_reduce

            def scaled_maximum(dst, scores):
                reduce(dst, scores, AX.X, ALU.max)
                dve.drain()
                ts(dst, dst, -SCALE, None, ALU.mult)

            with dve.Fori(0, NB) as i:
                for x in range(0, NPG, 2):
                    take_tile(dve, copy, i, x)
                now(dve, i, "queries_in_psum")
                for a in range(2):
                    src = c.bank[4][:, NH * a:NH * a + NH].unsqueeze(1).to_broadcast([P, 2, NH])
                    tt(c.queries[:, a], src, s["ownquery"].rearrange("p (g h) -> p g h", g=2), ALU.mult)
                dve.drain().then_inc(ev["queries_ready"], 1)
                for x in range(NPG, RING, 2):
                    take_tile(dve, copy, i, x)
                now(dve, i, "compressed_in_psum")
                copy(s["kc"], c.bank[2][:, 0:2 * NCMP_S].rearrange("p (g n) -> p g n", g=2))
                copy(s["vc"], c.bank[3][0:NCMP_S, 0:RW])
                dve.drain().then_inc(ev["compressed_ready"], 1)
                now(dve, i, "small_scores_ready")
                scaled_maximum(col(0), sc_cmp)
                scaled_maximum(col(2), sc_win)
                dve.drain().then_inc(ev["maxima_ready"], 1)
                now(dve, i, "exp_ready")
                ts(col(1), col(1), 1e-30, None, ALU.max)
                dve.drain()
                nc.vector.reciprocal(col(1), col(1))
                nc.vector.reciprocal(col(3), col(3))
                dve.drain()
                ts(sc_cmp, sc_cmp, col(1), None, ALU.mult)
                dve.drain().then_inc(ev["cmp_prob_ready"], 1)
                now(dve, i, "cmp_turned_in_psum")
                copy(s["pct"], c.bank[2][0:NCMP_S, 0:NH]).then_inc(ev["cmp_turned_ready"], 1)
                now(dve, i, "importance_in_psum")
                copy(s["imp"], c.bank[3][0:NH, 0:NSB]).then_inc(ev["importance_ready"], 1)
                now(dve, i, "group_importance_in_psum")
                tt(s["pick"], c.bank[2][0:NH, 0:NSB], s["notforced"], ALU.mult)
                dve.drain()
                tt(s["pick"], s["pick"], s["forced"], ALU.add)
                dve.drain()
                theirs = s["pick"].unsqueeze(1).to_broadcast([NH, NSB, NSB])
                mine = s["pick"].unsqueeze(2).to_broadcast([NH, NSB, NSB])
                cube = lambda a: a.rearrange("p (i j) -> p i j", i=NSB)
                tt(cube(s["rank"]), theirs, mine, ALU.is_gt)
                tt(cube(s["tie"]), theirs, mine, ALU.is_equal)
                dve.drain()
                tt(s["tie"], s["tie"], s["earlier"], ALU.mult)
                dve.drain()
                tt(s["rank"], s["rank"], s["tie"], ALU.add)
                dve.drain()
                reduce(s["pick"], cube(s["rank"]), AX.X, ALU.add)
                dve.drain()
                ts(s["pick"], s["pick"], float(NSEL), NEG, ALU.is_ge, ALU.mult)
                dve.drain()
                now(dve, i, "sel_scores_in_psum")
                for x in range(4):
                    blocks = s["pick"][:, 8 * x:8 * x + 8].unsqueeze(2).to_broadcast([NH, 8, HD])
                    tt(sc_sel[:, 512 * x:512 * x + 512].rearrange("p (a t) -> p a t", t=HD),
                       c.bank[4 + x][0:NH, :].rearrange("p (a t) -> p a t", t=HD), blocks, ALU.add)
                tt(sc_sel[:, PAST:PAST + 1], sc_sel[:, PAST:PAST + 1], s["pick"][:, NSB - 1:NSB], ALU.add)
                dve.drain()
                scaled_maximum(col(4), sc_sel)
                dve.drain().then_inc(ev["sel_maximum_ready"], 1)
                now(dve, i, "turned_in_psum")
                copy(s["pt"][:, 0:NH * NPG], c.bank[4][:, 0:NH * NPG])
                copy(s["pt"][0:1, NH * NPG:], c.bank[4][0:1, NH * NPG:NH * NPG + NH])
                copy(s["wt"], c.bank[5][:, 0:4 * NH])
                nc.vector.reciprocal(col(5), col(5))
                dve.drain().then_inc(ev["turned_ready"], 1)
                g = s["gate"]
                tt(col(5), col(5), g[:, ds(i, 1), 1], ALU.mult)
                tt(col(3), col(3), g[:, ds(i, 1), 2], ALU.mult)
                copy(col(1), g[:, ds(i, 1), 0])
                dve.drain()
                now(dve, i, "output_in_psum")
                acc = s["acc"]
                ts(acc, c.bank[7][0:NH, 0:RW], col(1), None, ALU.mult)
                for cf, at in ((5, 0), (3, RW)):
                    dve.drain()
                    nc.vector.scalar_tensor_tensor(acc, c.bank[6][0:NH, at:at + RW], col(cf), acc, ALU.mult, ALU.add)
                dve.drain()
                tt(acc, acc, s["ownkv"], ALU.mult)
                dve.drain()
                dve.wait_ge(stored, i * 16 + 16)
                reduce(s["head"], acc.rearrange("p (g d) -> p d g", g=KVH), AX.X, ALU.add).then_inc(ev["head_ready"], 1)

    back = c.work[0:NB, 0:D]
    with c.stage("sample_mixed") as st:
        loaded, turned2 = st.sem("rows_loaded"), st.sem("columns_in_psum")
        block = st.block()

        @block.sync
        def _(sp):
            sp.dma_start(back, out_rows).then_inc(loaded, 16)

        @block.tensor
        def _(pe):
            pe.wait_ge(loaded, 16)
            for k in range(KT):
                last = nc.tensor.transpose(c.bank[0][:, NB * k:NB * k + NB], back[:, P * k:P * k + P],
                                           c.ident[0:NB, 0:NB])
            last.then_inc(turned2, 1)

        @block.vector
        def _(dve):
            dve.wait_ge(turned2, 1)
            nc.vector.tensor_copy(c.slot(9)[:, :, TP:NT], c.bank[0][:, 0:NB * KT].rearrange("p (k b) -> p k b", b=NB))


def hybrid_step(nc, io):
    c = Core(nc, io)
    load_parameters(c)
    load_tokens(c)
    rms_norm(c, c.slot(0), "mix0", c.slot(1), c.slot(3))
    transpose_out(c, "shift_out", c.slot(1), TP - 1, [(TP - 1, TP, io["o_prompt_shift"][0, :, :]),
                                                      (TP, NT, io["o_sample_shift"][0, :, :])])
    rwkv_inputs(c)
    rwkv_prepare(c)
    sample_state(c)
    rwkv_chunks(c)
    rwkv_state_out(c)
    rwkv_finish(c)
    project(c, "rw_wo", c.slot(4), KT, io["rw_wo"][0, :, :], KT, add_to(c, c.slot(0)), "dve")
    mixture(c, 0)

    kv = c.flat(2, 2)[:, 0:KVT * NT].rearrange("p (k t) -> p k t", t=NT)
    rms_norm(c, c.slot(0), "kv", c.slot(1), c.slot(4))
    project(c, "w_kv", c.slot(1), KT, io["w_kv"], KVT, copy_to(c, kv), "act")
    rotate(c, "rotate_keys", kv, kv, (4, 5, 8, 9))
    kv_rows(c)
    compress_prompt(c)

    rms_norm(c, c.slot(0), "mix1", c.slot(1), c.slot(2))
    project(c, "nsa_wq", c.slot(1), KT, io["nsa_wqg"][0][:, 0:D], KT, copy_to(c, c.slot(6)), "act")
    rotate(c, "rotate_queries", c.slot(6), c.slot(7), range(KT))
    gates(c)
    prompt_attention(c)

    sample_memory(c)
    sample_prepare(c)
    sample_attention(c)
    project(c, "nsa_wo", c.slot(9), KT, io["nsa_wo"][0], KT, add_to(c, c.slot(0)), "dve")
    mixture(c, 1)

    rms_norm(c, c.slot(0), "out", c.slot(1), c.slot(2))
    transpose_out(c, "outputs", c.slot(1), 0,
                  [(P * n, P * n + P, io["o_y_prompt"][0, P * n:P * n + P, :]) for n in range(TT)]
                  + [(TP, NT, io["o_y_sample"][:, 0, :])])


_INS = ["x_prompt", "x_sample", "state_wkv", "state_shift", "cache_kv", "cache_win", "page_table",
        "ln_mix", "ln_ffn", "ln_kv", "ln_out", "rw_mu", "rw_wr", "rw_wk", "rw_wv", "rw_wo", "rw_w0", "rw_w1", "rw_w2",
        "rw_a0", "rw_a1", "rw_a2", "rw_g1", "rw_g2", "rw_kk", "rw_ka", "rw_rk", "rw_lnw", "rw_lnb",
        "w_kv", "cmp_pe", "cmp_w1", "cmp_b1", "cmp_w2", "nsa_wqg", "nsa_wo",
        "moe_wrg", "moe_brg", "moe_wre", "moe_bre", "moe_wgate", "moe_wup", "moe_wdown"]
_OUTS = [("o_y_prompt", (1, TP, D)), ("o_y_sample", (NB, 1, D)), ("o_prompt_wkv", (1, 1, NH, HD, HD)),
         ("o_prompt_shift", (1, 1, D)), ("o_prompt_rows", (1, TP, 4, KVH, HD)), ("o_prompt_win", (1, WIN, 2, KVH, HD)),
         ("o_sample_wkv", (1, NB, NH, HD, HD)), ("o_sample_shift", (1, NB, D)),
         ("o_sample_rows", (NB, 1, 4, KVH, HD)), ("o_sample_win", (NB, WIN, 2, KVH, HD))]


def _lay_out(inputs):
    arrays = {name: np.ascontiguousarray(inputs[name]) for name in _INS}
    arrays["consts"] = CONSTS
    return arrays


def kernel(**inputs):
    import concourse.bacc as _bacc
    from concourse.bass_utils import run_bass_kernel_spmd as _run

    nc = _bacc.Bacc("TRN2", target_bir_lowering=False, num_devices=1)
    arrays, io = _lay_out(inputs), {}
    for name, a in arrays.items():
        io[name] = nc.dram_tensor(f"in_{name}", a.shape, mybir.dt.from_np(a.dtype), kind="ExternalInput").ap()
    for name, shape in _OUTS:
        io[name] = nc.dram_tensor(name, shape, F32, kind="ExternalOutput").ap()
    hybrid_step(nc, io)
    r = _run(nc, [{f"in_{name}": a for name, a in arrays.items()}], core_ids=[0])
    return tuple(r.results[0][name] for name, _ in _OUTS)
```

```python
from contextlib import ExitStack

import numpy as np
import concourse.bass as bass
from concourse import mybir

F32 = mybir.dt.float32
I32 = mybir.dt.int32
U32 = mybir.dt.uint32
ALU = mybir.AluOpType
ACT = mybir.ActivationFunctionType
AX = mybir.AxisListType
ds = bass.ds

P = 128
D = 1024
KT = D // P
TP = 512
NB = 8
NT = TP + NB
HALF = NT // 2
TT = TP // P
HD = 64
NH = 16
KVH = 4
CH = 64
NCH = TP // CH
PAST = 2048
PAGE = 128
NPG = PAST // PAGE
NPHYS = 160
WIN = 512
SUB = 16
NSUB = PAST // SUB
NCMP_S = NSUB - 1
NCMP_P = TP // SUB - 1
CH_HID = 128
NSB = PAST // HD + 1
NSEL = 16
E = 32
JOBS = E + 2 * NT // P
LISTS = JOBS + 2
FE = 256
SCALE = HD ** -0.5
EPS = 1e-6
GN_EPS = 64e-5
NEG = -1.0e30

PVEC = ["mu0", "mu1", "mu2", "mu3", "mu4", "mu5", "mix0", "mix1", "ffn0", "ffn1", "kv", "out",
        "w0", "a0", "kk", "ka", "rk", "lnw", "lnb"]

def build_constants():
    cols, parts, at = {}, [], 0

    def put(name, a):
        nonlocal at
        a = np.asarray(a, np.float32)
        full = np.zeros((P, a.shape[1]), np.float32)
        full[:a.shape[0]] = a
        cols[name] = (at, at + a.shape[1])
        at += a.shape[1]
        parts.append(full)

    i, j = np.arange(P)[:, None], np.arange(P)[None, :]
    put("ident", i == j)
    put("ones", np.ones((P, P)))
    put("headones", (i // HD) == (j // HD))
    s, t = np.arange(P)[:, None] % HD, np.arange(HD)[None, :]
    put("ident64", s == t)
    put("before", s < t)
    put("upto", s <= t)
    for lvl in range(6):
        b = 1 << lvl
        put(f"join{lvl}", (s < t) & ((s ^ t) >= b) & ((s ^ t) < 2 * b))
    put("joinT0", ((t < s) & ((s ^ t) >= 1) & ((s ^ t) < 2)))
    put("keep", np.tile((np.arange(TP)[None, :] % CH != 0), (P, 1)))
    put("causal", np.where(j <= i, 0.0, -NEG))
    half = 8
    inv = np.power(np.float32(500000.0), -np.arange(half, dtype=np.float32) * np.float32(2.0 / 16))
    pos = np.concatenate([np.arange(TP), np.full(NB, PAST)]).astype(np.float32)
    ang = pos[None, :] * inv[:, None].astype(np.float32)
    cs, sn = np.cos(ang), np.sin(ang)
    c64 = np.ones((HD, NT)); s64 = np.zeros((HD, NT))
    c64[:half] = cs; c64[half:16] = cs
    s64[:half] = -sn; s64[half:16] = sn
    put("cos", np.tile(c64, (2, 1)))
    put("sin", np.tile(s64, (2, 1)))
    perm = np.zeros((P, P))
    for q in range(2):
        for c in range(half):
            perm[q * HD + half + c, q * HD + c] = 1
            perm[q * HD + c, q * HD + half + c] = 1
    put("swap", perm)
    tok = np.arange(TP).reshape(TT, P).T[:, :, None]
    end = (np.arange(NCMP_P) * SUB + 31)[None, None, :]
    put("cmpfar", np.where(end <= tok, 0.0, -NEG).reshape(P, -1))
    put("cmpone", (end <= tok).astype(np.float32).reshape(P, -1))
    st = np.arange(NCMP_S)[:, None] * SUB
    bl = np.arange(NSB)[None, :] * HD
    put("overlap", (st < bl + HD) & (st + 31 >= bl))
    hh = np.arange(NH)
    put("samegroup", (hh[:, None] // 4) == (hh[None, :] // 4))
    forced = np.zeros(NSB); forced[[0, NSB - 2, NSB - 1]] = 1
    put("notforced", np.tile(1 - forced, (NH, 1)))
    put("forced", np.tile(forced * 1.0e4, (NH, 1)))
    e = (np.arange(NSB)[None, :] < np.arange(NSB)[:, None]).astype(np.float32).reshape(1, -1)
    put("earlier", np.tile(e, (NH, 1)))
    own = (hh[:, None, None] // 4 == np.arange(KVH)[None, :, None]) * np.ones((1, 1, HD))
    put("ownkv", own.reshape(NH, -1))
    put("tokrow", np.arange(P)[:, None] * 2.0 + 1.0)
    oq = (hh[None, None, :] // 4 % 2 == (np.arange(P) // HD)[:, None, None]) & (hh[None, None, :] // 8 == np.arange(2)[None, :, None])
    put("ownquery", oq.reshape(P, -1))
    col = np.arange(TT + 1)[None, :] * P + np.arange(P)[:, None]
    put("valid", col < NT)
    put("token", col)
    put("triangle", i < j)
    put("jobid", np.tile(np.arange(LISTS)[None, :], (P, 1)))
    put("rank4", np.tile(4.0 - np.arange(4)[None, :], (P, 1)))
    put("rank8", np.tile(8.0 - np.arange(8)[None, :], (P, 1)))
    return cols, np.concatenate(parts, 1)


CCOL, CONSTS = build_constants()
NCONST = CONSTS.shape[1]



class Core:

    def __init__(self, nc, io):
        self.nc, self.io = nc, io
        self.n, self.last_sems = 0, []
        self.lists = nc.dram_tensor("expert_lists", [LISTS * P, 4], U32).ap()
        self.token_rows = nc.dram_tensor("expert_token_rows", [NT, D], F32).ap()
        self.expert_rows = nc.dram_tensor("expert_result_rows", [2 * NT, D], F32).ap()
        lists = nc.alloc_sbuf_tensor("job_lists", [P, LISTS * 4], U32)
        self.job_lists = lists[:, :].rearrange("p (j w) -> p j w", w=4)
        self.job_expert = nc.alloc_sbuf_tensor("job_expert", [1, LISTS], I32)[:, :]
        self.slots = nc.alloc_sbuf_tensor("slots", [P, 10 * KT * NT], F32)
        self.work = nc.alloc_sbuf_tensor("work", [P, 8320], F32)
        self.base = nc.alloc_sbuf_tensor("base_constants", [P, 384], F32)
        self.par = nc.alloc_sbuf_tensor("parameters", [P, 8 * len(PVEC)], F32)
        self.small = nc.alloc_sbuf_tensor("small", [P, 704], F32)
        self.z_state = nc.alloc_sbuf_tensor("z_state", [P, KT * HD], F32)
        psum = nc.alloc_psum_tensor("banks", [P, 8, 512], F32)
        self.bank = [psum[:, b, :] for b in range(8)]
        self.pair = [psum[:, 2 * b:2 * b + 2, 0:NT // 2] for b in range(4)]
        self.ident, self.ones, self.headones = (self.base[:, 128 * n:128 * n + 128] for n in range(3))

        keep = nc.alloc_sbuf_tensor("keep", [P, 840], F32)
        self.gate = keep[:, 0:240].rearrange("p (n g) -> p n g", n=TT + 1)
        self.kv_sample = keep[:, 240:336].rearrange("p (k b) -> p k b", b=NB)
        self.cmp_keys = keep[:, 336:336 + 4 * NCMP_P].rearrange("p (g n) -> p g n", g=KVH)
        self.cmp_values = keep[:, 464:464 + KVH * HD]
        self.cmp_bias = keep[:, 720:722]
        self.query_mask = keep[:, 724:756]
        self.queries = keep[:, 756:820].rearrange("p (a g h) -> p a g h", a=2, g=2)
        self.gate_rows = nc.dram_tensor("sample_gates", [NB, 3 * NH], F32).ap()
        self.query_rows = nc.dram_tensor("sample_queries", [2, NB, D], F32).ap()
        self.prompt_keys = self.slots[:, 8 * KT * NT:8 * KT * NT + 4096].rearrange("p (a g t) -> p a g t", a=2, g=KVH)

    def slot(self, n):
        return self.slots[:, n * KT * NT:(n + 1) * KT * NT].rearrange("p (k t) -> p k t", t=NT)

    def flat(self, n, count=1):
        return self.slots[:, n * KT * NT:(n + count) * KT * NT]

    def vec(self, name, k):
        c = 8 * PVEC.index(name) + k
        return self.par[:, c:c + 1]

    def stage(self, name):
        self.n += 1
        return Stage(self, f"{self.n}_{name}")


class Stage:

    def __init__(self, core, name):
        self.nc, self.core, self.name = core.nc, core, name

    def __enter__(self):
        self.ctx, self.sems, self.last, self.starts = ExitStack(), [], self.core.last_sems, []
        return self

    def sem(self, name, start=0):
        self.sems.append(self.nc.alloc_semaphore(f"{name}_{self.name}"))
        if start:
            self.starts.append((self.sems[-1], start))
        return self.sems[-1]

    def block(self):
        self.nc.clear_and_free_semaphores(self.last)
        for sem, start in self.starts:
            self.nc.gpsimd.sem_inc(sem, start)
        if self.starts:
            self.nc.all_engine_barrier()
        return self.ctx.enter_context(self.nc.Block())

    def __exit__(self, *a):
        self.ctx.close()
        self.core.last_sems = self.sems


def warm_up(c, bank, count):
    for _ in range(count):
        c.nc.tensor.matmul(bank[:, 0:P], c.ones, c.ones, start=True, stop=True)


def load_parameters(c):
    nc, io = c.nc, c.io
    nv = len(PVEC) * 8
    rows = c.work[:, 0:256]
    src = [io["rw_mu"][0, n, :] for n in range(6)] + [
        io["ln_mix"][0, :], io["ln_mix"][1, :], io["ln_ffn"][0, :], io["ln_ffn"][1, :], io["ln_kv"][:],
        io["ln_out"][:], io["rw_w0"][0, :], io["rw_a0"][0, :], io["rw_kk"][0, :], io["rw_ka"][0, :],
        io["rw_rk"][0, :, :].rearrange("h d -> (h d)"), io["rw_lnw"][0, :], io["rw_lnb"][0, :]]
    with c.stage("parameters") as st:
        loaded, cleared, turned = st.sem("vectors_loaded"), st.sem("rows_cleared"), st.sem("columns_in_psum")
        block = st.block()

        @block.sync
        def _(sp):
            sp.dma_start(c.base[:, :], io["consts"][:, 0:384]).then_inc(loaded, 16)
            sp.wait_ge(cleared, 1)
            for n, v in enumerate(src):
                r, half = (8 * n) % P, (8 * n) // P
                sp.dma_start(rows[r:r + 8, half * P:half * P + P],
                             v.rearrange("(k p) -> k p", p=P)).then_inc(loaded, 16)

        @block.vector
        def _(dve):
            nc.vector.memset(rows, 0.0).then_inc(cleared, 1)
            dve.wait_ge(turned, 1)
            nc.vector.tensor_copy(c.par[:, 0:nv], c.bank[0][:, 0:nv])

        @block.tensor
        def _(pe):
            pe.wait_ge(loaded, 16 * (len(src) + 1))
            nc.tensor.transpose(c.bank[0][:, 0:P], rows[:, 0:P], c.ident)
            nc.tensor.transpose(c.bank[0][:, P:2 * P], rows[:, P:2 * P], c.ident).then_inc(turned, 1)


def load_tokens(c):
    nc, io = c.nc, c.io
    h, prev = c.slot(0), c.slot(2)
    tiles = [(io["x_prompt"][0, P * n:P * n + P, :], h, P * n, P) for n in range(TT)]
    tiles += [(io["x_sample"][:, 0, :], h, TP, NB), (io["state_shift"][0, :, :], prev, TP, NB)]
    with c.stage("tokens") as st:
        loaded, turned, moved = st.sem("rows_loaded"), st.sem("tile_in_psum"), st.sem("tile_moved")
        block = st.block()
        rows = [c.work[:, D * n:D * n + D] for n in range(len(tiles))]

        @block.sync
        def _(sp):
            for n, (src, _, _, m) in enumerate(tiles):
                sp.dma_start(rows[n][0:m, :], src).then_inc(loaded, 16)

        @block.tensor
        def _(pe):
            pe.wait_ge(loaded, 16 * len(tiles))
            for n, (_, _, _, m) in enumerate(tiles):
                if n >= 2:
                    pe.wait_ge(moved, 2 * (n - 1))
                for k in range(KT):
                    out = c.bank[2 * (n % 2) + k // 4][:, P * (k % 4):P * (k % 4) + m]
                    last = nc.tensor.transpose(out, rows[n][0:m, P * k:P * k + P], c.ident[0:m, 0:m])
                last.then_inc(turned, 1)

        @block.vector
        def _(dve):
            for n, (_, dst, t0, m) in enumerate(tiles):
                dve.wait_ge(turned, n + 1)
                for a in range(2):
                    src = c.bank[2 * (n % 2) + a][:, :].rearrange("p (k t) -> p k t", t=P)
                    nc.vector.tensor_copy(dst[:, 4 * a:4 * a + 4, t0:t0 + m], src[:, :, 0:m]).then_inc(moved, 1)


def rms_norm(c, src, gain, dst, square):
    nc = c.nc
    rstd, root = c.work[:, 0:NT], c.work[:, NT:2 * NT]
    halves = lambda a: a.rearrange("p (s t) -> p s t", s=2)
    with c.stage("norm_" + gain) as st:
        squared = [st.sem(f"squares_ready{v}") for v in range(2)]
        summed, means, roots = st.sem("sums_in_psum"), st.sem("means_ready"), st.sem("roots_ready")
        block = st.block()

        @block.scalar
        def _(act):
            for k in range(0, KT, 2):
                nc.scalar.activation(square[:, k, :], src[:, k, :], ACT.Square).then_inc(squared[0], 1)
            act.wait_ge(means, 1)
            nc.scalar.activation(root, root, ACT.Sqrt).then_inc(roots, 1)

        @block.tensor
        def _(pe):
            for k in range(KT):
                pe.wait_ge(squared[k % 2], k // 2 + 1)
                for s in range(2):
                    last = nc.tensor.matmul(c.pair[0][:, s, :], c.ones, square[:, k, HALF * s:HALF * s + HALF],
                                            start=(k == 0), stop=(k == KT - 1))
            last.then_inc(summed, 1)

        @block.vector
        def _(dve):
            for k in range(1, KT, 2):
                nc.vector.tensor_tensor(square[:, k, :], src[:, k, :], src[:, k, :], ALU.mult).then_inc(squared[1], 1)
            dve.wait_ge(summed, 1)
            nc.vector.tensor_scalar(halves(root), c.pair[0], 1.0 / D, EPS, ALU.mult, ALU.add).then_inc(means, 1)
            dve.wait_ge(roots, 1)
            nc.vector.reciprocal(rstd, root)
            dve.drain()
            for k in range(KT):
                nc.vector.scalar_tensor_tensor(dst[:, k, :], src[:, k, :], c.vec(gain, k), rstd, ALU.mult, ALU.mult)


def project(c, name, x, kt, weight, tiles, evacuate, engine, out_rows=P, beside=None):
    nc = c.nc
    U = 4 if tiles % 4 == 0 else 1
    ring = [c.work[:, kt * out_rows * u:kt * out_rows * (u + 1)].rearrange("p (k n) -> p k n", n=out_rows)
            for u in range(U)]
    wv = weight.rearrange("(k p) n -> p k n", p=P)
    with c.stage(name) as st:
        ready = [st.sem(f"weight_ready{u}") for u in range(U)]
        done, free = st.sem("tiles_done"), st.sem("bank_free")
        block = st.block()

        @block.sync
        def _(sp):
            with sp.Fori(0, tiles // U) as i:
                for u in range(U):
                    sp.wait_ge(done, i * U + (u + 1))
                    sp.dma_start(ring[u], wv[:, :, ds((i * U + u) * out_rows, out_rows)]).then_inc(ready[u], 16)

        @block.tensor
        def _(pe):
            pe.sem_inc(done, U)
            warm_up(c, c.bank[7], 7)
            with pe.Fori(0, tiles // U) as i:
                for u in range(U):
                    pe.wait_ge(ready[u], i * 16 + 16)
                    pe.wait_ge(free, i * U + (u + 1))
                    for k in range(kt):
                        for s in range(2):
                            last = nc.tensor.matmul(c.pair[u][0:out_rows, s, :], ring[u][:, k, :],
                                                    x[:, k, HALF * s:HALF * s + HALF],
                                                    start=(k == 0), stop=(k == kt - 1))
                    last.then_inc(done, 1)

        def copies(eng):
            eng.sem_inc(free, U)
            with eng.Fori(0, tiles // U) as i:
                for u in range(U):
                    eng.wait_ge(done, i * U + (U + u + 1))
                    evacuate(eng, i * U + u, c.pair[u][0:out_rows]).then_inc(free, 1)

        if engine == "act":
            block.scalar(copies)
            if beside:
                block.vector(beside)
        else:
            block.vector(copies)


def copy_to(c, dst, rows=P):
    def evacuate(eng, m, tile):
        return c.nc.scalar.activation(dst[0:rows, ds(m, 1), :].rearrange("p a (s t) -> p (a s) t", s=2), tile,
                                      ACT.Copy)
    return evacuate


def add_to(c, dst):
    def evacuate(eng, m, tile):
        o = dst[:, ds(m, 1), :].rearrange("p a (s t) -> p (a s) t", s=2)
        return c.nc.vector.tensor_tensor(o, o, tile, ALU.add)
    return evacuate


def elementwise(c, name, body):
    with c.stage(name) as st:
        block = st.block()

        @block.vector
        def _(dve):
            body(dve)


def transpose_out(c, name, src, cols, stores):
    nc = c.nc
    with c.stage(name) as st:
        turned, moved, stored = st.sem("rows_in_psum"), st.sem("rows_moved"), st.sem("rows_stored")
        block = st.block()

        @block.tensor
        def _(pe):
            for n, (a, b, _) in enumerate(stores):
                if n >= 2:
                    pe.wait_ge(moved, 2 * (n - 1))
                for k in range(KT):
                    last = nc.tensor.transpose(c.bank[2 * (n % 2) + k // 4][0:b - a, P * (k % 4):P * (k % 4) + P],
                                               src[:, k, a:b], c.ident)
                last.then_inc(turned, 1)

        @block.vector
        def _(dve):
            for n, (a, b, _) in enumerate(stores):
                dve.wait_ge(turned, n + 1)
                for k in range(2):
                    nc.vector.tensor_copy(c.work[0:b - a, D * n + 512 * k:D * n + 512 * k + 512],
                                          c.bank[2 * (n % 2) + k][0:b - a, :]).then_inc(moved, 1)

        @block.sync
        def _(sp):
            for n, (a, b, dst) in enumerate(stores):
                sp.wait_ge(moved, 2 * (n + 1))
                sp.dma_start(dst, c.work[0:b - a, D * n:D * n + D]).then_inc(stored, 16)
            sp.wait_ge(stored, 16 * len(stores))



def rwkv_inputs(c):
    nc, io = c.nc, c.io
    xn, xx = c.slot(1), c.slot(2)

    def differences(dve):
        nc.vector.tensor_tensor(xx[:, :, 1:TP], xn[:, :, 0:TP - 1], xn[:, :, 1:TP], ALU.subtract)
        nc.vector.tensor_scalar(xx[:, :, 0:1], xn[:, :, 0:1], -1.0, None, ALU.mult)
        nc.vector.tensor_tensor(xx[:, :, TP:NT], xx[:, :, TP:NT], xn[:, :, TP:NT], ALU.subtract)
        dve.drain()
        mix(0)(dve)

    turn = [0, 2, 3, 1, 4, 5]

    def mix(x):
        def body(dve):
            for k in range(KT):
                nc.vector.scalar_tensor_tensor(mixed(x)[:, k, :], xx[:, k, :], c.vec(f"mu{turn[x]}", k), xn[:, k, :],
                                               ALU.mult, ALU.add)
        return body

    def mixed(x):
        return c.slot((3, 9)[x % 2])

    elementwise(c, "shift", differences)

    for x, (w, dst) in enumerate((("rw_wr", 4), ("rw_wk", 5), ("rw_wv", 6))):
        project(c, w, mixed(x), KT, io[w][0, :, :], KT, copy_to(c, c.slot(dst)), "act", beside=mix(x + 1))

    pairs = [("rw_w1", ACT.Tanh, 64, "rw_w2", "w0", 7), ("rw_a1", ACT.Copy, 64, "rw_a2", "a0", 8),
             ("rw_g1", ACT.Sigmoid, P, "rw_g2", None, 9)]
    first = [c.work[:, 1024 * n:1024 * n + KT * pairs[n][2]].rearrange("p (k n) -> p k n", k=KT) for n in range(3)]
    second = [c.work[0:pairs[n][2], 3072 + D * n:3072 + D * n + D] for n in range(3)]
    hidden = [c.work[0:pairs[n][2], 6144 + NT * n:6144 + NT * n + NT] for n in range(3)]
    order = [(0, None), (1, None)] + [(0, m) for m in range(KT)] + [(2, None)]
    order += [(n, m) for n in (1, 2) for m in range(KT)]
    halves = lambda a: a.rearrange("p (s t) -> p s t", s=2)
    with c.stage("low_rank") as st:
        loaded = [st.sem(f"weights_loaded{n}") for n in range(3)]
        mix_ready, full, free = st.sem("input_mixed"), st.sem("product_in_psum"), st.sem("product_taken")
        block = st.block()

        @block.sync
        def _(sp):
            for n, (w1, _, _, w2, _, _) in enumerate(pairs):
                sp.dma_start(first[n], io[w1][0, :, :].rearrange("(k p) n -> p k n", p=P)).then_inc(loaded[n], 16)
                sp.dma_start(second[n], io[w2][0, :, :]).then_inc(loaded[n], 16)

        @block.tensor
        def _(pe):
            for x, (n, m) in enumerate(order):
                rows = pairs[n][2]
                if x >= 4:
                    pe.wait_ge(free, x - 3)
                pair = c.pair[x % 4]
                if m is None:
                    pe.wait_ge(loaded[n], 32)
                    if n:
                        pe.wait_ge(mix_ready, n)
                    for k in range(KT):
                        for s in range(2):
                            last = nc.tensor.matmul(pair[0:rows, s, :], first[n][:, k, :],
                                                    mixed(3 + n)[:, k, HALF * s:HALF * s + HALF],
                                                    start=(k == 0), stop=(k == KT - 1))
                else:
                    pe.wait_ge(free, order.index((n, None)) + 1)
                    for s in range(2):
                        last = nc.tensor.matmul(pair[:, s, :], second[n][:, P * m:P * m + P],
                                                hidden[n][:, HALF * s:HALF * s + HALF], start=True, stop=True)
                last.then_inc(full, 1)

        @block.scalar
        def _(act):
            for x, (n, m) in enumerate(order):
                _, func, rows, _, bias, dst = pairs[n]
                act.wait_ge(full, x + 1)
                if m is None:
                    nc.scalar.activation(halves(hidden[n]), c.pair[x % 4][0:rows], func).then_inc(free, 1)
                elif bias:
                    nc.scalar.activation(halves(c.slot(dst)[:, m, :]), c.pair[x % 4], ACT.Sigmoid,
                                         bias=c.vec(bias, m)).then_inc(free, 1)
                else:
                    nc.scalar.activation(halves(c.slot(dst)[:, m, :]), c.pair[x % 4], ACT.Copy).then_inc(free, 1)

        @block.vector
        def _(dve):
            mix(4)(dve)
            dve.drain().then_inc(mix_ready, 1)
            dve.wait_ge(full, 1)
            mix(5)(dve)
            dve.drain().then_inc(mix_ready, 1)


def rwkv_prepare(c):
    nc, io = c.nc, c.io
    r, k_, v, w, a = (c.slot(n) for n in range(4, 9))
    kk, tmp, bonus = c.slot(1), c.slot(2), c.slot(3)
    keep = c.work[:, 0:TP]
    norm = [c.work[:, TP + NT * n:TP + NT * (n + 1)] for n in range(2)]
    ends = c.small[:, 0:KT * NCH].rearrange("p (k n) -> p k n", n=NCH)
    NLOG = -float(np.exp(-0.5))
    with c.stage("rwkv_prepare") as st:
        keep_in = st.sem("keep_loaded")
        sq, nrm, nfree = st.sem("squares_ready"), st.sem("norms_in_psum"), st.sem("norms_used")
        rk, bon, bfree = st.sem("rk_ready"), st.sem("bonus_in_psum"), st.sem("bonus_used")
        g_ready, roots = st.sem("decay_sums_ready"), st.sem("norms_ready")
        inverted, scaled = st.sem("norms_inverted"), st.sem("keys_scaled")
        banks, halves = c.pair, lambda a: a.rearrange("p (s t) -> p s t", s=2)
        block = st.block()

        @block.sync
        def _(sp):
            lo, hi = CCOL["keep"]
            sp.dma_start(keep, io["consts"][:, lo:hi]).then_inc(keep_in, 16)

        @block.vector
        def _(dve):
            dve.wait_ge(keep_in, 16)
            for k in range(KT + 1):
                if k < KT:
                    nc.vector.tensor_scalar(kk[:, k, :], k_[:, k, :], c.vec("kk", k), None, ALU.mult)
                    nc.vector.tensor_scalar(bonus[:, k, :], a[:, k, :], -1.0, c.vec("ka", k), ALU.add, ALU.mult)
                    dve.drain()
                    nc.vector.tensor_tensor(tmp[:, k, :], kk[:, k, :], kk[:, k, :], ALU.mult).then_inc(sq, 1)
                    nc.vector.scalar_tensor_tensor(k_[:, k, :], bonus[:, k, :], 1.0, k_[:, k, :], ALU.add, ALU.mult)
                    dve.drain()
                    nc.vector.scalar_tensor_tensor(bonus[:, k, :], r[:, k, :], c.vec("rk", k), k_[:, k, :],
                                                   ALU.mult, ALU.mult).then_inc(rk, 1)
                if k == 0:
                    continue
                j = k - 1
                dve.wait_ge(nrm, j + 1)
                if j >= 2:
                    dve.wait_ge(scaled, j - 1)
                nc.vector.tensor_scalar(halves(norm[j % 2]), banks[j % 2], 1e-24, None, ALU.max).then_inc(nfree, 1)
                nc.vector.tensor_scalar(w[:, j, :], w[:, j, :], NLOG, None, ALU.mult)
                dve.drain()
                nc.vector.tensor_tensor_scan(tmp[:, j, 0:TP], keep, w[:, j, 0:TP], 0.0, ALU.mult, ALU.add)
                dve.wait_ge(bon, j + 1)
                nc.vector.tensor_tensor(halves(bonus[:, j, :]), banks[2 + j % 2], halves(v[:, j, :]),
                                        ALU.mult).then_inc(bfree, 1)
                dve.drain()
                nc.vector.tensor_copy(ends[:, j, :], tmp[:, j, CH - 1:TP:CH])
                nc.vector.tensor_tensor(w[:, j, 0:TP], tmp[:, j, 0:TP], w[:, j, 0:TP],
                                        ALU.subtract).then_inc(g_ready, 1)
                dve.wait_ge(roots, j + 1)
                nc.vector.reciprocal(norm[j % 2], norm[j % 2]).then_inc(inverted, 1)

        @block.tensor
        def _(pe):
            for k in range(KT):
                for src, ready, x, free, done_ in ((tmp, sq, 0, nfree, nrm), (bonus, rk, 2, bfree, bon)):
                    pe.wait_ge(ready, k + 1)
                    if k >= 2:
                        pe.wait_ge(free, k - 1)
                    for s in range(2):
                        last = nc.tensor.matmul(banks[x + k % 2][:, s, :], c.headones,
                                                src[:, k, HALF * s:HALF * s + HALF], start=True, stop=True)
                    last.then_inc(done_, 1)

        @block.scalar
        def _(act):
            for k in range(KT):
                act.wait_ge(nfree, k + 1)
                nc.scalar.activation(norm[k % 2], norm[k % 2], ACT.Sqrt).then_inc(roots, 1)
            for k in range(KT):
                act.wait_ge(g_ready, k + 1)
                nc.scalar.activation(ends[:, k, :], ends[:, k, :], ACT.Exp)
                nc.scalar.activation(w[:, k, :], w[:, k, :], ACT.Exp)

        @block.gpsimd
        def _(pool):
            for k in range(KT):
                pool.wait_ge(inverted, k + 1)
                nc.gpsimd.tensor_tensor(kk[:, k, :], kk[:, k, :], norm[k % 2], ALU.mult).then_inc(scaled, 1)
                pool.drain()
                nc.gpsimd.tensor_tensor(a[:, k, :], a[:, k, :], kk[:, k, :], ALU.mult)

    prompt = slice(0, TP)
    with c.stage("rwkv_scale") as st:
        up = st.sem("growth_ready")
        used, also = st.sem("factors_used_by_vector"), st.sem("factors_used_by_pool")
        block = st.block()
        bufs = [c.work[:, 2048 + TP * n:2048 + TP * (n + 1)] for n in range(4)]

        @block.scalar
        def _(act):
            for k in range(KT):
                if k >= 2:
                    act.wait_ge(used, k - 1)
                    act.wait_ge(also, k - 1)
                nc.scalar.activation(bufs[k % 2], tmp[:, k, prompt], ACT.Exp)
                nc.scalar.activation(bufs[2 + k % 2], tmp[:, k, prompt], ACT.Exp, scale=-1.0).then_inc(up, 1)

        @block.vector
        def _(dve):
            for k in range(KT):
                nc.vector.scalar_tensor_tensor(w[:, k, prompt], kk[:, k, prompt], -1.0, w[:, k, prompt],
                                               ALU.mult, ALU.mult)
                dve.wait_ge(up, k + 1)
                nc.vector.tensor_tensor(r[:, k, prompt], r[:, k, prompt], bufs[k % 2], ALU.mult)
                nc.vector.tensor_tensor(a[:, k, prompt], a[:, k, prompt], bufs[2 + k % 2], ALU.mult).then_inc(used, 1)

        @block.gpsimd
        def _(pool):
            for k in range(KT):
                pool.wait_ge(up, k + 1)
                nc.gpsimd.tensor_tensor(k_[:, k, prompt], k_[:, k, prompt], bufs[2 + k % 2], ALU.mult).then_inc(also, 1)


def sample_state(c):
    nc, io = c.nc, c.io
    arrays = [c.slot(4), c.slot(5), c.slot(6), c.slot(7), c.slot(1), c.slot(8)]
    scratch = nc.dram_tensor("sample_vectors", [6, NB, D], F32).ap()
    out_scratch = nc.dram_tensor("sample_mixed", [NB, D], F32).ap()
    rows = c.work[0:NB, 0:6 * D].rearrange("b (n e) -> b n e", e=D)
    S = c.flat(2)[:, 0:HD * HD].rearrange("p (i j) -> p i j", j=HD)
    with c.stage("sample_vectors") as st:
        turned, moved, stored = st.sem("rows_in_psum"), st.sem("rows_moved"), st.sem("rows_stored")
        block = st.block()

        @block.tensor
        def _(pe):
            for n, a in enumerate(arrays):
                if n >= 2:
                    pe.wait_ge(moved, 2 * (n - 1))
                for k in range(KT):
                    last = nc.tensor.transpose(c.bank[2 * (n % 2) + k // 4][0:NB, P * (k % 4):P * (k % 4) + P],
                                               a[:, k, TP:NT], c.ident)
                last.then_inc(turned, 1)

        @block.vector
        def _(dve):
            for n in range(6):
                dve.wait_ge(turned, n + 1)
                for k in range(2):
                    nc.vector.tensor_copy(rows[:, n, 512 * k:512 * k + 512],
                                          c.bank[2 * (n % 2) + k][0:NB, :]).then_inc(moved, 1)

        @block.sync
        def _(sp):
            sp.dma_start(S, io["state_wkv"][0].rearrange("b h i j -> (b h) i j")).then_inc(stored, 16)
            sp.wait_ge(moved, 12)
            sp.dma_start(scratch.rearrange("n b e -> b n e"), rows).then_inc(stored, 16)
            sp.wait_ge(stored, 32)

    t1 = c.flat(1)[:, 0:HD * HD].rearrange("p (i j) -> p i j", j=HD)
    t2 = c.work[:, 0:HD * HD].rearrange("p (i j) -> p i j", j=HD)
    vec = c.work[:, 4096:4096 + 6 * HD].rearrange("p (n d) -> p n d", d=HD)
    sa, o = c.work[:, 4608:4608 + HD], c.work[:, 4672:4672 + HD]
    key = lambda n: vec[:, n, :].unsqueeze(1).to_broadcast([P, HD, HD])
    val = lambda a: a.unsqueeze(2).to_broadcast([P, HD, HD])
    with c.stage("sample_state") as st:
        outer_ready = st.sem("outer_product_ready")
        loaded, stepped, mixed, stored = (st.sem(n) for n in ("vectors_loaded", "state_stepped", "output_ready",
                                                              "stored"))
        block = st.block()

        @block.sync
        def _(sp):
            sp.dma_start(vec, scratch.rearrange("n b (h d) -> (b h) n d", d=HD)).then_inc(loaded, 16)
            sp.wait_ge(stepped, 1)
            sp.dma_start(io["o_sample_wkv"][0].rearrange("b h i j -> (b h) i j"), S).then_inc(stored, 16)
            sp.wait_ge(mixed, 1)
            sp.dma_start(out_scratch.rearrange("b (h d) -> (b h) d", d=HD), o).then_inc(stored, 16)
            sp.wait_ge(stored, 32)

        @block.gpsimd
        def _(pool):
            pool.wait_ge(loaded, 16)
            nc.gpsimd.tensor_tensor(t2, key(1), val(vec[:, 2, :]), ALU.mult).then_inc(outer_ready, 1)

        @block.vector
        def _(dve):
            tt = nc.vector.tensor_tensor
            dve.wait_ge(loaded, 16)
            tt(t1, S, key(4), ALU.mult)
            dve.drain()
            nc.vector.tensor_reduce(sa, t1, AX.X, ALU.add)
            tt(S, S, key(3), ALU.mult)
            dve.drain()
            tt(t1, key(5), val(sa), ALU.mult)
            dve.wait_ge(outer_ready, 1)
            tt(S, S, t2, ALU.add)
            dve.drain()
            tt(S, S, t1, ALU.subtract)
            dve.drain().then_inc(stepped, 1)
            tt(t1, S, key(0), ALU.mult)
            dve.drain()
            nc.vector.tensor_reduce(o, t1, AX.X, ALU.add).then_inc(mixed, 1)

    back = c.work[0:NB, 0:D]
    with c.stage("sample_output") as st:
        loaded, turned = st.sem("rows_loaded"), st.sem("columns_in_psum")
        block = st.block()

        @block.sync
        def _(sp):
            sp.dma_start(back, out_scratch).then_inc(loaded, 16)

        @block.tensor
        def _(pe):
            pe.wait_ge(loaded, 16)
            for k in range(KT):
                last = nc.tensor.transpose(c.bank[0][:, NB * k:NB * k + NB], back[:, P * k:P * k + P],
                                           c.ident[0:NB, 0:NB])
            last.then_inc(turned, 1)

        @block.vector
        def _(dve):
            dve.wait_ge(turned, 1)
            nc.vector.tensor_copy(c.slot(4)[:, :, TP:NT], c.bank[0][:, 0:NB * KT].rearrange("p (k b) -> p k b", b=NB))


def rwkv_chunks(c):
    nc, io = c.nc, c.io
    lo, hi = CCOL["ident64"][0], CCOL["joinT0"][1]
    table = c.small[:, 64:64 + hi - lo]
    const = lambda name: table[:, CCOL[name][0] - lo:CCOL[name][1] - lo]
    wide = lambda a: a.unsqueeze(1).to_broadcast([P, KT, CH])
    ends = c.small[:, 0:KT * NCH].rearrange("p (k n) -> p k n", n=NCH)
    area = [c.flat(1, 2), c.work[:, :]]
    names = ["r", "k", "a", "b", "v", "LT", "join", "T", "TT", "X", "MT", "AB", "AK", "Bt", "Kt", "Vt"]
    buf = [{n: area[u][:, 512 * x:512 * x + 512].rearrange("p (k t) -> p k t", t=CH)
            for x, n in enumerate(names)} for u in range(2)]
    for u in range(2):
        buf[u]["RHS"], buf[u]["U"] = buf[u]["X"], buf[u]["T"]
    Z = c.z_state[:, :].rearrange("p (k i) -> p k i", i=HD)
    src = {"r": c.slot(4), "k": c.slot(5), "v": c.slot(6), "a": c.slot(7), "b": c.slot(8)}

    order = [(u, n) for u in range(2) for n in ("LT", "L")]
    filler = {1: ["MT", "AB"], 2: ["AK"], 3: ["Bt"], 4: ["Kt"], 5: ["Vt"]}
    for lvl in range(1, 6):
        order += [(u, f"X{lvl}") for u in range(2)]
        order += [(u, n) for n in filler[lvl] for u in range(2)]
        order += [(u, f"{n}{lvl}") for u in range(2) for n in (("T", "TT") if lvl < 5 else ("TT",))]
    order += [(u, n) for u in range(2) for n in ("RHS", "U", "O", "Z")]
    place, per_round = {}, [0] * 8
    for u in range(2):
        for x, n in enumerate([n for v, n in order if v == u]):
            b = 4 * u + x % 4
            place[u, n] = (b, per_round[b])
            per_round[b] += 1

    with c.stage("rwkv_chunks") as st:
        table_in, window_moved = st.sem("masks_loaded"), st.sem("window_moved")
        chunk_ready = [st.sem(f"chunk_ready{u}") for u in range(2)]
        joins = [st.sem(f"join_ready{u}") for u in range(2)]
        state_ready = st.sem("state_ready", 1)
        full = [st.sem(f"product_in_bank{b}") for b in range(8)]
        taken = [st.sem(f"product_taken{b}", 1) for b in range(8)]
        block = st.block()

        def produced(eng, i, u, name):
            b, n = place[u, name]
            eng.wait_ge(full[b], i * per_round[b] + (n + 1))

        def in_sbuf(eng, i, u, names, before=None):
            least = {}
            for name in names:
                b, n = place[u, name]
                least[b] = max(least.get(b, 0), n + 1)
            if before:
                b, n = place[u, before]
                least[b] = max(least.get(b, 0), n)
            for b, n in least.items():
                eng.wait_ge(taken[b], i * per_round[b] + (n + 1))

        def bank(u, name):
            return c.bank[place[u, name][0]][:, :].rearrange("p (k t) -> p k t", t=CH)

        @block.sync
        def _(sp):
            sp.dma_start(table, io["consts"][:, lo:hi]).then_inc(table_in, 16)
            sp.dma_start(io["o_sample_win"][:, 0:WIN - 1].rearrange("b t s g d -> b (t s g d)"),
                         io["cache_win"][:, 1:WIN].rearrange("b t s g d -> b (t s g d)")).then_inc(window_moved, 16)
            sp.wait_ge(window_moved, 16)

        @block.tensor
        def _(pe):
            pe.wait_ge(table_in, 16)

            def product(i, u, name, terms, needs=()):
                b = place[u, name][0]
                in_sbuf(pe, i, u, needs, before=name)
                pe.nop(nofuse=True)
                out = bank(u, name)
                for k in range(KT):
                    for q in range(2):
                        half = slice(HD * q, HD * q + HD)
                        for x, (lhsT, rhs) in enumerate(terms):
                            if rhs is None and q == 0:
                                last = nc.tensor.transpose(out[half, k, :], lhsT[half, k, :], const("ident64")[half, :])
                                continue
                            right = const("ident64")[half, :] if rhs is None else rhs[half, k, :]
                            last = nc.tensor.matmul(out[half, k, :], lhsT[half, k, :], right,
                                                    start=(x == 0), stop=(x == len(terms) - 1))
                return last.then_inc(full[b], 1)

            with pe.Fori(0, NCH // 2) as i:
                for u in range(2):
                    w = buf[u]
                    pe.wait_ge(chunk_ready[u], i * 5 + 5)
                    product(i, u, "LT", [(w["b"], w["a"])])
                    product(i, u, "L", [(w["a"], w["b"])])
                for lvl in range(1, 6):
                    for u in range(2):
                        w = buf[u]
                        pe.wait_ge(joins[u], i * 5 + lvl)
                        product(i, u, f"X{lvl}", [(w["join"], w["T"])], ["L" if lvl == 1 else f"T{lvl - 1}"])
                    for name in filler[lvl]:
                        for u in range(2):
                            w = buf[u]
                            product(i, u, name, {
                                "MT": [(w["k"], w["a"])], "AB": [(w["b"], w["r"])], "AK": [(w["k"], w["r"])],
                                "Bt": [(w["b"], None)], "Kt": [(w["k"], None)], "Vt": [(w["v"], None)]}[name])
                    for u in range(2):
                        w = buf[u]
                        needs = [f"X{lvl}", "LT" if lvl == 1 else f"TT{lvl - 1}"]
                        if lvl < 5:
                            product(i, u, f"T{lvl}", [(w["TT"], w["X"])], needs)
                        product(i, u, f"TT{lvl}", [(w["X"], w["TT"])], needs)
                for u in range(2):
                    w = buf[u]
                    pe.wait_ge(state_ready, i * 2 + (u + 2))
                    product(i, u, "RHS", [(w["a"], Z), (w["MT"], w["Vt"])], ["MT", "Vt"])
                    product(i, u, "U", [(w["TT"], w["RHS"])], ["TT5", "RHS"])
                    product(i, u, "O", [(Z, w["r"]), (w["U"], w["AB"]), (w["Vt"], w["AK"])], ["U", "AB", "AK"])
                    product(i, u, "Z", [(w["Bt"], w["U"]), (w["Kt"], w["Vt"])], ["Bt", "Kt"])

        def take(eng, i, u, name, op):
            produced(eng, i, u, name)
            op(bank(u, name)).then_inc(taken[place[u, name][0]], 1)

        @block.scalar
        def _(act):
            with act.Fori(0, NCH // 2) as i:
                for u in range(2):
                    act.wait_ge(state_ready, i * 2 + (u + 1))
                    for n in ("a", "v"):
                        nc.scalar.copy(buf[u][n], src[n][:, :, ds(i * 2 * CH + u * CH, CH)]).then_inc(chunk_ready[u], 1)
                for u, name in order:
                    stem = name.rstrip("0123456789")
                    if stem in ("X", "Bt", "Kt", "Vt", "RHS", "U"):
                        take(act, i, u, name, lambda p: nc.scalar.copy(buf[u][stem], p))
                    if stem == "O":
                        take(act, i, u, name,
                             lambda p: nc.scalar.copy(c.slot(4)[:, :, ds(i * 2 * CH + u * CH, CH)], p))

        @block.gpsimd
        def _(pool):
            pool.wait_ge(table_in, 16)
            with pool.Fori(0, NCH // 2) as i:
                for u in range(2):
                    pool.wait_ge(state_ready, i * 2 + (u + 1))
                    for n in ("b", "r", "k"):
                        nc.gpsimd.tensor_copy(buf[u][n],
                                              src[n][:, :, ds(i * 2 * CH + u * CH, CH)]).then_inc(chunk_ready[u], 1)
                for lvl in range(1, 6):
                    for u in range(2):
                        if lvl == 1:
                            in_sbuf(pool, i, u, ["LT"])
                        else:
                            produced(pool, i, u, f"X{lvl - 1}")
                        nc.gpsimd.tensor_tensor(buf[u]["join"], buf[u]["LT"], wide(const(f"join{lvl}")),
                                                ALU.mult).then_inc(joins[u], 1)

        @block.vector
        def _(dve):
            nc.vector.memset(Z, 0.0).then_inc(state_ready, 1)
            dve.wait_ge(table_in, 16)
            tt = nc.vector.tensor_tensor
            with dve.Fori(0, NCH // 2) as i:
                for u, name in order:
                    w = buf[u]
                    stem = name.rstrip("0123456789")
                    if name == "LT":
                        produced(dve, i, u, name)
                        nc.vector.tensor_copy(w["LT"], bank(u, name))
                        tt(w["TT"], bank(u, name), wide(const("join0")), ALU.mult)
                        dve.drain()
                        tt(w["TT"], w["TT"], wide(const("ident64")), ALU.add).then_inc(taken[place[u, name][0]], 1)
                    if name == "L":
                        produced(dve, i, u, name)
                        tt(w["T"], bank(u, name), wide(const("joinT0")), ALU.mult)
                        dve.drain()
                        tt(w["T"], w["T"], wide(const("ident64")), ALU.add).then_inc(taken[place[u, name][0]], 1)
                    if name in ("MT", "AB", "AK"):
                        mask = const("before" if name == "MT" else "upto")
                        take(dve, i, u, name, lambda p: tt(w[name], p, wide(mask), ALU.mult))
                    if stem in ("T", "TT"):
                        take(dve, i, u, name, lambda p: tt(w[stem], w[stem], p, ALU.add))
                    if name == "Z":
                        take(dve, i, u, name, lambda p: tt(Z, Z, p, ALU.add))
                        dve.drain()
                        end = ends[:, :, ds(i * 2 + u, 1)].to_broadcast([P, KT, HD])
                        tt(Z, Z, end, ALU.mult).then_inc(state_ready, 1)


def rwkv_state_out(c):
    nc, io = c.nc, c.io
    Z = c.z_state[:, :].rearrange("p (k i) -> p k i", i=HD)
    rows = c.work[0:HD, 0:D]
    with c.stage("rwkv_state_out") as st:
        turned, moved, stored = st.sem("state_in_psum"), st.sem("state_moved"), st.sem("state_stored")
        block = st.block()

        @block.tensor
        def _(pe):
            for k in range(KT):
                last = nc.tensor.transpose(c.bank[k // 4][0:HD, P * (k % 4):P * (k % 4) + P], Z[:, k, :], c.ident)
            last.then_inc(turned, 1)

        @block.vector
        def _(dve):
            dve.wait_ge(turned, 1)
            for a in range(2):
                nc.vector.tensor_copy(rows[:, 512 * a:512 * a + 512], c.bank[a][0:HD, :]).then_inc(moved, 1)

        @block.sync
        def _(sp):
            sp.wait_ge(moved, 2)
            sp.dma_start(io["o_prompt_wkv"][0, 0].rearrange("h i j -> i h j"),
                         rows.rearrange("i (h j) -> i h j", j=HD)).then_inc(stored, 16)
            sp.wait_ge(stored, 16)


def rwkv_finish(c):
    nc = c.nc
    o, bonus, g, centred, normed = c.slot(4), c.slot(3), c.slot(9), c.slot(1), c.slot(2)
    rn = [c.work[:, NT * n:NT * n + NT] for n in range(2)]
    halves = lambda a: a.rearrange("p (s t) -> p s t", s=2)
    with c.stage("rwkv_finish") as st:
        mean, centred_ready, squared, var, var_read, roots, scaled = (st.sem(n) for n in (
            "mean_in_psum", "centred_ready", "squares_ready", "variance_in_psum", "variance_ready",
            "deviation_ready", "tile_scaled"))
        inverted = st.sem("deviation_inverted")
        block = st.block()

        def sums(src, k, pair):
            for s in range(2):
                last = nc.tensor.matmul(pair[:, s, :], c.headones, src[:, k, HALF * s:HALF * s + HALF],
                                        start=True, stop=True)
            return last

        @block.tensor
        def _(pe):
            for k in range(KT + 1):
                if k < KT:
                    if k >= 2:
                        pe.wait_ge(centred_ready, k - 1)
                    sums(o, k, c.pair[k % 2]).then_inc(mean, 1)
                if k >= 1:
                    pe.wait_ge(squared, k)
                    if k >= 3:
                        pe.wait_ge(var_read, k - 2)
                    sums(normed, k - 1, c.pair[2 + (k - 1) % 2]).then_inc(var, 1)

        @block.scalar
        def _(act):
            for k in range(KT + 1):
                if k < KT:
                    act.wait_ge(centred_ready, k + 1)
                    nc.scalar.activation(normed[:, k, :], centred[:, k, :], ACT.Square).then_inc(squared, 1)
                if k >= 1:
                    act.wait_ge(var_read, k)
                    nc.scalar.activation(rn[(k - 1) % 2], rn[(k - 1) % 2], ACT.Sqrt).then_inc(roots, 1)

        @block.gpsimd
        def _(pool):
            for k in range(KT):
                pool.wait_ge(inverted, k + 1)
                nc.gpsimd.tensor_tensor(normed[:, k, :], centred[:, k, :], rn[k % 2], ALU.mult).then_inc(scaled, 1)

        @block.vector
        def _(dve):
            for k in range(KT + 2):
                if k < KT:
                    dve.wait_ge(mean, k + 1)
                    nc.vector.scalar_tensor_tensor(halves(centred[:, k, :]), c.pair[k % 2], -1.0 / HD, halves(o[:, k, :]),
                                                   ALU.mult, ALU.add).then_inc(centred_ready, 1)
                if 1 <= k < KT + 1:
                    dve.wait_ge(var, k)
                    if k >= 3:
                        dve.wait_ge(scaled, k - 2)
                    nc.vector.tensor_scalar(halves(rn[(k - 1) % 2]), c.pair[2 + (k - 1) % 2], 1.0 / HD, GN_EPS,
                                            ALU.mult, ALU.add).then_inc(var_read, 1)
                if 1 <= k < KT + 1:
                    dve.wait_ge(roots, k)
                    nc.vector.reciprocal(rn[(k - 1) % 2], rn[(k - 1) % 2]).then_inc(inverted, 1)
                if k >= 2:
                    j = k - 2
                    dve.wait_ge(scaled, j + 1)
                    nc.vector.scalar_tensor_tensor(o[:, j, :], normed[:, j, :], c.vec("lnw", j), bonus[:, j, :],
                                                   ALU.mult, ALU.add)
                    dve.drain()
                    nc.vector.scalar_tensor_tensor(o[:, j, :], o[:, j, :], c.vec("lnb", j), g[:, j, :],
                                                   ALU.add, ALU.mult)



def route(c, layer):
    nc, io = c.nc, c.io
    x = c.slot(1)
    NTILE, NL, NG, EG = TT + 1, 36, 4, 8
    wr = c.work[:, 0:KT * NL].rearrange("p (k n) -> p k n", n=NL)
    bias = c.work[0:1, 300:300 + NL]
    at = [400]

    def area(*shape):
        n = int(np.prod(shape))
        a = c.work[:, at[0]:at[0] + n]
        at[0] += n
        return a if len(shape) == 1 else a.rearrange("p (a b) -> p a b", b=shape[1])

    rank4, rank8 = area(NG), area(EG)
    L = area(NTILE, NL)
    gmax, gexp, gsum, gkey, gtop = area(NTILE, 1), area(NTILE, NG), area(NTILE, 1), area(NTILE, NG), area(NTILE, 1)
    ghot, picked, part = area(NTILE, NG), area(NTILE, EG), area(NTILE, EG)
    m1, m2, k1, h1, h2 = area(NTILE, 1), area(NTILE, 1), area(NTILE, EG), area(NTILE, EG), area(NTILE, EG)
    e2, w1 = area(NTILE, 1), area(NTILE, 1)
    hot = [area(NTILE, E) for _ in range(2)]
    both, place = area(NTILE, E), area(NTILE, E)
    valid, token, before = area(NTILE, 1), area(NTILE, 1), area(P)
    count, jobs_of, start, more = area(E), area(E), area(E), area(E)
    ones = area(E)
    job_id, owner = area(LISTS), area(LISTS)
    cube = area(LISTS * E)[0:1].rearrange("p (j e) -> p j e", e=E)
    row = area(2, NTILE)
    row_u = area(2, NTILE).bitcast(U32)
    entry = area(2 * NTILE * 4).rearrange("p (a n w) -> p a n w", a=2, w=4)
    entry_u = entry.bitcast(U32)
    blank = c.flat(4)[:, 0:LISTS * 4].rearrange("p (j w) -> p j w", w=4)
    rows = c.flat(2, 2)[:, 0:NTILE * D].rearrange("p (n e) -> p n e", e=D)
    job_float = area(LISTS)
    lists = c.lists.rearrange("(j p) w -> p j w", p=P)
    wide = lambda a, n: a.to_broadcast([P, NTILE, n])
    with c.stage(f"route{layer}") as st:
        loaded, logits, differences, exps = (st.sem(n) for n in (
            "router_loaded", "logits_in_psum", "differences_ready", "exponentials_ready"))
        turned, moved, stored, blanked = (st.sem(n) for n in ("tokens_turned", "tokens_moved", "rows_stored",
                                                              "lists_blank"))
        chosen, counted, placed, listed = (st.sem(n) for n in ("choices_ready", "places_in_psum", "entries_ready",
                                                               "entries_listed"))
        block = st.block()

        @block.sync
        def _(sp):
            sp.dma_start(wr[:, :, 0:NG], io["moe_wrg"][layer].rearrange("(k p) n -> p k n", p=P)).then_inc(loaded, 16)
            sp.dma_start(wr[:, :, NG:NL], io["moe_wre"][layer].rearrange("(k p) n -> p k n", p=P)).then_inc(loaded, 16)
            sp.dma_start(bias[:, 0:NG], io["moe_brg"][layer:layer + 1, :]).then_inc(loaded, 16)
            sp.dma_start(bias[:, NG:NL], io["moe_bre"][layer:layer + 1, :]).then_inc(loaded, 16)
            for dst, name in ((rank4, "rank4"), (rank8, "rank8"), (valid, "valid"), (token, "token"),
                              (before, "triangle"), (job_id, "jobid")):
                sp.dma_start(dst, io["consts"][:, CCOL[name][0]:CCOL[name][1]]).then_inc(loaded, 16)
            sp.wait_ge(blanked, 1)
            sp.dma_start(lists, blank.bitcast(U32)).then_inc(stored, 16)
            sp.wait_ge(moved, 2 * NTILE)
            sp.dma_start(c.token_rows[0:TP].rearrange("(n p) e -> p n e", p=P), rows[:, 0:TT]).then_inc(stored, 16)
            sp.dma_start(c.token_rows[TP:NT], rows[0:NB, TT]).then_inc(stored, 16)
            sp.wait_ge(listed, 16 * 2 * NTILE)
            sp.dma_start(c.job_lists, lists).then_inc(stored, 16)
            sp.wait_ge(stored, 64)

        @block.gpsimd
        def _(pool):
            pool.wait_ge(placed, 1)
            pool.wait_ge(stored, 16 * 3)
            for n in range(NTILE):
                m = P if n < TT else NB
                for a in range(2):
                    nc.gpsimd.indirect_dma_start(
                        out=c.lists, out_offset=bass.IndirectOffsetOnAxis(ap=row_u[0:m, a, n:n + 1], axis=0),
                        in_=entry_u[0:m, a, n, :], in_offset=None,
                        bounds_check=LISTS * P - 1, oob_is_err=True).then_inc(listed, 16)

        @block.tensor
        def _(pe):
            pe.wait_ge(loaded, 16 * 10)
            for n in range(NTILE):
                m = P if n < TT else NB
                out = c.bank[0][0:m, NL * n:NL * n + NL]
                for k in range(KT):
                    nc.tensor.matmul(out, x[:, k, P * n:P * n + m], wr[:, k, :], start=(k == 0), stop=False)
                last = nc.tensor.matmul(out, c.ones[0:1, 0:m], bias, start=False, stop=True)
            last.then_inc(logits, 1)
            for n in range(NTILE):
                m = P if n < TT else NB
                if n >= 2:
                    pe.wait_ge(moved, 2 * (n - 1))
                for k in range(KT):
                    last = nc.tensor.transpose(c.bank[(1, 5)[n % 2] + k // 4][0:m, P * (k % 4):P * (k % 4) + P],
                                               x[:, k, P * n:P * n + m], c.ident)
                last.then_inc(turned, 1)
            pe.wait_ge(chosen, 1)
            for n in range(NTILE):
                for m in range(n + 1):
                    nc.tensor.matmul(c.bank[3][:, E * n:E * n + E], c.ones if m < n else before, both[:, m, :],
                                     start=(m == 0), stop=(m == n))
            for n in range(NTILE):
                last = nc.tensor.matmul(c.bank[4][:, 0:E], c.ones, both[:, n, :], start=(n == 0),
                                        stop=(n == NTILE - 1))
            last.then_inc(counted, 1)

        @block.scalar
        def _(act):
            def move(*tiles):
                for n in tiles:
                    m = P if n < TT else NB
                    act.wait_ge(turned, n + 1)
                    for a in range(2):
                        nc.scalar.copy(rows[0:m, n, 512 * a:512 * a + 512],
                                       c.bank[(1, 5)[n % 2] + a][0:m, :]).then_inc(moved, 1)

            act.wait_ge(differences, 1)
            nc.scalar.activation(gexp, gkey, ACT.Exp).then_inc(exps, 1)
            move(0, 1)
            act.wait_ge(differences, 2)
            nc.scalar.activation(e2, m2, ACT.Exp).then_inc(exps, 1)
            move(*range(2, NTILE))

        @block.vector
        def _(dve):
            tt, ts = nc.vector.tensor_tensor, nc.vector.tensor_scalar
            reduce = nc.vector.tensor_reduce
            nc.vector.memset(L, 0.0)
            blank_u = blank.bitcast(U32)
            nc.vector.memset(blank, 0.0)
            nc.vector.memset(job_float, float(1 << 20))
            dve.drain()
            for w in range(2):
                nc.vector.tensor_copy(blank_u[:, :, w], job_float)
            dve.drain().then_inc(blanked, 1)
            dve.wait_ge(logits, 1)
            dve.drain()
            nc.vector.tensor_copy(L[:, 0:TT, :], c.bank[0][:, 0:TT * NL].rearrange("p (a b) -> p a b", b=NL))
            nc.vector.tensor_copy(L[0:NB, TT, :], c.bank[0][0:NB, TT * NL:NTILE * NL])
            dve.drain()
            lg = L[:, :, 0:NG]
            reduce(gmax, lg, AX.X, ALU.max)
            dve.drain()
            tt(gkey, lg, wide(gmax, NG), ALU.subtract)
            dve.drain().then_inc(differences, 1)
            dve.wait_ge(exps, 1)
            reduce(gsum, gexp, AX.X, ALU.add)

            def first_of(hot, values, top, rank, n, key):
                tt(key, values, wide(top, n), ALU.is_equal)
                dve.drain()
                tt(key, key, rank.unsqueeze(1).to_broadcast([P, NTILE, n]), ALU.mult)
                dve.drain()
                reduce(gtop, key, AX.X, ALU.max)
                dve.drain()
                tt(hot, key, wide(gtop, n), ALU.is_equal)
                dve.drain()

            first_of(ghot, lg, gmax, rank4, NG, gkey)
            for g in range(NG):
                dst = picked if g == 0 else part
                tt(dst, L[:, :, NG + EG * g:NG + EG * g + EG], wide(ghot[:, :, g:g + 1], EG), ALU.mult)
                dve.drain()
                if g:
                    tt(picked, picked, part, ALU.add)
                    dve.drain()
            reduce(m1, picked, AX.X, ALU.max)
            dve.drain()
            first_of(h1, picked, m1, rank8, EG, k1)
            nc.vector.scalar_tensor_tensor(part, h1, NEG, picked, ALU.mult, ALU.add)
            dve.drain()
            reduce(m2, part, AX.X, ALU.max)
            dve.drain()
            first_of(h2, part, m2, rank8, EG, k1)
            tt(m2, m2, m1, ALU.subtract)
            dve.drain().then_inc(differences, 1)
            dve.wait_ge(exps, 2)
            ts(w1, e2, 1.0, None, ALU.add)
            dve.drain()
            tt(w1, w1, gsum, ALU.mult)
            dve.drain()
            nc.vector.reciprocal(w1, w1)
            dve.drain()
            tt(e2, e2, w1, ALU.mult)
            dve.drain()
            for a, h in ((0, h1), (1, h2)):
                for g in range(NG):
                    tt(hot[a][:, :, EG * g:EG * g + EG], h, wide(ghot[:, :, g:g + 1], EG), ALU.mult)
                dve.drain()
                tt(hot[a], hot[a], wide(valid, E), ALU.mult)
            dve.drain()
            tt(both, hot[0], hot[1], ALU.add)
            dve.drain().then_inc(chosen, 1)
            for a, w in ((0, w1), (1, e2)):
                nc.vector.tensor_copy(entry_u[:, a, :, 0:1], token)
                ts(row[:, a, :].unsqueeze(2), token, 2.0, float(a), ALU.mult, ALU.add)
                nc.vector.tensor_copy(entry[:, a, :, 2:3], w)
                nc.vector.memset(entry[:, a, :, 3:4], 0.0)
                dve.drain()
                nc.vector.tensor_copy(entry_u[:, a, :, 1:2], row[:, a, :].unsqueeze(2))
            nc.vector.memset(ones, 1.0)
            dve.wait_ge(counted, 1)
            nc.vector.tensor_copy(count, c.bank[4][:, 0:E])
            dve.drain()
            ts(jobs_of, count, 0.0, None, ALU.is_gt)
            for m in range(1, NTILE):
                ts(more, count, float(P * m), None, ALU.is_gt)
                dve.drain()
                tt(jobs_of, jobs_of, more, ALU.add)
                dve.drain()
            nc.vector.tensor_tensor_scan(start, ones, jobs_of, 0.0, ALU.mult, ALU.add)
            dve.drain()
            tt(start, start, jobs_of, ALU.subtract)
            dve.drain()
            tt(cube, start[0:1].unsqueeze(1).to_broadcast([1, LISTS, E]),
               job_id[0:1].unsqueeze(2).to_broadcast([1, LISTS, E]), ALU.is_le)
            ts(more, start, float(P), None, ALU.mult)
            dve.drain()
            reduce(owner[0:1], cube, AX.X, ALU.add)
            tt(place, c.bank[3][:, 0:NTILE * E].rearrange("p (n e) -> p n e", e=E),
               more.unsqueeze(1).to_broadcast([P, NTILE, E]), ALU.add)
            dve.drain()
            ts(owner[0:1], owner[0:1], -1.0, None, ALU.add)
            for a in range(2):
                tt(both, place, hot[a], ALU.mult)
                dve.drain()
                reduce(row[:, a, :].unsqueeze(2), both, AX.X, ALU.add)
                dve.drain()
            nc.vector.tensor_copy(c.job_expert, owner[0:1])
            nc.vector.tensor_copy(row_u, row)
            dve.drain().then_inc(placed, 1)



def experts(c, layer):
    nc, io = c.nc, c.io
    U = 4
    FT = FE // P
    wbuf = [c.flat(4, 6)[:, 6144 * u:6144 * (u + 1)] for u in range(U)]
    wgu = [b[:, 0:4096].rearrange("p (k n) -> p k n", n=2 * FE) for b in wbuf]
    wd = [b[:, 4096:6144].rearrange("p (f n) -> p f n", n=D) for b in wbuf]
    at = [0]

    def two(n):
        at[0] += 2 * n
        assert at[0] <= 8320
        return [c.work[:, at[0] - n * (2 - v):at[0] - n * (1 - v)] for v in range(2)]

    xg, xt = two(D), [a.rearrange("p (k t) -> p k t", t=P) for a in two(D)]
    y = [c.flat(2)[:, D * u:D * u + D] for u in range(U)]
    silu, hid, ht = two(FE), two(FE), [a.rearrange("p (f t) -> p f t", t=P) for a in two(FE)]
    now, token = two(2) + two(2), [a.bitcast(U32) for a in two(1) + two(1)]
    now_u = [a.bitcast(U32) for a in now]
    src = {"g": io["moe_wgate"][layer].rearrange("g e d f -> (g e) d f"),
           "u": io["moe_wup"][layer].rearrange("g e d f -> (g e) d f"),
           "d": io["moe_wdown"][layer].rearrange("g e f d -> (g e) f d")}

    with c.stage(f"experts{layer}") as st:
        up_ready = [st.sem(f"gate_up_loaded{u}") for u in range(U)]
        down_ready = [st.sem(f"down_loaded{u}") for u in range(U)]
        gathered = [st.sem(f"tokens_gathered{v}") for v in range(2)]
        scattered = [st.sem(f"rows_scattered{u}") for u in range(U)]
        cleared, indexed, staged, silu_ready = (st.sem(n) for n in ("token_buffers_cleared", "indices_ready",
                                                                    "entries_staged", "silu_ready"))
        start = {"tokens_turned": 2, "tokens_ready": 1, "gate_up_in_psum": 2, "hidden_ready": 2,
                 "hidden_turned": 2, "hidden_turned_ready": 1, "rows_in_psum": U, "rows_ready": 1}
        sems = {n: st.sem(n, s) for n, s in start.items()}
        block = st.block()

        def done(eng, name, i, w, back=0):
            eng.wait_ge(sems[name], i * U + (w + 1 - back + start[name]))

        @block.sync
        def _(sp):
            def load(i, w):
                u = w % U
                e = sp.value_load(c.job_expert[0:1, ds(i * U + w, 1)], min_val=0, max_val=E - 1)
                done(sp, "rows_in_psum", i, w, U)
                for n, a in enumerate("gu"):
                    sp.dma_start(wgu[u][:, :, FE * n:FE * n + FE],
                                 src[a][ds(e, 1)].rearrange("a (k p) n -> p (a k) n", p=P)).then_inc(up_ready[u], 16)
                sp.dma_start(wd[u], src["d"][ds(e, 1)].rearrange("a (k p) n -> p (a k) n",
                                                                 p=P)).then_inc(down_ready[u], 16)

            load(0, 0)
            with sp.Fori(0, JOBS // U) as i:
                for u in range(U):
                    load(i, u + 1)
            sp.wait_ge(up_ready[0], 32 * (JOBS // U + 1))
            sp.wait_ge(down_ready[0], 16 * (JOBS // U + 1))

        @block.gpsimd
        def _(pool):
            def fetch(i, w):
                u, v = w % U, w % 2
                done(pool, "tokens_turned", i, w, 2)
                nc.gpsimd.tensor_copy(token[u], c.job_lists[:, ds(i * U + w, 1), 0:1].rearrange(
                    "p a w -> p (a w)")).then_inc(indexed, 1)
                pool.wait_ge(indexed, i * U + (w + 1))
                pool.nop(nofuse=True)
                nc.gpsimd.indirect_dma_start(
                    out=xg[v], out_offset=None, in_=c.token_rows,
                    in_offset=bass.IndirectOffsetOnAxis(ap=token[u], axis=0),
                    bounds_check=NT - 1, oob_is_err=False).then_inc(gathered[v], 16)

            def stage(i, w):
                u = w % U
                scatters = i + w // U - 1
                if not isinstance(scatters, int) or scatters >= 0:
                    pool.wait_ge(scattered[u], scatters * 16 + 16)
                nc.gpsimd.tensor_copy(now_u[u], c.job_lists[:, ds(i * U + w, 1), 1:3].rearrange(
                    "p a w -> p (a w)")).then_inc(staged, 1)

            def send(i, w):
                u = w % U
                done(pool, "rows_ready", i, w)
                pool.nop(nofuse=True)
                nc.gpsimd.indirect_dma_start(
                    out=c.expert_rows, out_offset=bass.IndirectOffsetOnAxis(ap=now_u[u][:, 0:1], axis=0),
                    in_=y[u], in_offset=None,
                    bounds_check=2 * NT - 1, oob_is_err=False).then_inc(scattered[u], 16)

            pool.wait_ge(cleared, 1)
            fetch(0, 0)
            fetch(0, 1)
            fetch(0, 2)
            stage(0, 0)
            for u in range(U):
                fetch(0, u + 3)
                send(0, u)
                stage(0, u + 1)
            with pool.Fori(1, JOBS // U - 1) as i:
                for u in range(U):
                    fetch(i, u + 3)
                    send(i, u)
                    stage(i, u + 1)
            last = JOBS // U - 1
            for u in range(U):
                if last * U + u + 3 < LISTS:
                    fetch(last, u + 3)
                send(last, u)
                if u < U - 1:
                    stage(last, u + 1)
            for u in range(U):
                pool.wait_ge(scattered[u], 16 * JOBS // U)
            for v in range(2):
                pool.wait_ge(gathered[v], 16 * LISTS // 2)

        @block.tensor
        def _(pe):
            mm, tr = nc.tensor.matmul, nc.tensor.transpose

            def turn_tokens(i, w):
                v = w % 2
                pe.wait_ge(gathered[v], (i * (U // 2) + (w // 2 + 1)) * 16)
                done(pe, "tokens_ready", i, w, 1)
                for k in range(KT):
                    last = tr(c.bank[2 + k // 4][:, P * (k % 4):P * (k % 4) + P], xg[v][:, P * k:P * k + P], c.ident)
                last.then_inc(sems["tokens_turned"], 1)

            def gate_up(i, w):
                u, v = w % U, w % 2
                pe.wait_ge(up_ready[u], (i + (w // U + 1)) * 32)
                done(pe, "tokens_ready", i, w)
                done(pe, "hidden_ready", i, w, 2)
                for k in range(KT):
                    last = mm(c.bank[v], xt[v][:, k, :], wgu[u][:, k, :], start=(k == 0), stop=(k == KT - 1))
                last.then_inc(sems["gate_up_in_psum"], 1)

            turn_tokens(0, 0)
            turn_tokens(0, 1)
            gate_up(0, 0)
            with pe.Fori(0, JOBS // U) as i:
                for u in range(U):
                    v = u % 2
                    done(pe, "hidden_ready", i, u)
                    done(pe, "hidden_turned_ready", i, u, 1)
                    for f in range(FT):
                        last = tr(c.bank[4][:, P * f:P * f + P], hid[v][:, P * f:P * f + P], c.ident)
                    last.then_inc(sems["hidden_turned"], 1)
                    gate_up(i, u + 1)
                    turn_tokens(i, u + 2)
                    pe.wait_ge(down_ready[u], i * 16 + 16)
                    done(pe, "hidden_turned_ready", i, u)
                    done(pe, "rows_ready", i, u, 1)
                    for a in range(2):
                        for f in range(FT):
                            last = mm(c.bank[5 + a], ht[v][:, f, :], wd[u][:, f, 512 * a:512 * a + 512],
                                      start=(f == 0), stop=(f == FT - 1))
                    last.then_inc(sems["rows_in_psum"], 1)

        @block.scalar
        def _(act):
            def tokens(i, w):
                v = w % 2
                done(act, "tokens_turned", i, w)
                done(act, "gate_up_in_psum", i, w, 2)
                for a in range(2):
                    nc.scalar.copy(xt[v][:, 4 * a:4 * a + 4, :], c.bank[2 + a].rearrange("p (k t) -> p k t", t=P))
                act.drain().then_inc(sems["tokens_ready"], 1)

            def gate(i, w):
                v = w % 2
                done(act, "gate_up_in_psum", i, w)
                done(act, "hidden_ready", i, w, 2)
                nc.scalar.activation(silu[v], c.bank[v][:, 0:FE], ACT.Silu).then_inc(silu_ready, 1)

            tokens(0, 0)
            tokens(0, 1)
            gate(0, 0)
            with act.Fori(0, JOBS // U) as i:
                for u in range(U):
                    gate(i, u + 1)
                    tokens(i, u + 2)

        @block.vector
        def _(dve):
            def hidden(i, w):
                v = w % 2
                dve.wait_ge(silu_ready, i * U + (w + 1))
                done(dve, "hidden_turned", i, w, 2)
                nc.vector.tensor_tensor(hid[v], silu[v], c.bank[v][:, FE:2 * FE],
                                        ALU.mult).then_inc(sems["hidden_ready"], 1)

            for v in range(2):
                nc.vector.memset(xg[v], 0.0)
            dve.drain().then_inc(cleared, 1)
            hidden(0, 0)
            with dve.Fori(0, JOBS // U) as i:
                for u in range(U):
                    v = u % 2
                    done(dve, "hidden_turned", i, u)
                    done(dve, "rows_in_psum", i, u, 2)
                    nc.vector.tensor_copy(ht[v], c.bank[4][:, 0:FE].rearrange("p (f t) -> p f t", t=P)).then_inc(
                        sems["hidden_turned_ready"], 1)
                    hidden(i, u + 1)
                    done(dve, "rows_in_psum", i, u)
                    dve.wait_ge(staged, i * U + (u + 1))
                    for a in range(2):
                        nc.vector.tensor_scalar(y[u][:, 512 * a:512 * a + 512], c.bank[5 + a], now[u][:, 1:2], None,
                                                ALU.mult)
                    dve.drain().then_inc(sems["rows_ready"], 1)


def combine(c, layer):
    nc = c.nc
    h, NTILE = c.slot(0), TT + 1
    rows = c.flat(2, 3)[:, 0:NTILE * 2 * D].rearrange("p (n a e) -> p n a e", a=2, e=D)
    with c.stage(f"combine{layer}") as st:
        loaded = [st.sem(f"rows_loaded{n}") for n in range(NTILE)]
        summed, turned, added = st.sem("rows_summed"), st.sem("sums_turned"), st.sem("sums_added")
        block = st.block()

        @block.sync
        def _(sp):
            for n in range(NTILE):
                m = P if n < TT else NB
                two = c.expert_rows[2 * P * n:2 * P * n + 2 * m].rearrange("(p a) e -> p a e", a=2)
                sp.dma_start(rows[0:m, n], two).then_inc(loaded[n], 16)

        @block.tensor
        def _(pe):
            for n in range(NTILE):
                m = P if n < TT else NB
                pe.wait_ge(summed, n + 1)
                if n >= 2:
                    pe.wait_ge(added, 2 * (n - 1))
                for k in range(KT):
                    last = nc.tensor.transpose(c.bank[2 * (n % 2) + k // 4][:, P * (k % 4):P * (k % 4) + m],
                                               rows[0:m, n, 0, P * k:P * k + P], c.ident[0:m, 0:m])
                last.then_inc(turned, 1)

        @block.gpsimd
        def _(pool):
            for n in range(NTILE):
                m = P if n < TT else NB
                pool.wait_ge(loaded[n], 16)
                nc.gpsimd.tensor_tensor(rows[0:m, n, 0, :], rows[0:m, n, 0, :], rows[0:m, n, 1, :],
                                        ALU.add).then_inc(summed, 1)

        @block.vector
        def _(dve):
            for n in range(NTILE):
                m = P if n < TT else NB
                dve.wait_ge(turned, n + 1)
                for a in range(2):
                    o = h[:, 4 * a:4 * a + 4, P * n:P * n + m]
                    src = c.bank[2 * (n % 2) + a].rearrange("p (k t) -> p k t", t=P)[:, :, 0:m]
                    nc.vector.tensor_tensor(o, o, src, ALU.add).then_inc(added, 1)


def mixture(c, layer):
    rms_norm(c, c.slot(0), f"ffn{layer}", c.slot(1), c.slot(3))
    route(c, layer)
    experts(c, layer)
    combine(c, layer)



NSTR = 6
KVW = NSTR * KVH * HD
KVT = KVW // P
RW = KVH * HD


def rotate(c, name, src, dst, tiles):
    nc, io = c.nc, c.io
    cos, sin = c.work[:, 0:NT], c.work[:, NT:2 * NT]
    swap = c.work[:, 2 * NT:2 * NT + P]
    parts = [c.work[:, 1200 + NT * n:1200 + NT * (n + 1)] for n in range(2)]
    halves = lambda a: a.rearrange("p (s t) -> p s t", s=2)
    with c.stage(name) as st:
        loaded, full, taken = st.sem("tables_loaded"), st.sem("partners_in_psum"), st.sem("partners_taken")
        block = st.block()

        @block.sync
        def _(sp):
            for dst_, n in ((cos, "cos"), (sin, "sin"), (swap, "swap")):
                sp.dma_start(dst_, io["consts"][:, CCOL[n][0]:CCOL[n][1]]).then_inc(loaded, 16)

        @block.tensor
        def _(pe):
            pe.wait_ge(loaded, 48)
            for x, m in enumerate(tiles):
                if x >= 4:
                    pe.wait_ge(taken, x - 3)
                for s in range(2):
                    last = nc.tensor.matmul(c.pair[x % 4][:, s, :], swap, src[:, m, HALF * s:HALF * s + HALF],
                                            start=True, stop=True)
                last.then_inc(full, 1)

        @block.vector
        def _(dve):
            dve.wait_ge(loaded, 48)
            for x, m in enumerate(tiles):
                dve.wait_ge(full, x + 1)
                part = parts[x % 2]
                nc.vector.tensor_tensor(halves(part), c.pair[x % 4], halves(sin), ALU.mult).then_inc(taken, 1)
                nc.vector.tensor_tensor(dst[:, m, :], src[:, m, :], cos, ALU.mult)
                dve.drain()
                nc.vector.tensor_tensor(dst[:, m, :], dst[:, m, :], part, ALU.add)


def kv_rows(c):
    nc, io = c.nc, c.io
    kv = c.flat(2, 2)[:, 0:KVT * NT].rearrange("p (k t) -> p k t", t=NT)
    rows = c.flat(4, 2)[:, 0:(TT + 1) * KVW].rearrange("p (n e) -> p n e", e=KVW)
    with c.stage("kv_rows") as st:
        turned, moved, stored = st.sem("rows_in_psum"), st.sem("rows_moved"), st.sem("rows_stored")
        block = st.block()
        jobs = [(n, a) for n in range(TT + 1) for a in range(3)]

        @block.tensor
        def _(pe):
            for x, (n, a) in enumerate(jobs):
                m = P if n < TT else NB
                if x >= 8:
                    pe.wait_ge(moved, x - 7)
                for k in range(4):
                    last = nc.tensor.transpose(c.bank[x % 8][0:m, P * k:P * k + P],
                                               kv[:, 4 * a + k, P * n:P * n + m], c.ident)
                last.then_inc(turned, 1)

        @block.vector
        def _(dve):
            nc.vector.tensor_copy(c.kv_sample, kv[:, :, TP:NT])
            for x, (n, a) in enumerate(jobs):
                m = P if n < TT else NB
                dve.wait_ge(turned, x + 1)
                nc.vector.tensor_copy(rows[0:m, n, 512 * a:512 * a + 512], c.bank[x % 8][0:m, :]).then_inc(moved, 1)

        @block.sync
        def _(sp):
            stores = 0
            for n in range(TT):
                sp.wait_ge(moved, 3 * (n + 1))
                sp.dma_start(io["o_prompt_rows"][0, P * n:P * n + P].rearrange("t s g d -> t (s g d)"),
                             rows[:, n, 0:4 * RW]).then_inc(stored, 16)
                sp.dma_start(io["o_prompt_win"][0, P * n:P * n + P].rearrange("t s g d -> t (s g d)"),
                             rows[:, n, 4 * RW:KVW]).then_inc(stored, 16)
                stores += 2
            sp.wait_ge(moved, len(jobs))
            sp.dma_start(io["o_sample_rows"][:, 0].rearrange("b s g d -> b (s g d)"),
                         rows[0:NB, TT, 0:4 * RW]).then_inc(stored, 16)
            sp.dma_start(io["o_sample_win"][:, WIN - 1].rearrange("b s g d -> b (s g d)"),
                         rows[0:NB, TT, 4 * RW:KVW]).then_inc(stored, 16)
            for a, stream in ((0, 2), (1, 4)):
                for q in range(2):
                    sp.dma_start(c.prompt_keys[0:HD, a, q:KVH:2, :],
                                 kv[HD * q:HD * q + HD, 2 * stream:2 * stream + 2, 0:TP]).then_inc(stored, 16)
            sp.wait_ge(stored, 16 * (stores + 2 + 4))


def load_compression(c, sp, w1, w2, pe_rows, b1, done):
    io = c.io
    for kv in range(2):
        sp.dma_start(w1[:, kv], io["cmp_w1"][kv].rearrange("(j p) n -> p j n", p=P)).then_inc(done, 16)
        sp.dma_start(w2[:, kv, :], io["cmp_w2"][kv]).then_inc(done, 16)
        sp.dma_start(pe_rows[:, kv, :], io["cmp_pe"][kv].rearrange("(j a) d -> j (a d)", a=2)).then_inc(done, 16)
        sp.dma_start(b1[:, kv:kv + 1], io["cmp_b1"][kv].rearrange("(c a) -> c a", a=1)).then_inc(done, 16)
    return 16 * 8


def by_parity(copy, dst, src, done):
    for q in range(2):
        for par in range(2):
            s = src[HD * q:HD * q + HD].rearrange("p v (n j a) -> p v j n a", j=8, a=2)[:, :, :, :, par]
            copy(dst[HD * par:HD * par + HD, q:2 * KVH:2, :, :], s).then_inc(done, 1)


def compress_prompt(c):
    nc, io = c.nc, c.io
    w1 = c.flat(6)[:, 0:4096].rearrange("p (a j n) -> p a j n", a=2, j=16)
    w2 = c.work[:, 0:2 * HD].rearrange("p (a d) -> p a d", a=2)
    pe_rows = c.work[0:16, 128:384].rearrange("p (a d) -> p a d", a=2)
    b1, pe_cols = c.work[:, 384:386], c.work[:, 386:418].rearrange("p (a j) -> p a j", a=2)
    kv_t = c.flat(2, 2)[:, 0:KVT * NT].rearrange("p (k t) -> p k t", t=NT)
    XT = c.work[:, 2560:2560 + 2048].rearrange("p (v x n) -> p v x n", v=2 * KVH, x=8)
    XV = [c.work[:, 2560 + 1024 * v:2560 + 1024 * (v + 1)].rearrange("p (g j n) -> p g j n", g=KVH, j=8)
          for v in range(2)]
    G = [c.work[:, 4608 + 128 * v:4608 + 128 * v + KVH * NCMP_P].rearrange("p (g n) -> p g n", g=KVH)
         for v in range(2)]
    with c.stage("compress_prompt") as st:
        loaded, pe_in, pe_out, bias_in, bias_out = (st.sem(n) for n in (
            "weights_loaded", "encoding_turned", "encoding_moved", "bias_in_psum", "bias_ready"))
        moved, hid_in, hid_out, out_in = (st.sem(n) for n in (
            "pairs_moved", "hidden_in_psum", "hidden_ready", "outputs_in_psum"))
        block = st.block()

        @block.sync
        def _(sp):
            load_compression(c, sp, w1, w2, pe_rows, b1, loaded)

        @block.tensor
        def _(pe):
            pe.wait_ge(loaded, 16 * 8)
            for v in range(2):
                last = nc.tensor.transpose(c.bank[0][:, 16 * v:16 * v + 16], pe_rows[:, v, :], c.ident[0:16, 0:16])
            last.then_inc(pe_in, 1)
            pe.wait_ge(pe_out, 1)
            for v in range(2):
                for j in range(16):
                    last = nc.tensor.matmul(c.bank[5][:, v:v + 1], w1[:, v, j, :], pe_cols[:, v, j:j + 1],
                                            start=(j == 0), stop=(j == 15))
            last.then_inc(bias_in, 1)
            pe.wait_ge(moved, 4)
            for v in range(2):
                for j in range(16):
                    first = j // 8
                    last = nc.tensor.matmul(c.bank[6 + v][:, 0:KVH * NCMP_P], w1[:, v, j, :],
                                            XV[v][:, :, j % 8, first:first + NCMP_P], start=(j == 0), stop=(j == 15))
            last.then_inc(hid_in, 1)
            pe.wait_ge(hid_out, 2)
            nc.tensor.matmul(c.bank[0][0:HD, 0:KVH * NCMP_P], w2[:, 0, :], G[0], start=True, stop=True)
            for g in range(KVH):
                last = nc.tensor.matmul(c.bank[1][0:NCMP_P, HD * g:HD * g + HD], G[1][:, g, :], w2[:, 1, :],
                                        start=True, stop=True)
            last.then_inc(out_in, 1)

        @block.vector
        def _(dve):
            nc.vector.memset(c.cmp_keys, 0.0)
            nc.vector.memset(c.cmp_values, 0.0)
            dve.drain()
            dve.wait_ge(pe_in, 1)
            nc.vector.tensor_copy(pe_cols, c.bank[0][:, 0:32].rearrange("p (a j) -> p a j", a=2)).then_inc(pe_out, 1)
            by_parity(nc.vector.tensor_copy, XT, kv_t[:, 0:4, 0:TP], moved)
            dve.wait_ge(bias_in, 1)
            nc.vector.tensor_tensor(c.cmp_bias, c.bank[5][:, 0:2], b1, ALU.add).then_inc(bias_out, 1)
            dve.wait_ge(out_in, 1)
            nc.vector.tensor_copy(c.cmp_keys[0:HD], c.bank[0][0:HD, 0:KVH * NCMP_P].rearrange("p (g n) -> p g n", g=KVH))
            nc.vector.tensor_copy(c.cmp_values[0:NCMP_P, :], c.bank[1][0:NCMP_P, 0:RW])

        @block.scalar
        def _(act):
            act.wait_ge(hid_in, 1)
            act.wait_ge(bias_out, 1)
            for v in range(2):
                nc.scalar.activation(G[v], c.bank[6 + v][:, 0:KVH * NCMP_P].rearrange("p (g n) -> p g n", g=KVH),
                                     ACT.Gelu_apprx_tanh, bias=c.cmp_bias[:, v:v + 1]).then_inc(hid_out, 1)



def gates(c):
    nc, io = c.nc, c.io
    x, NGATE = c.slot(1), 3 * NH
    w = c.work[:, 0:KT * NGATE].rearrange("p (k n) -> p k n", n=NGATE)
    with c.stage("gates") as st:
        loaded, full, ready, stored = (st.sem(n) for n in ("weight_loaded", "gates_in_psum", "gates_ready", "stored"))
        cleared = st.sem("rows_cleared")
        block = st.block()

        @block.gpsimd
        def _(pool):
            nc.gpsimd.memset(c.gate, 0.0).then_inc(cleared, 1)

        @block.sync
        def _(sp):
            sp.dma_start(w, io["nsa_wqg"][0][:, D:D + NGATE].rearrange("(k p) n -> p k n", p=P)).then_inc(loaded, 16)
            sp.wait_ge(ready, 1)
            sp.dma_start(c.gate_rows, c.gate[0:NB, TT, :]).then_inc(stored, 16)
            sp.wait_ge(stored, 16)

        @block.tensor
        def _(pe):
            pe.wait_ge(loaded, 16)
            for n in range(TT + 1):
                m = P if n < TT else NB
                for k in range(KT):
                    last = nc.tensor.matmul(c.bank[0][0:m, NGATE * n:NGATE * n + NGATE], x[:, k, P * n:P * n + m],
                                            w[:, k, :], start=(k == 0), stop=(k == KT - 1))
            last.then_inc(full, 1)

        @block.scalar
        def _(act):
            act.wait_ge(cleared, 1)
            act.wait_ge(full, 1)
            nc.scalar.activation(c.gate[:, 0:TT, :], c.bank[0][:, 0:TT * NGATE].rearrange("p (a b) -> p a b", b=NGATE),
                                 ACT.Sigmoid)
            nc.scalar.activation(c.gate[0:NB, TT, :], c.bank[0][0:NB, TT * NGATE:(TT + 1) * NGATE], ACT.Sigmoid)
            act.drain().then_inc(ready, 1)


def prompt_attention(c):
    nc, io = c.nc, c.io
    q_plain, q_rot = c.slot(6), c.slot(7)
    rows = c.flat(4, 2)[:, 0:(TT + 1) * KVW].rearrange("p (n e) -> p n e", e=KVW)
    out = c.flat(1)[:, 0:TT * D].rearrange("p (n e) -> p n e", e=D)
    lo, hi = CCOL["cmpfar"][0], CCOL["cmpone"][1]
    NK = NCMP_P
    work, at = c.work, [0]

    def area(n):
        at[0] += n
        return work[:, at[0] - n:at[0]]

    masks, causal = area(hi - lo), area(P)
    far, one = (masks[:, x * TT * NK:(x + 1) * TT * NK].rearrange("p (n k) -> p n k", k=NK) for x in range(2))
    queries = [area(4 * TP).rearrange("p (r t) -> p r t", t=TP)[0:HD] for _ in range(2)]
    prob = [area(TP) for _ in range(4)]
    turned_sb = [area(TP) for _ in range(3)]
    top, total, coef = area(64), area(64), area(64)
    CMP, SEL, WINB = range(3)
    jobs = [(r, b, n) for r in range(4) for n in (3, 0, 2, 1) for b in (CMP, SEL, WINB)]
    NJ = len(jobs)
    unseen = lambda b, n: b == CMP and n == 0
    width = lambda b, n: NK if b == CMP else P * (n + 1)
    STREAM = {SEL: 3, WINB: 5}
    with c.stage("prompt_attention") as st:
        loaded, q_ready = st.sem("tables_loaded"), st.sem("queries_ready")
        topped, score_free = st.sem("maximum_ready"), st.sem("scores_used")
        scored, expd, p_in, p_out, mixed, added = (st.sem(n, 1) for n in (
            "scores_in_psum", "probabilities_ready", "turned_in_psum", "turned_ready", "output_in_psum",
            "output_added"))
        block = st.block()
        S = [c.bank[x] for x in range(4)]
        Tb = [c.bank[4], c.bank[5]]
        O = [c.bank[6], c.bank[7]]

        @block.sync
        def _(sp):
            sp.dma_start(masks, io["consts"][:, lo:hi]).then_inc(loaded, 16)
            sp.dma_start(causal, io["consts"][:, CCOL["causal"][0]:CCOL["causal"][1]]).then_inc(loaded, 16)

        def queries_of(src, odd, i):
            return src[HD * odd:HD * odd + HD, ds(i * 2, 2), 0:TP]

        @block.tensor
        def _(pe):
            pe.wait_ge(loaded, 32)
            with pe.Fori(0, KVH) as i:
                pe.wait_ge(added, i * NJ + 1)
                warm_up(c, O[1], 10)
                pe.wait_ge(q_ready, i * 4 + 4)
                for x in range(NJ + 4):
                    if x < NJ:
                        r, b, n = jobs[x]
                        q = queries[0 if b == CMP else 1][:, r, P * n:P * n + P]
                        keys = (c.cmp_keys[0:HD, ds(i, 1), :] if b == CMP else
                                c.prompt_keys[0:HD, b - 1, ds(i, 1), 0:P * (n + 1)])
                        pe.wait_ge(expd, i * NJ + max(0, x - 3) + 1)
                        pe.nop(nofuse=True)
                        nc.tensor.matmul(S[x % 4][:, 0:width(b, n)], q, keys.rearrange("p a t -> p (a t)"),
                                         start=True, stop=False)
                        part, mask = ((S[x % 4][:, 0:NK], far[:, n, :]) if b == CMP
                                      else (S[x % 4][:, P * n:P * n + P], causal))
                        nc.tensor.matmul(part, c.ident, mask, start=False, stop=True).then_inc(scored, 1)
                    if 3 <= x < NJ + 3:
                        y = x - 3
                        r, b, n = jobs[y]
                        pe.wait_ge(expd, i * NJ + y + 2)
                        pe.wait_ge(p_out, i * NJ + max(0, y - 1) + 1)
                        if b == CMP:
                            last = nc.tensor.transpose(Tb[y % 2][0:NK, 0:P], prob[y % 4][:, 0:NK], c.ident)
                        else:
                            for s in range(n + 1):
                                last = nc.tensor.transpose(Tb[y % 2][:, P * s:P * s + P],
                                                           prob[y % 4][:, P * s:P * s + P], c.ident)
                        last.then_inc(p_in, 1)
                    if x >= 4:
                        y = x - 4
                        r, b, n = jobs[y]
                        pe.wait_ge(p_out, i * NJ + y + 2)
                        pe.wait_ge(added, i * NJ + max(0, y - 1) + 1)
                        pe.nop(nofuse=True)
                        if b == CMP:
                            last = nc.tensor.matmul(O[y % 2][:, 0:HD], turned_sb[y % 3][0:NK, 0:P],
                                                    c.cmp_values[0:NK, ds(i * HD, HD)], start=True, stop=True)
                        else:
                            for s in range(n + 1):
                                v = rows[:, s, ds(i * HD + STREAM[b] * RW, HD)]
                                last = nc.tensor.matmul(O[y % 2][:, 0:HD], turned_sb[y % 3][:, P * s:P * s + P], v,
                                                        start=(s == 0), stop=(s == n))
                        last.then_inc(mixed, 1)

        @block.scalar
        def _(act):
            with act.Fori(0, KVH) as i:
                for odd in range(2):
                    nc.scalar.activation(queries[1][:, odd:4:2, :], queries_of(q_rot, odd, i), ACT.Copy,
                                         scale=-SCALE).then_inc(q_ready, 1)
                for x in range(NJ + 2):
                    if x < NJ:
                        r, b, n = jobs[x]
                        w = width(b, n)
                        act.wait_ge(topped, i * NJ + x + 1)
                        act.wait_ge(p_in, i * NJ + max(0, x - 3) + 1)
                        act.wait_ge(added, i * NJ + max(0, x - 4) + 1)
                        nc.scalar.activation(prob[x % 4][:, 0:w], S[x % 4][:, 0:w], ACT.Exp, bias=top[:, x:x + 1],
                                             scale=-1.0, accum_out=total[:, x:x + 1])
                        act.drain().then_inc(score_free if unseen(b, n) else expd, 1)
                    if x >= 2:
                        y = x - 2
                        r, b, n = jobs[y]
                        rows_, w = (NK, P) if b == CMP else (P, P * (n + 1))
                        act.wait_ge(p_in, i * NJ + y + 2)
                        act.wait_ge(mixed, i * NJ + max(0, y - 2) + 1)
                        nc.scalar.copy(turned_sb[y % 3][0:rows_, 0:w], Tb[y % 2][0:rows_, 0:w]).then_inc(p_out, 1)

        @block.vector
        def _(dve):
            nc.vector.memset(out, 0.0)
            dve.wait_ge(loaded, 32)
            with dve.Fori(0, KVH) as i:
                for odd in range(2):
                    nc.vector.tensor_scalar(queries[0][:, odd:4:2, :], queries_of(q_plain, odd, i), -SCALE, None,
                                            ALU.mult).then_inc(q_ready, 1)
                seen = 0
                for x in range(NJ + 4):
                    if x < NJ:
                        r, b, n = jobs[x]
                        dve.wait_ge(scored, i * NJ + x + 2)
                        nc.vector.tensor_reduce(top[:, x:x + 1], S[x % 4][:, 0:width(b, n)], AX.X,
                                                ALU.min).then_inc(topped, 1)
                        if unseen(b, n):
                            seen += 1
                            dve.wait_ge(score_free, i * 4 + seen)
                            nc.vector.tensor_tensor(prob[x % 4][:, 0:NK], prob[x % 4][:, 0:NK], one[:, n, :], ALU.mult)
                            dve.drain()
                            nc.vector.tensor_reduce(total[:, x:x + 1], prob[x % 4][:, 0:NK], AX.X, ALU.add)
                            dve.drain()
                            nc.vector.tensor_scalar(total[:, x:x + 1], total[:, x:x + 1], 1e-30, None, ALU.max)
                            dve.drain().then_inc(expd, 1)
                    if x >= 4:
                        y = x - 4
                        r, b, n = jobs[y]
                        if b == CMP:
                            cf = coef[:, y:y + 3]
                            dve.wait_ge(expd, i * NJ + y + 4)
                            nc.vector.reciprocal(cf, total[:, y:y + 3])
                            dve.drain()
                            nc.vector.tensor_tensor(cf, cf, c.gate[:, n, ds(i * 12 + 3 * r, 3)], ALU.mult)
                            dve.drain()
                        dve.wait_ge(mixed, i * NJ + y + 2)
                        o = out[:, n, ds(i * (4 * HD) + r * HD, HD)]
                        nc.vector.scalar_tensor_tensor(o, O[y % 2][:, 0:HD], coef[:, y:y + 1], o, ALU.mult, ALU.add)
                        dve.drain().then_inc(added, 1)

    with c.stage("prompt_mixed") as st:
        turned, moved = st.sem("columns_in_psum"), st.sem("columns_moved")
        block = st.block()

        @block.tensor
        def _(pe):
            for k in range(KT):
                for n in range(TT):
                    last = nc.tensor.transpose(c.bank[k][:, P * n:P * n + P], out[:, n, P * k:P * k + P], c.ident)
                last.then_inc(turned, 1)

        @block.vector
        def _(dve):
            for k in range(KT):
                dve.wait_ge(turned, k + 1)
                nc.vector.tensor_copy(c.slot(9)[:, k, 0:TP], c.bank[k])


def sample_prepare(c):
    nc, io = c.nc, c.io
    rows = c.slot(1)[0:NB, :, :].rearrange("b k t -> b (k t)")[:, 0:2 * D].rearrange("b (a e) -> b a e", a=2)
    s = c.sample
    pages_i = c.flat(8)[:, 0:NB * NPG].bitcast(I32)
    pages_f = c.flat(8)[:, 128:128 + NB * NPG]
    tok = c.flat(8)[:, 256:257]
    with c.stage("sample_prepare") as st:
        loaded, turned, moved, stored = (st.sem(n) for n in ("loaded", "queries_turned", "queries_moved", "stored"))
        weights = st.sem("weights_loaded")
        block = st.block()

        @block.sync
        def _(sp):
            table = io["page_table"].rearrange("(a b) p -> a (b p)", a=1).to_broadcast([P, NB * NPG])
            sp.dma_start(pages_i, table).then_inc(loaded, 16)
            sp.dma_start(tok, io["consts"][:, CCOL["tokrow"][0]:CCOL["tokrow"][1]], allow_slow_non_contiguous=True).then_inc(loaded, 16)
            sp.wait_ge(turned, 1)
            n = load_compression(c, sp, s["w1"], s["w2"], c.flat(8)[0:16, 300:556].rearrange("p (a d) -> p a d", a=2),
                                 c.flat(8)[:, 556:558], weights)
            for name in ("overlap", "samegroup", "notforced", "forced", "earlier", "ownkv", "ownquery"):
                sp.dma_start(s[name], io["consts"][0:s[name].shape[0], CCOL[name][0]:CCOL[name][1]]).then_inc(weights, 16)
                n += 16
            sp.dma_start(s["gate"], c.gate_rows.rearrange("b (h r) -> h b r", r=3)).then_inc(weights, 16)
            sp.wait_ge(weights, n + 16)
            sp.wait_ge(moved, 4)
            sp.dma_start(c.query_rows.rearrange("a b e -> b a e"), rows).then_inc(stored, 16)
            sp.wait_ge(stored, 16)

        @block.tensor
        def _(pe):
            for a in range(2):
                for k in range(KT):
                    last = nc.tensor.transpose(c.bank[2 * a + k // 4][0:NB, P * (k % 4):P * (k % 4) + P],
                                               c.slot(6 + a)[:, k, TP:NT], c.ident)
            last.then_inc(turned, 1)

        @block.vector
        def _(dve):
            dve.wait_ge(loaded, 32)
            nc.vector.tensor_copy(pages_f, pages_i)
            dve.drain()
            nc.vector.tensor_scalar(pages_f, pages_f, float(2 * PAGE), tok, ALU.mult, ALU.add)
            dve.drain()
            nc.vector.tensor_copy(s["index"][:, 1, :], pages_f)
            nc.vector.tensor_scalar(pages_f, pages_f, -1.0, None, ALU.add)
            dve.drain()
            nc.vector.tensor_copy(s["index"][:, 0, :], pages_f)
            dve.wait_ge(turned, 1)
            for a in range(2):
                for k in range(2):
                    nc.vector.tensor_copy(rows[:, a, 512 * k:512 * k + 512], c.bank[2 * a + k][0:NB, :]).then_inc(moved, 1)


def sample_memory(c):
    f, w, at = c.flat, c.work, [0]

    def area(n, rows=P):
        at[0] += n
        assert at[0] <= 8320
        return w[0:rows, at[0] - n:at[0]]

    NSC = NCMP_S + PAST + 1 + WIN
    c.sample = {
        "sel": f(1, 2)[:, 0:NPG * 512].rearrange("p (n e) -> p n e", e=512),
        "xt": f(3, 2)[:, 0:8192].rearrange("p (v j n) -> p v j n", v=2 * KVH, j=8),
        "kt": f(5)[:, 0:2 * PAST].rearrange("p (g t) -> p g t", g=2),
        "w1": f(6)[:, 0:4096].rearrange("p (a j n) -> p a j n", a=2, j=16),
        "cmp": f(7)[:, 0:2048].rearrange("p (n e) -> p n e", e=512),
        "win": f(7)[:, 2048:4096].rearrange("p (n e) -> p n e", e=512),
        "kwt": f(8)[:, 0:1024].rearrange("p (g t) -> p g t", g=2),
        "score": f(8)[0:NH, 1024:1024 + NSC],
        "w2": area(2 * HD).rearrange("p (a d) -> p a d", a=2),
        "index": area(2 * NB * NPG).rearrange("p (a n) -> p a n", a=2).bitcast(U32),
        "now": area(2 * NPG).rearrange("p (a n) -> p a n", a=2).bitcast(U32),
        "hidden": area(2 * KVH * NCMP_S).rearrange("p (a g n) -> p a g n", a=2, g=KVH),
        "kc": area(2 * NCMP_S).rearrange("p (g n) -> p g n", g=2),
        "vc": area(RW, NCMP_S),
        "overlap": area(NSB, NCMP_S), "samegroup": area(NH, NH), "notforced": area(NSB, NH), "forced": area(NSB, NH),
        "earlier": area(NSB * NSB, NH), "ownkv": area(RW, NH), "ownquery": area(2 * NH),
        "gate": area(3 * NB, NH).rearrange("p (b r) -> p b r", r=3),
        "qrow": area(4 * HD, NH).rearrange("p (a x d) -> p a x d", a=2, x=2),
        "vnew": area(RW, 1),
        "rank": area(NSB * NSB, NH), "tie": area(NSB * NSB, NH),
        "imp": area(NSB, NH), "pick": area(NSB, NH),
        "pct": area(NH, NCMP_S), "pt": area((NPG + 1) * NH), "wt": area(4 * NH),
        "acc": area(RW, NH), "head": area(HD, NH), "col": area(16, NH),
    }


def sample_attention(c):
    nc, io = c.nc, c.io
    s = c.sample
    cache = io["cache_kv"].rearrange("n t (a s) g d -> (n t a) (s g d)", a=2)
    sc_cmp, sc_sel = s["score"][:, 0:NCMP_S], s["score"][:, NCMP_S:NCMP_S + PAST + 1]
    sc_win = s["score"][:, NCMP_S + PAST + 1:]
    col = lambda n: s["col"][:, n:n + 1]
    out_rows = nc.dram_tensor("sample_attended", [NB, D], F32).ap()
    CAP = 4
    NSEL_T, NWIN_T = NPG // 2, 2
    RING = NSEL_T + NWIN_T + NPG

    def tiles_before(i, x):
        return i * (RING // 2) + (NPG // 2 + x // 2)

    def cmp_tile(i, p):
        return (i - 1, NSEL_T + NWIN_T + p)

    with c.stage("sample_attention") as st:
        cmp_in = [st.sem(f"cmp_page_loaded{n}") for n in range(CAP)]
        sel_in = [st.sem(f"sel_pages_loaded{n}") for n in range(4)]
        win_in, row_in, stored = st.sem("window_loaded"), st.sem("query_rows_loaded"), st.sem("head_rows_stored", 16)
        turned = [st.sem(f"tile_turned{n}", 1) for n in range(2)]
        taken = [st.sem(f"tile_taken{n}", 1) for n in range(2)]
        ev = {n: st.sem(n, 1) for n in (
            "hidden_in_psum", "hidden_ready", "compressed_in_psum", "compressed_ready",
            "indices_ready", "queries_in_psum", "queries_ready", "small_scores_in_psum", "small_scores_ready", "sel_scores_in_psum",
            "maxima_ready", "exp_ready", "cmp_prob_ready", "cmp_turned_in_psum", "cmp_turned_ready",
            "importance_in_psum", "importance_ready", "group_importance_in_psum", "sel_maximum_ready",
            "sel_exp_ready", "turned_in_psum", "turned_ready", "output_in_psum", "head_ready")}
        block = st.block()

        def now(eng, i, *names):
            for n in names:
                eng.wait_ge(ev[n], i + 2)

        def before(eng, i, *names):
            for n in names:
                eng.wait_ge(ev[n], i + 1)

        @block.gpsimd
        def _(pool):
            def gather(dst, a, p, done):
                pool.nop(nofuse=True)
                nc.gpsimd.indirect_dma_start(
                    out=dst, out_offset=None, in_=cache,
                    in_offset=bass.IndirectOffsetOnAxis(ap=s["now"][:, a, p:p + 1], axis=0),
                    bounds_check=NPHYS * PAGE * 2 - 1, oob_is_err=True).then_inc(done, 16)

            def indices(a, i):
                nc.gpsimd.tensor_copy(s["now"][:, a], s["index"][:, a, ds(i * NPG, NPG)]).then_inc(ev["indices_ready"], 1)
                pool.wait_ge(ev["indices_ready"], i * 2 + (a + 2))

            def cmp_pages(i):
                indices(0, i)
                for p in range(NPG):
                    if p >= CAP:
                        r, x = cmp_tile(i, p - CAP)
                        pool.wait_ge(turned[x % 2], tiles_before(r, x) + 2)
                    gather(s["cmp"][:, p % CAP, :], 0, p, cmp_in[p % CAP])

            def sel_pages(i):
                indices(1, i)
                for p in range(NPG):
                    gather(s["sel"][:, p, :], 1, p, sel_in[p // 4])

            cmp_pages(0)
            sel_pages(0)
            with pool.Fori(0, NB - 1) as i:
                now(pool, i, "hidden_in_psum")
                cmp_pages(i + 1)
                now(pool, i, "output_in_psum")
                sel_pages(i + 1)

        @block.sync
        def _(sp):
            with sp.Fori(0, NB) as i:
                before(sp, i, "output_in_psum")
                window = io["o_sample_win"][ds(i, 1)].rearrange("b (n p) s g d -> p (b n) (s g d)", p=P)
                sp.dma_start(s["win"], window).then_inc(win_in, 16)
                sp.dma_start(s["vnew"], io["o_sample_rows"][ds(i, 1), 0, 3].rearrange("b g d -> b (g d)")).then_inc(win_in, 16)
                for x in range(2):
                    q = c.query_rows[:, ds(i, 1), :].rearrange("a b (h d) -> h (a b) d", d=HD)
                    sp.dma_start(s["qrow"][:, :, x, :], q).then_inc(row_in, 16)
                now(sp, i, "head_ready")
                sp.dma_start(out_rows[ds(i, 1), :].rearrange("b (h d) -> (b h) d", d=HD), s["head"]).then_inc(stored, 16)
            sp.wait_ge(stored, 16 * NB + 16)

        @block.tensor
        def _(pe):
            mm, tr = nc.tensor.matmul, nc.tensor.transpose

            def tile(i, x, sources):
                pe.wait_ge(taken[x % 2], tiles_before(i, x) + 1)
                for at, src in sources:
                    last = tr(c.bank[x % 2][:, at:at + P], src, c.ident)
                last.then_inc(turned[x % 2], 1)

            def cmp_page(i, p):
                pe.wait_ge(cmp_in[p % CAP], i * (16 * NPG // CAP) + 16 * (p // CAP + 1))
                tile(*cmp_tile(i, p), [(P * v, s["cmp"][:, p % CAP, P * v:P * v + P]) for v in range(4)])

            def attend(i, last_round):
                def next_pages(*pages):
                    if not last_round:
                        for p in pages:
                            cmp_page(i + 1, p)

                for n in range(2):
                    pe.wait_ge(taken[n], tiles_before(i, 0) + 1)
                for v in range(2):
                    for j in range(16):
                        first = j // 8
                        last = mm(c.bank[2 + v][:, 0:KVH * NCMP_S], s["w1"][:, v, j, :],
                                  s["xt"][:, KVH * v:KVH * v + KVH, j % 8, first:first + NCMP_S],
                                  start=(j == 0), stop=(j == 15))
                last.then_inc(ev["hidden_in_psum"], 1)
                pe.wait_ge(row_in, i * 32 + 32)
                pe.nop(nofuse=True)
                for a in range(2):
                    last = tr(c.bank[4][:, NH * a:NH * a + NH], s["qrow"][:, a].rearrange("h x d -> h (x d)"),
                              c.ident[0:NH, 0:NH])
                last.then_inc(ev["queries_in_psum"], 1)
                for x in range(NPG // 2):
                    pe.wait_ge(sel_in[x // 2], i * (16 * NPG // 4) + 64)
                    tile(i, x, [(2 * P * g + P * y, s["sel"][:, 2 * x + y, P * g:P * g + P])
                                      for g in range(2) for y in range(2)])
                pe.wait_ge(win_in, i * 32 + 32)
                for g in range(2):
                    tile(i, NSEL_T + g, [(P * y, s["win"][:, y, P * g:P * g + P]) for y in range(4)])
                now(pe, i, "hidden_ready")
                for q in range(2):
                    mm(c.bank[2][HD * q:HD * q + HD, 0:2 * NCMP_S], s["w2"][:, 0, :], s["hidden"][:, 0, q:KVH:2, :],
                       start=True, stop=True)
                for g in range(KVH):
                    last = mm(c.bank[3][0:NCMP_S, HD * g:HD * g + HD], s["hidden"][:, 1, g, :], s["w2"][:, 1, :],
                              start=True, stop=True)
                last.then_inc(ev["compressed_in_psum"], 1)
                for n in range(2):
                    pe.wait_ge(taken[n], tiles_before(i, NSEL_T + NWIN_T) + 1)
                now(pe, i, "compressed_ready", "queries_ready")
                Q = c.queries
                for g in range(2):
                    mm(c.bank[2][0:NH, 0:NCMP_S], Q[:, 0, g, :], s["kc"][:, g, :], start=(g == 0), stop=(g == 1))
                for g in range(2):
                    mm(c.bank[2][0:NH, 128:129], Q[:, 1, g, :], c.kv_sample[:, 4 + g, ds(i, 1)],
                       start=(g == 0), stop=(g == 1))
                for g in range(2):
                    last = mm(c.bank[3][0:NH, :], Q[:, 1, g, :], s["kwt"][:, g, :], start=(g == 0), stop=(g == 1))
                last.then_inc(ev["small_scores_in_psum"], 1)
                before(pe, i, "head_ready")

                def sel_scores(*parts):
                    for x in parts:
                        for g in range(2):
                            last = mm(c.bank[4 + x][0:NH, :], Q[:, 1, g, :], s["kt"][:, g, 512 * x:512 * x + 512],
                                      start=(g == 0), stop=(g == 1))
                    return last

                sel_scores(0)
                next_pages(0)
                sel_scores(1)
                next_pages(1)
                now(pe, i, "cmp_prob_ready", "small_scores_ready")
                pe.nop(nofuse=True)
                tr(c.bank[2][0:NCMP_S, 0:NH], sc_cmp, c.ident[0:NH, 0:NH]).then_inc(ev["cmp_turned_in_psum"], 1)
                next_pages(2)
                now(pe, i, "cmp_turned_ready")
                mm(c.bank[3][0:NH, 0:NSB], s["pct"], s["overlap"], start=True,
                   stop=True).then_inc(ev["importance_in_psum"], 1)
                next_pages(3)
                now(pe, i, "importance_ready")
                pe.nop(nofuse=True)
                mm(c.bank[2][0:NH, 0:NSB], s["samegroup"], s["imp"], start=True,
                   stop=True).then_inc(ev["group_importance_in_psum"], 1)
                sel_scores(2, 3).then_inc(ev["sel_scores_in_psum"], 1)
                next_pages(*range(4, 12))
                now(pe, i, "sel_exp_ready", "exp_ready")
                pe.nop(nofuse=True)
                for p in range(NPG):
                    tr(c.bank[4][:, NH * p:NH * p + NH], sc_sel[:, P * p:P * p + P], c.ident[0:NH, 0:NH])
                tr(c.bank[4][0:1, NH * NPG:NH * NPG + NH], sc_sel[:, PAST:PAST + 1], c.ident[0:NH, 0:NH])
                for y in range(4):
                    last = tr(c.bank[5][:, NH * y:NH * y + NH], sc_win[:, P * y:P * y + P], c.ident[0:NH, 0:NH])
                last.then_inc(ev["turned_in_psum"], 1)
                now(pe, i, "turned_ready")
                for p in range(NPG):
                    mm(c.bank[6][0:NH, 0:RW], s["pt"][:, NH * p:NH * p + NH], s["sel"][:, p, RW:2 * RW],
                       start=(p == 0), stop=False)
                    if p % 4 == 3:
                        next_pages(12 + p // 4)
                mm(c.bank[6][0:NH, 0:RW], s["pt"][0:1, NH * NPG:NH * NPG + NH], s["vnew"], start=False, stop=True)
                for y in range(4):
                    mm(c.bank[6][0:NH, RW:2 * RW], s["wt"][:, NH * y:NH * y + NH], s["win"][:, y, RW:2 * RW],
                       start=(y == 0), stop=(y == 3))
                mm(c.bank[7][0:NH, 0:RW], s["pct"], s["vc"], start=True, stop=True).then_inc(ev["output_in_psum"], 1)

            for p in range(NPG):
                cmp_page(0, p)
            with pe.Fori(0, NB - 1) as i:
                attend(i, False)
            attend(NB - 1, True)

        def take_tile(eng, copy, i, x):
            b = x % 2
            eng.wait_ge(turned[b], tiles_before(i, x) + 2)
            bank = c.bank[b]
            if x >= NSEL_T + NWIN_T:
                p = x - NSEL_T - NWIN_T
                src = bank.rearrange("p (v t) -> p v t", v=4)
                for q in range(2):
                    for par in range(2):
                        half = src[HD * q:HD * q + HD].rearrange("p v (n j a) -> p v j n a", j=8, a=2)[:, :, :, :, par]
                        last = copy(s["xt"][HD * par:HD * par + HD, q:2 * KVH:2, :, 8 * p:8 * p + 8], half)
            elif x < NSEL_T:
                last = copy(s["kt"][:, :, 2 * P * x:2 * P * x + 2 * P], bank.rearrange("p (g t) -> p g t", g=2))
            else:
                last = copy(s["kwt"][:, x - NSEL_T, :], bank)
            eng.drain().then_inc(taken[b], 1)

        @block.scalar
        def _(act):
            def take_pages(i, pages):
                for p in pages:
                    take_tile(act, nc.scalar.copy, *cmp_tile(i, p))

            def attend(i, last_round):
                now(act, i, "hidden_in_psum")
                for v in range(2):
                    nc.scalar.activation(s["hidden"][:, v],
                                         c.bank[2 + v][:, 0:KVH * NCMP_S].rearrange("p (g n) -> p g n", g=KVH),
                                         ACT.Gelu_apprx_tanh, bias=c.cmp_bias[:, v:v + 1])
                act.drain().then_inc(ev["hidden_ready"], 1)
                for x in range(1, NSEL_T + NWIN_T, 2):
                    take_tile(act, nc.scalar.copy, i, x)
                now(act, i, "small_scores_in_psum")
                nc.scalar.copy(sc_cmp, c.bank[2][0:NH, 0:NCMP_S])
                nc.scalar.copy(sc_sel[:, PAST:PAST + 1], c.bank[2][0:NH, 128:129])
                nc.scalar.copy(sc_win, c.bank[3][0:NH, :])
                act.drain().then_inc(ev["small_scores_ready"], 1)
                now(act, i, "maxima_ready")
                nc.scalar.activation(sc_cmp, sc_cmp, ACT.Exp, bias=col(0), scale=SCALE, accum_out=col(1))
                nc.scalar.activation(sc_win, sc_win, ACT.Exp, bias=col(2), scale=SCALE, accum_out=col(3))
                act.drain().then_inc(ev["exp_ready"], 1)
                if not last_round:
                    take_pages(i + 1, range(0, 12))
                now(act, i, "sel_maximum_ready")
                nc.scalar.activation(sc_sel, sc_sel, ACT.Exp, bias=col(4), scale=SCALE, accum_out=col(5))
                act.drain().then_inc(ev["sel_exp_ready"], 1)
                if not last_round:
                    take_pages(i + 1, (13, 15))

            take_pages(0, range(1, NPG, 2))
            with act.Fori(0, NB - 1) as i:
                attend(i, False)
            attend(NB - 1, True)

        @block.vector
        def _(dve):
            tt, ts, copy = nc.vector.tensor_tensor, nc.vector.tensor_scalar, nc.vector.tensor_copy
            reduce = nc.vector.tensor_reduce

            def scaled_maximum(dst, scores):
                reduce(dst, scores, AX.X, ALU.max)
                dve.drain()
                ts(dst, dst, -SCALE, None, ALU.mult)

            def attend(i, last_round):
                now(dve, i, "queries_in_psum")
                for a in range(2):
                    src = c.bank[4][:, NH * a:NH * a + NH].unsqueeze(1).to_broadcast([P, 2, NH])
                    tt(c.queries[:, a], src, s["ownquery"].rearrange("p (g h) -> p g h", g=2), ALU.mult)
                dve.drain().then_inc(ev["queries_ready"], 1)
                for x in range(0, NSEL_T + NWIN_T, 2):
                    take_tile(dve, copy, i, x)
                now(dve, i, "compressed_in_psum")
                copy(s["kc"], c.bank[2][:, 0:2 * NCMP_S].rearrange("p (g n) -> p g n", g=2))
                copy(s["vc"], c.bank[3][0:NCMP_S, 0:RW])
                dve.drain().then_inc(ev["compressed_ready"], 1)
                now(dve, i, "small_scores_ready")
                scaled_maximum(col(0), sc_cmp)
                scaled_maximum(col(2), sc_win)
                dve.drain().then_inc(ev["maxima_ready"], 1)
                now(dve, i, "exp_ready")
                ts(col(1), col(1), 1e-30, None, ALU.max)
                dve.drain()
                nc.vector.reciprocal(col(1), col(1))
                nc.vector.reciprocal(col(3), col(3))
                dve.drain()
                ts(sc_cmp, sc_cmp, col(1), None, ALU.mult)
                dve.drain().then_inc(ev["cmp_prob_ready"], 1)
                now(dve, i, "cmp_turned_in_psum")
                copy(s["pct"], c.bank[2][0:NCMP_S, 0:NH]).then_inc(ev["cmp_turned_ready"], 1)
                now(dve, i, "importance_in_psum")
                copy(s["imp"], c.bank[3][0:NH, 0:NSB]).then_inc(ev["importance_ready"], 1)
                now(dve, i, "group_importance_in_psum")
                tt(s["pick"], c.bank[2][0:NH, 0:NSB], s["notforced"], ALU.mult)
                dve.drain()
                tt(s["pick"], s["pick"], s["forced"], ALU.add)
                dve.drain()
                theirs = s["pick"].unsqueeze(1).to_broadcast([NH, NSB, NSB])
                mine = s["pick"].unsqueeze(2).to_broadcast([NH, NSB, NSB])
                cube = lambda a: a.rearrange("p (i j) -> p i j", i=NSB)
                tt(cube(s["rank"]), theirs, mine, ALU.is_gt)
                tt(cube(s["tie"]), theirs, mine, ALU.is_equal)
                dve.drain()
                tt(s["tie"], s["tie"], s["earlier"], ALU.mult)
                dve.drain()
                tt(s["rank"], s["rank"], s["tie"], ALU.add)
                dve.drain()
                reduce(s["pick"], cube(s["rank"]), AX.X, ALU.add)
                dve.drain()
                ts(s["pick"], s["pick"], float(NSEL), NEG, ALU.is_ge, ALU.mult)
                dve.drain()
                now(dve, i, "sel_scores_in_psum")
                for x in range(4):
                    blocks = s["pick"][:, 8 * x:8 * x + 8].unsqueeze(2).to_broadcast([NH, 8, HD])
                    tt(sc_sel[:, 512 * x:512 * x + 512].rearrange("p (a t) -> p a t", t=HD),
                       c.bank[4 + x][0:NH, :].rearrange("p (a t) -> p a t", t=HD), blocks, ALU.add)
                tt(sc_sel[:, PAST:PAST + 1], sc_sel[:, PAST:PAST + 1], s["pick"][:, NSB - 1:NSB], ALU.add)
                dve.drain()
                scaled_maximum(col(4), sc_sel)
                dve.drain().then_inc(ev["sel_maximum_ready"], 1)
                now(dve, i, "turned_in_psum")
                copy(s["pt"][:, 0:NH * NPG], c.bank[4][:, 0:NH * NPG])
                copy(s["pt"][0:1, NH * NPG:], c.bank[4][0:1, NH * NPG:NH * NPG + NH])
                copy(s["wt"], c.bank[5][:, 0:4 * NH])
                nc.vector.reciprocal(col(5), col(5))
                dve.drain().then_inc(ev["turned_ready"], 1)
                if not last_round:
                    for p in (12, 14):
                        take_tile(dve, copy, *cmp_tile(i + 1, p))
                g = s["gate"]
                tt(col(5), col(5), g[:, ds(i, 1), 1], ALU.mult)
                tt(col(3), col(3), g[:, ds(i, 1), 2], ALU.mult)
                copy(col(1), g[:, ds(i, 1), 0])
                dve.drain()
                now(dve, i, "output_in_psum")
                acc = s["acc"]
                ts(acc, c.bank[7][0:NH, 0:RW], col(1), None, ALU.mult)
                for cf, at in ((5, 0), (3, RW)):
                    dve.drain()
                    nc.vector.scalar_tensor_tensor(acc, c.bank[6][0:NH, at:at + RW], col(cf), acc, ALU.mult, ALU.add)
                dve.drain()
                tt(acc, acc, s["ownkv"], ALU.mult)
                dve.drain()
                dve.wait_ge(stored, i * 16 + 16)
                reduce(s["head"], acc.rearrange("p (g d) -> p d g", g=KVH), AX.X, ALU.add).then_inc(ev["head_ready"], 1)

            for p in range(0, NPG, 2):
                take_tile(dve, copy, *cmp_tile(0, p))
            with dve.Fori(0, NB - 1) as i:
                attend(i, False)
            attend(NB - 1, True)

    back = c.work[0:NB, 0:D]
    with c.stage("sample_mixed") as st:
        loaded, turned2 = st.sem("rows_loaded"), st.sem("columns_in_psum")
        block = st.block()

        @block.sync
        def _(sp):
            sp.dma_start(back, out_rows).then_inc(loaded, 16)

        @block.tensor
        def _(pe):
            pe.wait_ge(loaded, 16)
            for k in range(KT):
                last = nc.tensor.transpose(c.bank[0][:, NB * k:NB * k + NB], back[:, P * k:P * k + P],
                                           c.ident[0:NB, 0:NB])
            last.then_inc(turned2, 1)

        @block.vector
        def _(dve):
            dve.wait_ge(turned2, 1)
            nc.vector.tensor_copy(c.slot(9)[:, :, TP:NT], c.bank[0][:, 0:NB * KT].rearrange("p (k b) -> p k b", b=NB))


def hybrid_step(nc, io):
    c = Core(nc, io)
    load_parameters(c)
    load_tokens(c)
    rms_norm(c, c.slot(0), "mix0", c.slot(1), c.slot(3))
    transpose_out(c, "shift_out", c.slot(1), TP - 1, [(TP - 1, TP, io["o_prompt_shift"][0, :, :]),
                                                      (TP, NT, io["o_sample_shift"][0, :, :])])
    rwkv_inputs(c)
    rwkv_prepare(c)
    sample_state(c)
    rwkv_chunks(c)
    rwkv_state_out(c)
    rwkv_finish(c)
    project(c, "rw_wo", c.slot(4), KT, io["rw_wo"][0, :, :], KT, add_to(c, c.slot(0)), "dve")
    mixture(c, 0)

    kv = c.flat(2, 2)[:, 0:KVT * NT].rearrange("p (k t) -> p k t", t=NT)
    rms_norm(c, c.slot(0), "kv", c.slot(1), c.slot(4))
    project(c, "w_kv", c.slot(1), KT, io["w_kv"], KVT, copy_to(c, kv), "act")
    rotate(c, "rotate_keys", kv, kv, (4, 5, 8, 9))
    kv_rows(c)
    compress_prompt(c)

    rms_norm(c, c.slot(0), "mix1", c.slot(1), c.slot(2))
    project(c, "nsa_wq", c.slot(1), KT, io["nsa_wqg"][0][:, 0:D], KT, copy_to(c, c.slot(6)), "act")
    rotate(c, "rotate_queries", c.slot(6), c.slot(7), range(KT))
    gates(c)
    prompt_attention(c)

    sample_memory(c)
    sample_prepare(c)
    sample_attention(c)
    project(c, "nsa_wo", c.slot(9), KT, io["nsa_wo"][0], KT, add_to(c, c.slot(0)), "dve")
    mixture(c, 1)

    rms_norm(c, c.slot(0), "out", c.slot(1), c.slot(2))
    transpose_out(c, "outputs", c.slot(1), 0,
                  [(P * n, P * n + P, io["o_y_prompt"][0, P * n:P * n + P, :]) for n in range(TT)]
                  + [(TP, NT, io["o_y_sample"][:, 0, :])])


_INS = ["x_prompt", "x_sample", "state_wkv", "state_shift", "cache_kv", "cache_win", "page_table",
        "ln_mix", "ln_ffn", "ln_kv", "ln_out", "rw_mu", "rw_wr", "rw_wk", "rw_wv", "rw_wo", "rw_w0", "rw_w1", "rw_w2",
        "rw_a0", "rw_a1", "rw_a2", "rw_g1", "rw_g2", "rw_kk", "rw_ka", "rw_rk", "rw_lnw", "rw_lnb",
        "w_kv", "cmp_pe", "cmp_w1", "cmp_b1", "cmp_w2", "nsa_wqg", "nsa_wo",
        "moe_wrg", "moe_brg", "moe_wre", "moe_bre", "moe_wgate", "moe_wup", "moe_wdown"]
_OUTS = [("o_y_prompt", (1, TP, D)), ("o_y_sample", (NB, 1, D)), ("o_prompt_wkv", (1, 1, NH, HD, HD)),
         ("o_prompt_shift", (1, 1, D)), ("o_prompt_rows", (1, TP, 4, KVH, HD)), ("o_prompt_win", (1, WIN, 2, KVH, HD)),
         ("o_sample_wkv", (1, NB, NH, HD, HD)), ("o_sample_shift", (1, NB, D)),
         ("o_sample_rows", (NB, 1, 4, KVH, HD)), ("o_sample_win", (NB, WIN, 2, KVH, HD))]


def _lay_out(inputs):
    arrays = {name: np.ascontiguousarray(inputs[name]) for name in _INS}
    arrays["consts"] = CONSTS
    return arrays


def kernel(**inputs):
    import concourse.bacc as _bacc
    from concourse.bass_utils import run_bass_kernel_spmd as _run

    nc = _bacc.Bacc("TRN2", target_bir_lowering=False, num_devices=1)
    arrays, io = _lay_out(inputs), {}
    for name, a in arrays.items():
        io[name] = nc.dram_tensor(f"in_{name}", a.shape, mybir.dt.from_np(a.dtype), kind="ExternalInput").ap()
    for name, shape in _OUTS:
        io[name] = nc.dram_tensor(name, shape, F32, kind="ExternalOutput").ap()
    hybrid_step(nc, io)
    r = _run(nc, [{f"in_{name}": a for name, a in arrays.items()}], core_ids=[0])
    return tuple(r.results[0][name] for name, _ in _OUTS)
```
